# Optimizing a Trainium2 kernel written in Bass

```python
import math
import jax, jax.numpy as jnp
from jax import lax
import numpy as np

D_MODEL = 1024
BATCH = 1
SEQ = 256
DEPTH = 2

N_HEADS = 8
HEAD_DIM = 64
ATTN_WIDTH = N_HEADS * HEAD_DIM
CONV_WIDTH = 512
CONV_K = 31
DILATED_GROUPS = ((128, 1), (512, 4), (2048, 16))
BLK = 128
ROPE_THETA = 10000.0
N_EXPERT_GROUPS = 4
EXPERTS_PER_GROUP = 8
N_EXPERTS = N_EXPERT_GROUPS * EXPERTS_PER_GROUP
EXPERT_FF = 512
TOP_K_IN_GROUP = 2
MOE_BLOCK = 128
PLE_DIM = 256
EPS = 1e-6
NEG_INF = -1e30

W_IN_SPLITS = (ATTN_WIDTH, 2 * ATTN_WIDTH, 3 * ATTN_WIDTH,
               3 * ATTN_WIDTH + CONV_WIDTH, 3 * ATTN_WIDTH + 2 * CONV_WIDTH,
               3 * ATTN_WIDTH + 2 * CONV_WIDTH + D_MODEL)
W_IN_COLS = 3 * ATTN_WIDTH + 2 * CONV_WIDTH + 2 * D_MODEL


def _rms_norm(t, g):
    tf = t.astype(jnp.float32)
    y = tf * lax.rsqrt(jnp.mean(tf * tf, axis=-1, keepdims=True) + EPS)
    return (y * g.astype(jnp.float32)).astype(t.dtype)

def _layer_norm(t, g, b):
    tf = t.astype(jnp.float32)
    mu = jnp.mean(tf, axis=-1, keepdims=True)
    var = jnp.mean(jnp.square(tf - mu), axis=-1, keepdims=True)
    y = (tf - mu) * lax.rsqrt(var + EPS)
    return (y * g.astype(jnp.float32) + b.astype(jnp.float32)).astype(t.dtype)

def _rope(t):
    S = t.shape[1]
    inv = jnp.power(ROPE_THETA, -jnp.arange(0, HEAD_DIM, 2, dtype=jnp.float32) / HEAD_DIM)
    ang = jnp.arange(S, dtype=jnp.float32)[:, None] * inv[None, :]
    cos = jnp.cos(ang)[None, :, None, :]
    sin = jnp.sin(ang)[None, :, None, :]
    tf = t.astype(jnp.float32)
    t1, t2 = tf[..., :HEAD_DIM // 2], tf[..., HEAD_DIM // 2:]
    return jnp.concatenate([t1 * cos - t2 * sin, t1 * sin + t2 * cos], axis=-1).astype(t.dtype)

def _to_dilated_blocks(t, dilation):
    B, S = t.shape[0], t.shape[1]
    rest = t.shape[2:]
    seg = dilation * BLK
    Sp = -(-S // seg) * seg
    t = jnp.pad(t, [(0, 0), (0, Sp - S)] + [(0, 0)] * len(rest))
    t = t.reshape((B, Sp // dilation, dilation) + rest)
    t = jnp.moveaxis(t, 2, 1)
    return t.reshape((B, dilation, Sp // seg, BLK) + rest)

def _from_dilated_blocks(t, S):
    B, d, nb, blk = t.shape[:4]
    rest = t.shape[4:]
    t = t.reshape((B, d, nb * blk) + rest)
    t = jnp.moveaxis(t, 1, 2).reshape((B, nb * blk * d) + rest)
    return t[:, :S]

def _dilated_window_attention(q, k, v, window, dilation):
    band = window // dilation
    assert band <= BLK
    S = q.shape[1]
    qb, kb, vb = (_to_dilated_blocks(t, dilation) for t in (q, k, v))

    def with_prev(t):
        prev = jnp.pad(t, ((0, 0), (0, 0), (1, 0), (0, 0), (0, 0), (0, 0)))[:, :, :-1]
        return jnp.concatenate([prev, t], axis=3)

    kk, vv = with_prev(kb), with_prev(vb)
    s = jnp.einsum('brnqhe,brnkhe->brnhqk', qb, kk,
                   preferred_element_type=jnp.float32) * (HEAD_DIM ** -0.5)
    nb = qb.shape[2]
    qi = jnp.arange(BLK)[:, None] + BLK
    kj = jnp.arange(2 * BLK)[None, :]
    in_band = (kj <= qi) & (qi - kj <= band)
    not_before_start = (jnp.arange(nb)[:, None, None] > 0) | (kj >= BLK)[None]
    allowed = in_band[None] & not_before_start
    s = jnp.where(allowed[:, None], s, NEG_INF)
    m = jnp.max(s, axis=-1)
    pexp = jnp.exp(s - m[..., None])
    l = jnp.sum(pexp, axis=-1)
    acc = jnp.einsum('brnhqk,brnkhe->brnqhe', pexp.astype(v.dtype), vv,
                     preferred_element_type=jnp.float32)
    m = jnp.moveaxis(m, 3, 4)
    l = jnp.moveaxis(l, 3, 4)
    return (_from_dilated_blocks(acc, S), _from_dilated_blocks(m, S), _from_dilated_blocks(l, S))

def _dilated_mixture_attention(q, k, v):
    parts = [_dilated_window_attention(q, k, v, w, d) for (w, d) in DILATED_GROUPS]
    M = parts[0][1]
    for _, m_g, _ in parts[1:]:
        M = jnp.maximum(M, m_g)
    num = 0.0
    den = 0.0
    for acc_g, m_g, l_g in parts:
        scale = jnp.exp(m_g - M)
        num = num + acc_g * scale[..., None]
        den = den + l_g * scale
    o = num / den[..., None]
    B, S = q.shape[0], q.shape[1]
    return o.reshape(B, S, ATTN_WIDTH).astype(q.dtype)

def _conformer_conv(cu, cg, w_dw, b_dw, ln_g, ln_b):
    u = cu * jax.nn.sigmoid(cg)
    rhs = w_dw.reshape(CONV_K, 1, CONV_WIDTH).astype(u.dtype)
    y = lax.conv_general_dilated(u, rhs, window_strides=(1,), padding=[(CONV_K - 1, 0)],
                                 dimension_numbers=('NWC', 'WIO', 'NWC'),
                                 feature_group_count=CONV_WIDTH)
    y = y + b_dw
    y = _layer_norm(y, ln_g, ln_b)
    return jax.nn.silu(y)

def _hier_moe(h, w_rg, b_rg, w_re, b_re, w_gate, w_up, w_down):
    B, S, D = h.shape
    T = B * S
    hf = h.reshape(T, D)
    lg = (hf @ w_rg + b_rg).astype(jnp.float32)
    pg = jax.nn.softmax(lg, axis=-1)
    gsel = jnp.argmax(lg, axis=-1)
    le = (hf @ w_re + b_re).astype(jnp.float32).reshape(T, N_EXPERT_GROUPS, EXPERTS_PER_GROUP)
    le_sel = jnp.take_along_axis(le, gsel[:, None, None], axis=1)[:, 0]
    top_v, top_i = lax.top_k(le_sel, TOP_K_IN_GROUP)
    gate = jnp.take_along_axis(pg, gsel[:, None], axis=1) * jax.nn.softmax(top_v, axis=-1)
    eid = gsel[:, None] * EXPERTS_PER_GROUP + top_i

    A = T * TOP_K_IN_GROUP
    flat_e = eid.reshape(-1)
    order = jnp.argsort(flat_e)
    sorted_e = flat_e[order]
    counts = jnp.bincount(flat_e, length=N_EXPERTS)
    padded = ((counts + MOE_BLOCK - 1) // MOE_BLOCK) * MOE_BLOCK
    ends = jnp.cumsum(padded)
    pad_start = ends - padded
    start = jnp.cumsum(counts) - counts
    dest = pad_start[sorted_e] + (jnp.arange(A) - start[sorted_e])
    n_rows = (-(-A // MOE_BLOCK)) * MOE_BLOCK + N_EXPERTS * MOE_BLOCK
    n_blocks = n_rows // MOE_BLOCK
    tok = order // TOP_K_IN_GROUP
    buf = jnp.zeros((n_rows, D), hf.dtype).at[dest].set(hf[tok])
    block_e = jnp.minimum(jnp.searchsorted(ends, jnp.arange(n_blocks) * MOE_BLOCK, side='right'),
                          N_EXPERTS - 1)

    def expert_block(args):
        xb, e = args
        hb = jax.nn.silu(xb @ w_gate[e]) * (xb @ w_up[e])
        return hb @ w_down[e]

    yb = lax.map(expert_block, (buf.reshape(n_blocks, MOE_BLOCK, D), block_e))
    y_rows = yb.reshape(n_rows, D)[dest]
    contrib = y_rows * gate.reshape(-1)[order][:, None].astype(y_rows.dtype)
    out = jnp.zeros((T, D), hf.dtype).at[tok].add(contrib)
    return out.reshape(B, S, D)

def first_inputs(seed: int = 0) -> dict:
    key = jax.random.key(seed)
    ks = jax.random.split(key, 24)
    L, D, f32 = DEPTH, D_MODEL, jnp.float32

    def nrm(k, shape, fan_in):
        return jax.random.normal(k, shape, f32) * (fan_in ** -0.5)

    def gain(k, shape):
        return 1.0 + 0.05 * jax.random.normal(k, shape, f32)

    def small(k, shape, s=0.02):
        return s * jax.random.normal(k, shape, f32)

    return {
        "x": jax.random.normal(ks[0], (BATCH, SEQ, D), f32),
        "p": jax.random.normal(ks[1], (DEPTH, BATCH, SEQ, PLE_DIM), f32),
        "norm_mix": gain(ks[2], (L, D)),
        "w_in": nrm(ks[3], (L, D, W_IN_COLS), D),
        "w_dw": nrm(ks[4], (L, CONV_K, CONV_WIDTH), CONV_K),
        "b_dw": small(ks[5], (L, CONV_WIDTH)),
        "ln_conv_g": gain(ks[6], (L, CONV_WIDTH)),
        "ln_conv_b": small(ks[7], (L, CONV_WIDTH)),
        "w_attn_out": nrm(ks[8], (L, ATTN_WIDTH, D), ATTN_WIDTH),
        "w_conv_out": nrm(ks[9], (L, CONV_WIDTH, D), CONV_WIDTH),
        "b_conv_out": small(ks[10], (L, D)),
        "w_out": nrm(ks[11], (L, D, D), D),
        "norm_ffn": gain(ks[12], (L, D)),
        "w_route_group": nrm(ks[13], (L, D, N_EXPERT_GROUPS), D),
        "b_route_group": small(ks[14], (L, N_EXPERT_GROUPS), 0.01),
        "w_route_expert": nrm(ks[15], (L, D, N_EXPERTS), D),
        "b_route_expert": small(ks[16], (L, N_EXPERTS), 0.01),
        "w_exp_gate": nrm(ks[17], (L, N_EXPERTS, D, EXPERT_FF), D),
        "w_exp_up": nrm(ks[18], (L, N_EXPERTS, D, EXPERT_FF), D),
        "w_exp_down": nrm(ks[19], (L, N_EXPERTS, EXPERT_FF, D), EXPERT_FF),
        "norm_ple": gain(ks[20], (L, D)),
        "w_ple_proj": nrm(ks[21], (L, PLE_DIM, D), PLE_DIM),
        "w_ple_gate": nrm(ks[22], (L, D, D), D),
        "norm_final": gain(ks[23], (D,)),
    }

def first_block(x, p, norm_mix, w_in, w_dw, b_dw, ln_conv_g, ln_conv_b, w_attn_out,
              w_conv_out, b_conv_out, w_out, norm_ffn, w_route_group, b_route_group,
              w_route_expert, b_route_expert, w_exp_gate, w_exp_up, w_exp_down,
              norm_ple, w_ple_proj, w_ple_gate, norm_final):
    B, S, _ = x.shape
    for i in range(DEPTH):
        h = _rms_norm(x, norm_mix[i])
        z = h @ w_in[i]
        q, k, v, cu, cg, ga, gb = jnp.split(z, W_IN_SPLITS, axis=-1)
        q = _rope(q.reshape(B, S, N_HEADS, HEAD_DIM))
        k = _rope(k.reshape(B, S, N_HEADS, HEAD_DIM))
        v = v.reshape(B, S, N_HEADS, HEAD_DIM)
        y_a = _dilated_mixture_attention(q, k, v) @ w_attn_out[i]
        y_b = _conformer_conv(cu, cg, w_dw[i], b_dw[i], ln_conv_g[i], ln_conv_b[i]) \
            @ w_conv_out[i] + b_conv_out[i]
        merged = jax.nn.sigmoid(ga) * y_a + jax.nn.sigmoid(gb) * y_b
        x = x + merged @ w_out[i]
        h2 = _rms_norm(x, norm_ffn[i])
        x = x + _hier_moe(h2, w_route_group[i], b_route_group[i], w_route_expert[i],
                          b_route_expert[i], w_exp_gate[i], w_exp_up[i], w_exp_down[i])
        g_ple = jax.nn.sigmoid(_rms_norm(x, norm_ple[i]) @ w_ple_gate[i])
        x = x + g_ple * (p[i] @ w_ple_proj[i])
    return _rms_norm(x, norm_final)


DEPTH_2 = 1

D_RNN = 1344
LRU_BLOCKS = 4
LRU_BLOCK_W = D_RNN // LRU_BLOCKS
CONV_W = 4
LRU_C = 8.0
N_HEADS_2 = 16
N_KV_GROUPS = 4
HEADS_PER_GROUP = N_HEADS_2 // N_KV_GROUPS
CMP_BLOCK = 32
CMP_STRIDE = 16
SEL_BLOCK = 64
N_SELECT = 16
WINDOW = 512
PHI_HIDDEN = 256
Q_BLOCK = 32
SEL_FORCED = 1e4
NEG_INF_2 = -1e30
REL_BUCKETS = 32
REL_MAX_DIST = 128
D_FF = 4 * D_MODEL
NORM_EPS = 1e-6

Q_W = N_HEADS_2 * HEAD_DIM
KV_W = N_KV_GROUPS * HEAD_DIM
SPLIT_SIZES = (D_RNN, D_RNN, Q_W, KV_W, KV_W, KV_W, KV_W, KV_W, KV_W, 3 * N_HEADS_2, D_MODEL, D_MODEL)
D_IN = 2 * D_RNN + Q_W + 6 * KV_W + 3 * N_HEADS_2 + 2 * D_MODEL


def rmsnorm(x, g):
    xf = x.astype(jnp.float32)
    y = xf * lax.rsqrt(jnp.mean(xf * xf, axis=-1, keepdims=True) + NORM_EPS)
    return y.astype(x.dtype) * g

def t5_bucket(dist):
    max_exact = REL_BUCKETS // 2
    d = jnp.maximum(dist, 0)
    df = jnp.maximum(d.astype(jnp.float32), 1.0)
    large = max_exact + (jnp.log(df / max_exact) / math.log(REL_MAX_DIST / max_exact)
                         * (REL_BUCKETS - max_exact)).astype(jnp.int32)
    large = jnp.minimum(large, REL_BUCKETS - 1)
    return jnp.where(d < max_exact, d, large)

def masked_softmax(s, mask):
    p = jax.nn.softmax(jnp.where(mask, s.astype(jnp.float32), NEG_INF_2), axis=-1)
    return jnp.where(mask, p, 0.0)

def causal_depthwise_conv(x, w, b):
    y = lax.conv_general_dilated(x, w[:, None, :], window_strides=(1,), padding=[(CONV_W - 1, 0)],
                                 dimension_numbers=("NWC", "WIO", "NWC"),
                                 feature_group_count=x.shape[-1])
    return y + b

def block_diag_linear(x, w, b):
    xb = x.reshape(x.shape[0], x.shape[1], LRU_BLOCKS, LRU_BLOCK_W)
    y = jnp.einsum("btni,nij->btnj", xb, w) + b
    return y.reshape(x.shape)

def rg_lru(x, w_a, b_a, w_x, b_x, lam):
    r = jax.nn.sigmoid(block_diag_linear(x, w_a, b_a)).astype(jnp.float32)
    i = jax.nn.sigmoid(block_diag_linear(x, w_x, b_x))
    log_a = -LRU_C * r * jax.nn.softplus(-lam.astype(jnp.float32))
    a = jnp.exp(log_a)
    mult = jnp.sqrt(-jnp.expm1(2.0 * log_a))
    first = (jnp.arange(x.shape[1]) == 0)[None, :, None]
    mult = jnp.where(first, 1.0, mult)
    u = mult * (i * x).astype(jnp.float32)

    def combine(c1, c2):
        a1, b1 = c1
        a2, b2 = c2
        return a1 * a2, a2 * b1 + b2

    _, h = lax.associative_scan(combine, (a, u), axis=1)
    return h.astype(x.dtype)

def compress_blocks(z, pe, w1, w2):
    b, t = z.shape[0], z.shape[1]
    n_c = (t - CMP_BLOCK) // CMP_STRIDE + 1
    idx = jnp.arange(n_c)[:, None] * CMP_STRIDE + jnp.arange(CMP_BLOCK)[None, :]
    blk = z[:, idx] + pe[None, None, :, None, :]
    flat = blk.transpose(0, 3, 1, 2, 4).reshape(b, N_KV_GROUPS, n_c, CMP_BLOCK * HEAD_DIM)
    return jax.nn.gelu(flat @ w1, approximate=True) @ w2

def nsa_mixer(q, k_c, v_c, k_s, v_s, k_w, v_w, g_nsa, rel_bias,
              phi_k_pe, phi_k_w1, phi_k_w2, phi_v_pe, phi_v_w1, phi_v_w2,
              q_norm, kc_norm, ks_norm, kw_norm):
    B, T, _ = q.shape
    G, R, hd = N_KV_GROUPS, HEADS_PER_GROUP, HEAD_DIM
    qh = rmsnorm(q.reshape(B, T, N_HEADS_2, hd), q_norm) * (hd ** -0.5)
    qh = qh.reshape(B, T, G, R, hd).transpose(0, 2, 3, 1, 4)
    kv = lambda z: z.reshape(B, T, G, hd)
    kc = rmsnorm(compress_blocks(kv(k_c), phi_k_pe, phi_k_w1, phi_k_w2), kc_norm)
    vc = compress_blocks(kv(v_c), phi_v_pe, phi_v_w1, phi_v_w2)
    n_c = kc.shape[2]
    n_sblk = T // SEL_BLOCK
    ks = rmsnorm(kv(k_s), ks_norm).transpose(0, 2, 1, 3).reshape(B, G, n_sblk, SEL_BLOCK, hd)
    vs = kv(v_s).transpose(0, 2, 1, 3).reshape(B, G, n_sblk, SEL_BLOCK, hd)
    pad = ((0, 0), (0, 0), (WINDOW, 0), (0, 0))
    kw = jnp.pad(rmsnorm(kv(k_w), kw_norm).transpose(0, 2, 1, 3), pad)
    vw = jnp.pad(kv(v_w).transpose(0, 2, 1, 3), pad)
    gates = jax.nn.sigmoid(g_nsa.reshape(B, T, G, R, 3).transpose(0, 2, 3, 1, 4))
    bias_gr = rel_bias.T.reshape(G, R, REL_BUCKETS)

    cstart = jnp.arange(n_c) * CMP_STRIDE
    cend = cstart + CMP_BLOCK - 1
    sj = jnp.arange(n_sblk)
    cover = ((cstart[:, None] < (sj[None, :] + 1) * SEL_BLOCK)
             & (cend[:, None] >= sj[None, :] * SEL_BLOCK)).astype(jnp.float32)
    n_top = min(N_SELECT, n_sblk)
    L = n_top * SEL_BLOCK
    bi = jnp.arange(B)[:, None, None, None]
    gi = jnp.arange(G)[None, :, None, None]
    gi5 = jnp.arange(G)[None, :, None, None, None]
    ri5 = jnp.arange(R)[None, None, :, None, None]

    def attend_block(blk):
        t0 = blk * Q_BLOCK
        tq = t0 + jnp.arange(Q_BLOCK)
        qb = lax.dynamic_slice_in_dim(qh, t0, Q_BLOCK, axis=3)
        gb = lax.dynamic_slice_in_dim(gates, t0, Q_BLOCK, axis=3)
        s_c = (jnp.einsum("bgrqd,bgcd->bgrqc", qb, kc).astype(jnp.float32)
               + bias_gr[:, :, t5_bucket(tq[:, None] - cend[None, :])])
        p_c = masked_softmax(s_c, cend[None, :] <= tq[:, None])
        o_c = jnp.einsum("bgrqc,bgcd->bgrqd", p_c.astype(vc.dtype), vc)
        imp = jnp.einsum("bgrqc,cj->bgqj", p_c, cover)
        qblk = tq // SEL_BLOCK
        causal_j = sj[None, :] <= qblk[:, None]
        forced = causal_j & ((sj[None, :] == 0) | (sj[None, :] >= qblk[:, None] - 1))
        score = jnp.where(forced, SEL_FORCED, jnp.where(causal_j, imp, -1.0))
        top_v, top_i = lax.top_k(score, n_top)
        k_sel = ks[bi, gi, top_i].reshape(B, G, Q_BLOCK, L, hd)
        v_sel = vs[bi, gi, top_i].reshape(B, G, Q_BLOCK, L, hd)
        pos = top_i[..., None] * SEL_BLOCK + jnp.arange(SEL_BLOCK)
        mask_s = ((top_v >= 0.0)[..., None] & (pos <= tq[:, None, None])).reshape(B, G, Q_BLOCK, L)
        dist_s = tq[:, None] - pos.reshape(B, G, Q_BLOCK, L)
        s_s = (jnp.einsum("bgrqd,bgqld->bgrql", qb, k_sel).astype(jnp.float32)
               + bias_gr[gi5, ri5, t5_bucket(dist_s)[:, :, None]])
        p_s = masked_softmax(s_s, mask_s[:, :, None])
        o_s = jnp.einsum("bgrql,bgqld->bgrqd", p_s.astype(v_sel.dtype), v_sel)
        kwb = lax.dynamic_slice_in_dim(kw, t0, WINDOW + Q_BLOCK, axis=2)
        vwb = lax.dynamic_slice_in_dim(vw, t0, WINDOW + Q_BLOCK, axis=2)
        sk = t0 - WINDOW + jnp.arange(WINDOW + Q_BLOCK)
        dist_w = tq[:, None] - sk[None, :]
        mask_w = (dist_w >= 0) & (dist_w < WINDOW) & (sk[None, :] >= 0)
        s_w = (jnp.einsum("bgrqd,bgsd->bgrqs", qb, kwb).astype(jnp.float32)
               + bias_gr[:, :, t5_bucket(dist_w)])
        p_w = masked_softmax(s_w, mask_w)
        o_w = jnp.einsum("bgrqs,bgsd->bgrqd", p_w.astype(vwb.dtype), vwb)
        return gb[..., 0:1] * o_c + gb[..., 1:2] * o_s + gb[..., 2:3] * o_w

    o = lax.map(attend_block, jnp.arange(T // Q_BLOCK))
    return o.transpose(1, 0, 4, 2, 3, 5).reshape(B, T, Q_W)

def hybrid_layer(x, rel_bias, norm_mix, w_in, conv_w, conv_b, gate_a_w, gate_a_b, gate_x_w, gate_x_b,
                 lru_lambda, phi_k_pe, phi_k_w1, phi_k_w2, phi_v_pe, phi_v_w1, phi_v_w2,
                 q_norm, kc_norm, ks_norm, kw_norm, proj_a, proj_b, w_out,
                 norm_mlp, w_mlp_in, w_mlp_out):
    xn = rmsnorm(x, norm_mix)
    cuts = [int(c) for c in np.cumsum(SPLIT_SIZES)[:-1]]
    (u_rnn, u_gate, q, k_c, v_c, k_s, v_s, k_w, v_w, g_nsa, g_a, g_b) = jnp.split(xn @ w_in, cuts, axis=-1)
    h_a = rg_lru(causal_depthwise_conv(u_rnn, conv_w, conv_b), gate_a_w, gate_a_b, gate_x_w, gate_x_b, lru_lambda)
    y_a = h_a * jax.nn.gelu(u_gate, approximate=True)
    y_b = nsa_mixer(q, k_c, v_c, k_s, v_s, k_w, v_w, g_nsa, rel_bias,
                    phi_k_pe, phi_k_w1, phi_k_w2, phi_v_pe, phi_v_w1, phi_v_w2,
                    q_norm, kc_norm, ks_norm, kw_norm)
    merged = jax.nn.sigmoid(g_a) * (y_a @ proj_a) + jax.nn.sigmoid(g_b) * (y_b @ proj_b)
    h = x + merged @ w_out
    z = rmsnorm(h, norm_mlp) @ w_mlp_in
    return h + jnp.square(jax.nn.relu(z)) @ w_mlp_out

def second_inputs(seed: int = 0) -> dict:
    key = jax.random.key(seed)
    ks = jax.random.split(key, 32)
    nrm = lambda k, shape, scale: jax.random.normal(k, shape, jnp.float32) * scale
    gain = lambda k, shape: 1.0 + 0.05 * jax.random.normal(k, shape, jnp.float32)
    a0 = jax.random.uniform(ks[9], (DEPTH_2, D_RNN), jnp.float32, minval=0.9, maxval=0.999)
    s = a0 ** (1.0 / LRU_C)
    lam = jnp.log(s) - jnp.log1p(-s)
    cw = CMP_BLOCK * HEAD_DIM
    return {
        "x": nrm(ks[0], (BATCH, SEQ, D_MODEL), 1.0),
        "norm_mix": gain(ks[1], (DEPTH_2, D_MODEL)),
        "w_in": nrm(ks[2], (DEPTH_2, D_MODEL, D_IN), D_MODEL ** -0.5),
        "conv_w": nrm(ks[3], (DEPTH_2, CONV_W, D_RNN), CONV_W ** -0.5),
        "conv_b": nrm(ks[4], (DEPTH_2, D_RNN), 0.1),
        "gate_a_w": nrm(ks[5], (DEPTH_2, LRU_BLOCKS, LRU_BLOCK_W, LRU_BLOCK_W), LRU_BLOCK_W ** -0.5),
        "gate_a_b": nrm(ks[6], (DEPTH_2, LRU_BLOCKS, LRU_BLOCK_W), 0.1),
        "gate_x_w": nrm(ks[7], (DEPTH_2, LRU_BLOCKS, LRU_BLOCK_W, LRU_BLOCK_W), LRU_BLOCK_W ** -0.5),
        "gate_x_b": nrm(ks[8], (DEPTH_2, LRU_BLOCKS, LRU_BLOCK_W), 0.1),
        "lru_lambda": lam,
        "phi_k_pe": nrm(ks[10], (DEPTH_2, CMP_BLOCK, HEAD_DIM), 0.1),
        "phi_k_w1": nrm(ks[11], (DEPTH_2, cw, PHI_HIDDEN), cw ** -0.5),
        "phi_k_w2": nrm(ks[12], (DEPTH_2, PHI_HIDDEN, HEAD_DIM), PHI_HIDDEN ** -0.5),
        "phi_v_pe": nrm(ks[13], (DEPTH_2, CMP_BLOCK, HEAD_DIM), 0.1),
        "phi_v_w1": nrm(ks[14], (DEPTH_2, cw, PHI_HIDDEN), cw ** -0.5),
        "phi_v_w2": nrm(ks[15], (DEPTH_2, PHI_HIDDEN, HEAD_DIM), PHI_HIDDEN ** -0.5),
        "q_norm": gain(ks[16], (DEPTH_2, HEAD_DIM)),
        "kc_norm": gain(ks[17], (DEPTH_2, HEAD_DIM)),
        "ks_norm": gain(ks[18], (DEPTH_2, HEAD_DIM)),
        "kw_norm": gain(ks[19], (DEPTH_2, HEAD_DIM)),
        "rel_bias": nrm(ks[20], (REL_BUCKETS, N_HEADS_2), 0.5),
        "proj_a": nrm(ks[21], (DEPTH_2, D_RNN, D_MODEL), D_RNN ** -0.5),
        "proj_b": nrm(ks[22], (DEPTH_2, Q_W, D_MODEL), Q_W ** -0.5),
        "w_out": nrm(ks[23], (DEPTH_2, D_MODEL, D_MODEL), D_MODEL ** -0.5),
        "norm_mlp": gain(ks[24], (DEPTH_2, D_MODEL)),
        "w_mlp_in": nrm(ks[25], (DEPTH_2, D_MODEL, D_FF), D_MODEL ** -0.5),
        "w_mlp_out": nrm(ks[26], (DEPTH_2, D_FF, D_MODEL), D_FF ** -0.5),
    }

def second_block(x, norm_mix, w_in, conv_w, conv_b, gate_a_w, gate_a_b, gate_x_w, gate_x_b, lru_lambda,
              phi_k_pe, phi_k_w1, phi_k_w2, phi_v_pe, phi_v_w1, phi_v_w2,
              q_norm, kc_norm, ks_norm, kw_norm, rel_bias, proj_a, proj_b, w_out,
              norm_mlp, w_mlp_in, w_mlp_out):
    h = x
    for l in range(DEPTH_2):
        h = hybrid_layer(h, rel_bias, norm_mix[l], w_in[l], conv_w[l], conv_b[l],
                         gate_a_w[l], gate_a_b[l], gate_x_w[l], gate_x_b[l], lru_lambda[l],
                         phi_k_pe[l], phi_k_w1[l], phi_k_w2[l], phi_v_pe[l], phi_v_w1[l], phi_v_w2[l],
                         q_norm[l], kc_norm[l], ks_norm[l], kw_norm[l],
                         proj_a[l], proj_b[l], w_out[l], norm_mlp[l], w_mlp_in[l], w_mlp_out[l])
    return h


def setup_inputs(seed=0):
    out = dict(first_inputs(seed))
    for name, value in second_inputs(seed + 1).items():
        if name != "x":
            out[name + "_2"] = value
    return out


def reference(
    x, p, norm_mix, w_in, w_dw, b_dw, ln_conv_g, ln_conv_b, w_attn_out, w_conv_out, b_conv_out,
    w_out, norm_ffn, w_route_group, b_route_group, w_route_expert, b_route_expert, w_exp_gate,
    w_exp_up, w_exp_down, norm_ple, w_ple_proj, w_ple_gate, norm_final, norm_mix_2, w_in_2,
    conv_w_2, conv_b_2, gate_a_w_2, gate_a_b_2, gate_x_w_2, gate_x_b_2, lru_lambda_2,
    phi_k_pe_2, phi_k_w1_2, phi_k_w2_2, phi_v_pe_2, phi_v_w1_2, phi_v_w2_2, q_norm_2, kc_norm_2,
    ks_norm_2, kw_norm_2, rel_bias_2, proj_a_2, proj_b_2, w_out_2, norm_mlp_2, w_mlp_in_2,
    w_mlp_out_2,
):
    x = first_block(
        x, p, norm_mix, w_in, w_dw, b_dw, ln_conv_g, ln_conv_b, w_attn_out, w_conv_out,
        b_conv_out, w_out, norm_ffn, w_route_group, b_route_group, w_route_expert,
        b_route_expert, w_exp_gate, w_exp_up, w_exp_down, norm_ple, w_ple_proj, w_ple_gate,
        norm_final,
    )
    return second_block(
        x, norm_mix_2, w_in_2, conv_w_2, conv_b_2, gate_a_w_2, gate_a_b_2, gate_x_w_2,
        gate_x_b_2, lru_lambda_2, phi_k_pe_2, phi_k_w1_2, phi_k_w2_2, phi_v_pe_2, phi_v_w1_2,
        phi_v_w2_2, q_norm_2, kc_norm_2, ks_norm_2, kw_norm_2, rel_bias_2, proj_a_2, proj_b_2,
        w_out_2, norm_mlp_2, w_mlp_in_2, w_mlp_out_2,
    )


_drawn_inputs = setup_inputs


def setup_inputs(seed=0):
    import zlib

    import numpy as np

    out = dict(_drawn_inputs(seed))
    spreads = {}
    factors = {'b_route_group': 2.852,
     'gate_a_b_2': 8.0,
     'gate_x_b_2': 4.384,
     'phi_k_pe_2': 8.0,
     'phi_v_pe_2': 3.797,
     'q_norm_2': 8.0,
     'kc_norm_2': 8.0,
     'ks_norm_2': 8.0,
     'kw_norm_2': 8.0}
    for name, (base, spread) in spreads.items():
        noise = np.random.default_rng([zlib.crc32(name.encode()), seed]).standard_normal(out[name].shape)
        drawn = base * np.exp(spread * noise) if base else spread * noise
        out[name] = __import__('jax').numpy.asarray(drawn.astype(out[name].dtype))
    for name, factor in factors.items():
        out[name] = (out[name] * factor).astype(out[name].dtype)
    return out
```

```python
from contextlib import ExitStack

import concourse.bass as bass
import numpy as np
from concourse import mybir

F32 = mybir.dt.float32
U32 = mybir.dt.uint32
ALU = mybir.AluOpType
ACT = mybir.ActivationFunctionType
AX_X = mybir.AxisListType.X

P = 128
T = 256
TT = T // P
D = 1024
DC = D // P
BANK = 512
BANKS = 8
EPS = 1e-6
NEG = -1e30

DEPTH = 2
HEADS, HD = 8, 64
AW = HEADS * HD
AC = AW // P
CW = 512
CC = CW // P
TAPS = 31
GROUPS, PER_GROUP, FF = 4, 8, 512
EXPERTS = GROUPS * PER_GROUP
FC = FF // P
PLE = 256
ROUTES = GROUPS + EXPERTS
W_IN_COLS = 3 * AW + 2 * CW + 2 * D
DILATED = ((128, 1), (512, 4), (2048, 16))

RNN, RP = 1344, 112
RC = RNN // RP
RBLOCKS = 4
RB = RC // RBLOCKS
RTAPS = 4
H2, KVG = 16, 4
HPG = H2 // KVG
KVW = KVG * HD
CMP, STRIDE = 32, 16
NCMP = (T - CMP) // STRIDE + 1
PHI = 256
BUCKETS, MAX_DIST = 32, 128
SKEW = 2 * T + 1
DFF = 4 * D
IN2 = dict(u_rnn=0, u_gate=RNN, q=2 * RNN)
IN2["kc"] = IN2["q"] + H2 * HD
IN2["ks"] = IN2["kc"] + 2 * KVW
IN2["kw"] = IN2["ks"] + 2 * KVW
IN2["g_nsa"] = IN2["kw"] + 2 * KVW
IN2["g_a"] = IN2["g_nsa"] + 3 * H2
IN2["g_b"] = IN2["g_a"] + D
assert IN2["g_b"] + D == 7344

C_ID, C_MASK, C_COS, C_SIN, C_HEAD, C_IOTA, C_SEEN = 0, 128, 512, 768, 1024, 1152, 1160
C_COLS = C_SEEN + TT * NCMP


def constants():
    c = np.zeros((P, C_COLS), np.float32)
    c[:, C_ID:C_ID + P] = np.eye(P)
    for n, off in enumerate((0, P, 0)):
        d = off + np.arange(P)[:, None] - np.arange(P)[None, :]
        count = sum(((d >= 0) & (d % dil == 0) & (d <= win)).astype(np.float32) for win, dil in DILATED)
        c[:, C_MASK + n * P:C_MASK + (n + 1) * P] = np.where(count > 0, np.log(np.maximum(count, 1)), NEG)
    inv = np.power(np.float32(10000.0), -np.arange(0, HD, 2, dtype=np.float32) / np.float32(HD))
    ang = (np.arange(T, dtype=np.float32)[:, None] * inv[None, :]).T.astype(np.float32)
    for q in range(4):
        c[32 * q:32 * q + 32, C_COS:C_COS + T] = np.cos(ang)
        c[32 * q:32 * q + 32, C_SIN:C_SIN + T] = np.sin(ang) * (-1 if q % 2 == 0 else 1)
    for h in range(2):
        c[HD * h:HD * h + HD, C_HEAD + HD * h:C_HEAD + HD * h + HD] = 1.0 / HD
    c[:, C_IOTA:C_IOTA + 8] = np.arange(8)
    ends = np.arange(NCMP) * STRIDE + CMP - 1
    for t in range(TT):
        c[:, C_SEEN + t * NCMP:C_SEEN + (t + 1) * NCMP] = ends[None, :] <= (t * P + np.arange(P))[:, None]

    def one_hot(d):
        d = d.reshape(-1)
        near = BUCKETS // 2
        df = np.maximum(d, 1).astype(np.float32)
        large = near + (np.log(df / near) / np.float32(np.log(MAX_DIST / near)) * (BUCKETS - near)).astype(np.int32)
        b = np.where(d < near, d, np.minimum(large, BUCKETS - 1))
        b = np.where(d < 0, BUCKETS, b)
        return (np.arange(BUCKETS + 1)[:, None] == b[None, :]).astype(np.float32)

    far = one_hot(2 * T // 2 - 1 - np.arange(2 * T))
    cmp_d = np.arange(T).reshape(TT, 1, P) - ends.reshape(1, NCMP, 1)
    return c, far, one_hot(cmp_d)


class Chain:

    def __init__(self, eng, sem):
        self.eng, self.sem, self.n = eng, sem, 0

    def __call__(self, ins):
        ins.then_inc(self.sem, 1)
        self.n += 1

    def settle(self):
        self.eng.wait_ge(self.sem, self.n)


def clear(nc, sems):
    nums = sorted(s.num for s in sems)
    assert nums == list(range(nums[0], nums[0] + len(nums)))
    nc.sync.sem_clear(range(nums[0], nums[-1] + 1))
    nc.all_engine_barrier()


def first_block_layer(nc, ctx, dram, const, keep, layer):
    R = 6

    def sb(name, shape, dt=F32):
        return ctx.enter_context(nc.sbuf_tensor("l_" + name, shape, dt))

    sems = []

    def sem(name):
        sems.append(ctx.enter_context(nc.semaphore("l_" + name)))
        return sems[-1]

    xT, hT, sq, eps, ones = keep["xT"], keep["hT"], keep["sq"], keep["eps"], keep["ones"]
    ps = keep["ps"]
    ident = const[:, C_ID:C_ID + P]
    ring = sb("ring", [P, R, 4096])
    rows = sb("rows", [48, P])
    taprows = sb("taprows", [TAPS, CW])
    par = sb("par", [P, 48 + CC * TAPS])
    wroute = sb("wroute", [P, DC, ROUTES])
    broute = sb("broute", [1, ROUTES])
    one_row = sb("one_row", [1, P])
    ptok = sb("ptok", [P, TT, PLE])
    pT = sb("pT", [P, PLE // P, T])
    stat = sb("stat", [P, T])
    rstd = sb("rstd", [P, T])
    u = sb("u", [P, CC, TAPS - 1 + T])
    conv = sb("conv", [P, CC, T])
    sig = sb("sig", [P, 2, BANK])
    raw = sb("raw", [P, 2, BANK])
    rot = sb("rot", [P, 2, BANK])
    qk = sb("qk", [P, 2, AC, T])
    v = sb("v", [P, TT, AW])
    gates_ab = sb("gates_ab", [P, 2, DC, T])
    attn = sb("attn", [P, AC, T])
    merged = sq
    S = sb("S", [P, 2, 3 * P])
    E = sb("E", [P, 2, 3 * P])
    PT = sb("PT", [P, 2, 3 * P])
    smax = sb("smax", [P, 2, 2])
    ssum = sb("ssum", [P, 2, 2])
    logit = sb("logit", [P, TT, ROUTES])
    rt = sb("rt", [P, TT, 64])
    top = sb("top", [P, TT, 2, 8])
    topi = sb("topi", [P, TT, 2, 8], U32)
    gate = sb("gate", [P, TT, EXPERTS])
    yacc = gates_ab[:, 0]
    yacc = yacc.rearrange("p (t c) n -> p t (c n)", t=TT)
    silu = sb("silu", [P, FC, T])
    hid = qk

    names = ("norm_mix", "b_dw", "ln_conv_g", "ln_conv_b", "b_conv_out", "norm_ffn", "norm_ple")
    col, at = {}, 0
    for n in names:
        col[n] = at
        at += dram[n].shape[-1] // P
    n_rows = at
    TAP0 = 48

    def param(name, c):
        return par[:, col[name] + c:col[name] + c + 1]

    def tap(c, k):
        return par[:, TAP0 + c * TAPS + k:TAP0 + c * TAPS + k + 1]

    stages = dict(params=1, mean_mix=1, cu=2, cg=2, q=2, k=2, v=2, ga=4, gb=4, score=HEADS, probT=HEADS,
                  o=AC, y_a=4, ln_mean=1, ln_var=1, y_b=4, w_out=4, mean_ffn=1, route=1,
                  gate_up=2 * FC, down=2 * 4, turn=4, pT=1, mean_ple=1, ple_gate=4, ple=4)
    banks, n = {}, 0
    for stage, count in stages.items():
        if stage in ("gate_up", "down"):
            n = 0
            continue
        for i in range(count):
            if stage in ("score", "probT", "o"):
                banks[stage, i] = {"score": i % 3, "probT": 3 + i % 3, "o": 6 + i % 2}[stage]
            else:
                banks[stage, i] = n % BANKS
                n += 1

    def bank(stage, i=0):
        return ps[banks[stage, i]]

    exp_bank = ps.__getitem__

    filled = {s: sem("filled_" + s) for s in stages}
    emptied = {s: sem("emptied_" + s) for s in stages}
    landed = [sem(f"landed{i}") for i in range(R)]
    params_in = sem("params_in")
    dve_steps, act_steps = sem("dve_steps"), sem("act_steps")
    squares = {n: sem("squares_" + n) for n in ("mix", "ffn", "ple")}
    normed = {n: sem("normed_" + n) for n in ("mix", "ffn", "ple")}
    centred, conv_act, rope_raw = sem("centred"), sem("conv_act"), sem("rope_raw")
    conv_out = sem("conv_out")
    ln_done = sem("ln_done")
    smax_ready, exps_ready, probs_ready = sem("smax_ready"), sem("exps_ready"), sem("probs_ready")
    silu_ready = sem("silu_ready")
    lmax_ready, lexp_ready, pair_ready, pexp_ready = sem("lmax"), sem("lexp"), sem("pair"), sem("pexp")

    lay = bass.ds(layer, 1)

    def w_cols(name, c0, n=BANK):
        return lambda: dram[name][lay, :, c0:c0 + n].rearrange("a (c p) n -> p (a c) n", p=P)

    def w_all(name):
        return lambda: dram[name][lay].rearrange("a (c p) n -> p (a c) n", p=P)

    cu0, cg0 = 3 * AW, 3 * AW + CW
    ga0, gb0 = cg0 + CW, cg0 + CW + D
    stream = [
        (w_cols("w_in", cu0), "cu", 2), (w_cols("w_in", cg0), "cg", 2),
        (w_cols("w_in", 0), "q", 2), (w_cols("w_in", AW), "k", 2), (w_cols("w_in", 2 * AW), "v", 2),
        (w_cols("w_in", ga0), "ga", 2), (w_cols("w_in", ga0 + BANK), "ga", 4),
        (w_cols("w_in", gb0), "gb", 2), (w_cols("w_in", gb0 + BANK), "gb", 4),
        (w_all("w_attn_out"), "y_a", 4), (w_all("w_conv_out"), "y_b", 4),
        (w_cols("w_out", 0), "w_out", 2), (w_cols("w_out", BANK), "w_out", 4),
    ]
    N0 = len(stream)
    TURNS = EXPERTS // 2
    PER_TURN = 6
    tail = [(w_cols("w_ple_gate", 0), "ple_gate", 2), (w_cols("w_ple_gate", BANK), "ple_gate", 4),
            (w_all("w_ple_proj"), "ple", 4)]

    def slot(i, rows_=DC, part=P):
        return ring[0:part, i % R].rearrange("p (c n) -> p c n", c=rows_)

    def expert_weights(e, j):
        name = ("w_exp_gate", "w_exp_up", "w_exp_down")[j % 3]
        w = dram[name][lay, bass.ds(e * 2 + j // 3, 1)].rearrange("a b (c p) n -> p (a b c) n", p=P)
        return w, (FC if j % 3 == 2 else DC)

    with nc.Block(no_gpsimd_drain=True) as block:

        @block.sync
        def _(sp):
            at = 0
            for n in names:
                k = dram[n].shape[-1] // P
                sp.dma_start(rows[at:at + k, :], dram[n][lay].rearrange("a (c p) -> (a c) p", p=P)).then_inc(params_in, 16)
                at += k
            sp.dma_start(taprows[:], dram["w_dw"][lay].rearrange("a k c -> (a k) c")).then_inc(params_in, 16)
            sp.dma_start(wroute[:, :, 0:GROUPS], dram["w_route_group"][lay].rearrange("a (c p) n -> p (a c) n", p=P)).then_inc(params_in, 16)
            sp.dma_start(wroute[:, :, GROUPS:], dram["w_route_expert"][lay].rearrange("a (c p) n -> p (a c) n", p=P)).then_inc(params_in, 16)
            sp.dma_start(broute[:, 0:GROUPS], dram["b_route_group"][lay]).then_inc(params_in, 16)
            sp.dma_start(broute[:, GROUPS:], dram["b_route_expert"][lay]).then_inc(params_in, 16)
            sp.dma_start(ptok[:], dram["p"][lay, 0].rearrange("a (t p) n -> p (a t) n", p=P)).then_inc(params_in, 16)
            for i, (src, _, _) in enumerate(stream):
                if i >= R:
                    _, stage, n = stream[i - R]
                    sp.wait_ge(filled[stage], n)
                s = src()
                sp.dma_start(slot(i, s.shape[1]), s).then_inc(landed[i % R], 16)
            for j in range(PER_TURN):
                _, stage, n = stream[N0 + j - R]
                sp.wait_ge(filled[stage], n)
                s, k = expert_weights(0, j)
                sp.dma_start(slot(N0 + j, k), s).then_inc(landed[(N0 + j) % R], 16)
            with sp.Fori(1, TURNS) as e:
                for j in range(PER_TURN):
                    if j % 3 == 2:
                        sp.wait_ge(filled["down"], (e - 1) * 8 + (j // 3) * 4 + 4)
                    else:
                        sp.wait_ge(filled["gate_up"], (e - 1) * 8 + (j // 3) * 4 + 4)
                    s, k = expert_weights(e, j)
                    sp.dma_start(slot(N0 + j, k), s).then_inc(landed[(N0 + j) % R], 16)
            for j, (src, _, _) in enumerate(tail):
                sp.wait_ge(filled["down" if j % 3 == 2 else "gate_up"], (TURNS - 1) * 8 + (j // 3) * 4 + 4)
                s = src()
                sp.dma_start(slot(N0 + PER_TURN * TURNS + j, s.shape[1])[:, :, 0:s.shape[2]], s)\
                    .then_inc(landed[(N0 + j) % R], 16)

        @block.tensor
        def _(pe):
            last_in = {}

            def claim(stage, i):
                b = banks[stage, i]
                if b in last_in:
                    s, n = last_in[b]
                    pe.wait_ge(emptied[s], n + 1)
                last_in[b] = (stage, i)
                return ps[b]

            def weights(i):
                pe.wait_ge(landed[i % R], 16 * (i // R + 1))

            def mean(name, src, chunks, sem_ready, stage, step=4):
                out = claim(stage, 0)
                for c in range(chunks):
                    if c % step == 0:
                        pe.wait_ge(sem_ready, c // step + 1)
                    mm = nc.tensor.matmul(out[:, 0:T], ones[name][:], src[:, c, :], start=(c == 0), stop=(c == chunks - 1))
                mm.then_inc(filled[stage], 1)

            def project(i, stage, n0, src, kc, m0=0, cols=4):
                weights(i)
                w = slot(i, kc)
                for b in range(cols // 2):
                    out = claim(stage, n0 + b)
                    for m in range(2):
                        for k in range(kc):
                            mm = nc.tensor.matmul(out[:, m * T:(m + 1) * T], w[:, k, (m0 + 2 * b + m) * P:(m0 + 2 * b + m + 1) * P],
                                                  src[:, k, :], start=(k == 0), stop=(k == kc - 1))
                    mm.then_inc(filled[stage], 1)

            pe.wait_ge(params_in, 16 * (len(names) + 6))
            out = claim("params", 0)
            nc.tensor.transpose(out[:, 0:n_rows], rows[0:n_rows, :], ident[0:n_rows, 0:n_rows])
            for c in range(CC):
                mm = nc.tensor.transpose(out[:, TAP0 + c * TAPS:TAP0 + (c + 1) * TAPS],
                                         taprows[:, c * P:(c + 1) * P], ident[0:TAPS, 0:TAPS])
            mm.then_inc(filled["params"], 1)
            mean("D", sq, DC, squares["mix"], "mean_mix")
            pe.wait_ge(normed["mix"], DC)
            for i, stage in enumerate(("cu", "cg", "q", "k")):
                project(i, stage, 0, hT, DC)
            weights(4)
            for t in range(TT):
                out = claim("v", t)
                for k in range(DC):
                    mm = nc.tensor.matmul(out[:], hT[:, k, t * P:(t + 1) * P], slot(4)[:, k, :], start=(k == 0), stop=(k == DC - 1))
                mm.then_inc(filled["v"], 1)
            for i, (stage, n0) in enumerate((("ga", 0), ("ga", 2), ("gb", 0), ("gb", 2))):
                project(5 + i, stage, n0, hT, DC)

            pe.wait_ge(emptied["q"], 2)
            pe.wait_ge(emptied["k"], 2)
            pe.wait_ge(emptied["v"], 2)

            def score(h):
                out = claim("score", h)
                r = slice(HD * (h % 2), HD * (h % 2) + HD)
                q, k = qk[r, 0, h // 2, :], qk[r, 1, h // 2, :]
                nc.tensor.matmul(out[:, 0:P], q[:, 0:P], k[:, 0:P], start=True, stop=True)
                nc.tensor.matmul(out[:, P:3 * P], q[:, P:T], k, start=True, stop=True).then_inc(filled["score"], 1)

            def prob_t(h):
                out = claim("probT", h)
                pe.wait_ge(probs_ready, h + 1)
                e = E[:, h % 2]
                nc.tensor.transpose(out[:, 0:P], e[:, 0:P], ident)
                nc.tensor.transpose(out[:, P:T], e[:, P:T], ident)
                nc.tensor.transpose(out[:, T:3 * P], e[:, T:3 * P], ident).then_inc(filled["probT"], 1)

            def values(h):
                if h % 2 == 0:
                    claim("o", h // 2)
                pe.wait_ge(emptied["probT"], h + 1)
                r = slice(HD * (h % 2), HD * (h % 2) + HD)
                out = ps[banks["o", h // 2]][r, 0:T]
                pt = PT[:, h % 2]
                nc.tensor.matmul(out, v[:, 0, h * HD:(h + 1) * HD], pt[:, 0:T], start=True, stop=False)
                mm = nc.tensor.matmul(out[:, P:T], v[:, 1, h * HD:(h + 1) * HD], pt[:, T:3 * P], start=False, stop=True)
                mm.then_inc(filled["o"], 1)

            for i in range(HEADS + 3):
                if i < HEADS:
                    score(i)
                if 2 <= i < HEADS + 2:
                    prob_t(i - 2)
                if i >= 3:
                    values(i - 3)

            mean("C", conv, CC, conv_out, "ln_mean", 1)
            mean("C", sq, CC, centred, "ln_var", 1)
            pe.wait_ge(emptied["o"], AC)
            project(9, "y_a", 0, attn, AC, cols=8)
            pe.wait_ge(conv_act, CC)
            project(10, "y_b", 0, conv, CC, cols=8)
            pe.wait_ge(emptied["y_b"], 4)
            project(11, "w_out", 0, merged, DC)
            project(12, "w_out", 2, merged, DC)
            mean("D", sq, DC, squares["ffn"], "mean_ffn")
            pe.wait_ge(normed["ffn"], DC)
            out = claim("route", 0)
            for t in range(TT):
                o = out[:, t * ROUTES:(t + 1) * ROUTES]
                for k in range(DC):
                    nc.tensor.matmul(o, hT[:, k, t * P:(t + 1) * P], wroute[:, k, :], start=(k == 0), stop=False)
                mm = nc.tensor.matmul(o, one_row[:], broute[:], start=False, stop=True)
            mm.then_inc(filled["route"], 1)

            for b in range(BANKS):
                s, n = last_in.pop(b)
                pe.wait_ge(emptied[s], n + 1)
            pe.sem_inc(emptied["gate_up"], 4)
            pe.sem_inc(emptied["down"], 4)
            with pe.Fori(0, TURNS) as e:
                for j in range(2):
                    i = N0 + 3 * j
                    pe.wait_ge(landed[i % R], (e + (i // R + 1)) * 16)
                    pe.wait_ge(landed[(i + 1) % R], (e + ((i + 1) // R + 1)) * 16)
                    for f in range(FC):
                        out = ps[f]
                        pe.wait_ge(emptied["gate_up"], e * 8 + (4 * j + f + 1))
                        for half in range(2):
                            for k in range(DC):
                                mm = nc.tensor.matmul(out[:, half * T:(half + 1) * T], slot(i + half)[:, k, f * P:(f + 1) * P],
                                                      hT[:, k, :], start=(k == 0), stop=(k == DC - 1))
                        mm.then_inc(filled["gate_up"], 1)
                    pe.wait_ge(landed[(i + 2) % R], (e + ((i + 2) // R + 1)) * 16)
                    pe.wait_ge(emptied["gate_up"], e * 8 + (4 * j + 4 + 4))
                    for t in range(TT):
                        for half in range(2):
                            n = 2 * t + half
                            pe.wait_ge(emptied["down"], e * 8 + (4 * j + n + 1))
                            for k in range(FC):
                                mm = nc.tensor.matmul(ps[4 + n][:], hid[:, j, k, t * P:(t + 1) * P],
                                                      slot(i + 2, FC)[:, k, half * BANK:(half + 1) * BANK],
                                                      start=(k == 0), stop=(k == FC - 1))
                            mm.then_inc(filled["down"], 1)
            pe.wait_ge(emptied["gate_up"], TURNS * 8 + 4)
            pe.wait_ge(emptied["down"], TURNS * 8 + 4)
            for b in range(4):
                out = claim("turn", b)
                for m in range(2):
                    for t in range(TT):
                        c = 2 * b + m
                        mm = nc.tensor.transpose(out[:, m * T + t * P:m * T + (t + 1) * P], yacc[:, t, c * P:(c + 1) * P], ident)
                mm.then_inc(filled["turn"], 1)
            out = claim("pT", 0)
            for c in range(PLE // P):
                for t in range(TT):
                    mm = nc.tensor.transpose(out[:, c * T + t * P:c * T + (t + 1) * P], ptok[:, t, c * P:(c + 1) * P], ident)
            mm.then_inc(filled["pT"], 1)
            mean("D", sq, DC, squares["ple"], "mean_ple")
            pe.wait_ge(normed["ple"], DC)
            N1 = N0 + PER_TURN * TURNS
            project(N1, "ple_gate", 0, hT, DC)
            project(N1 + 1, "ple_gate", 2, hT, DC)
            pe.wait_ge(emptied["pT"], 1)
            weights(N1 + 2)
            for b in range(4):
                out = claim("ple", b)
                for m in range(2):
                    for k in range(PLE // P):
                        c = 2 * b + m
                        w = slot(N1 + 2, PLE // P)
                        mm = nc.tensor.matmul(out[:, m * T:(m + 1) * T], w[:, k, c * P:(c + 1) * P], pT[:, k, :],
                                              start=(k == 0), stop=(k == PLE // P - 1))
                mm.then_inc(filled["ple"], 1)

        @block.scalar
        def _(act):
            step = Chain(act, act_steps)

            def norm(name, src=xT, stage=None):
                for h in range(2):
                    nc.scalar.activation(sq[:, 4 * h:4 * h + 4, :], src[:, 4 * h:4 * h + 4, :], ACT.Square).then_inc(squares[name], 1)
                act.wait_ge(filled["mean_" + name], 1)
                nc.scalar.activation(stat[:], bank("mean_" + name)[:, 0:T], ACT.Sqrt, bias=eps[:, 0:1]).then_inc(emptied["mean_" + name], 1)

            norm("mix")
            for b in range(2):
                act.wait_ge(filled["cg"], b + 1)
                nc.scalar.activation(sig[:, b], bank("cg", b)[:], ACT.Sigmoid).then_inc(emptied["cg"], 1)
            for n, stage in enumerate(("q", "k")):
                for b in range(2):
                    act.wait_ge(filled[stage], b + 1)
                    if n == 1:
                        act.wait_ge(emptied["q"], b + 1)
                    src = bank(stage, b)
                    for g in range(4):
                        o = g ^ 1
                        step(nc.scalar.copy(rot[32 * g:32 * g + 32, b], src[32 * o:32 * o + 32, :]))
                    nc.scalar.copy(raw[:, b], src[:]).then_inc(rope_raw, 1)
            for t in range(TT):
                act.wait_ge(filled["v"], t + 1)
                nc.scalar.copy(v[:, t], bank("v", t)[:]).then_inc(emptied["v"], 1)
            for n, stage in enumerate(("ga", "gb")):
                for b in range(4):
                    act.wait_ge(filled[stage], b + 1)
                    nc.scalar.activation(gates_ab[:, n, 2 * b:2 * b + 2, :].rearrange("p c n -> p (c n)"),
                                         bank(stage, b)[:], ACT.Sigmoid).then_inc(emptied[stage], 1)
            for h in range(HEADS + 1):
                if h < HEADS:
                    act.wait_ge(smax_ready, h + 1)
                    if h >= 2:
                        act.wait_ge(filled["probT"], h - 1)
                    e, s = E[:, h % 2], S[:, h % 2]
                    nc.scalar.activation(e[:, 0:P], s[:, 0:P], ACT.Exp, bias=smax[:, h % 2, 0:1],
                                         accum_out=ssum[:, h % 2, 0:1]).then_inc(exps_ready, 1)
                    nc.scalar.activation(e[:, P:], s[:, P:], ACT.Exp, bias=smax[:, h % 2, 1:2],
                                         accum_out=ssum[:, h % 2, 1:2]).then_inc(exps_ready, 1)
                if h >= 1:
                    g = h - 1
                    act.wait_ge(filled["probT"], g + 1)
                    if g >= 2:
                        act.wait_ge(filled["o"], g - 1)
                    nc.scalar.copy(PT[:, g % 2], bank("probT", g)[:, 0:3 * P]).then_inc(emptied["probT"], 1)
                    if g % 2 and g >= 3:
                        c = g // 2 - 1
                        act.wait_ge(filled["o"], 2 * c + 2)
                        nc.scalar.copy(attn[:, c, :], bank("o", c)[:, 0:T]).then_inc(emptied["o"], 1)
            act.wait_ge(filled["o"], HEADS)
            nc.scalar.copy(attn[:, AC - 1, :], bank("o", AC - 1)[:, 0:T]).then_inc(emptied["o"], 1)
            act.wait_ge(filled["ln_var"], 1)
            nc.scalar.activation(stat[:], bank("ln_var")[:, 0:T], ACT.Sqrt, bias=eps[:, 0:1]).then_inc(emptied["ln_var"], 1)
            for c in range(CC):
                act.wait_ge(ln_done, c + 1)
                nc.scalar.activation(conv[:, c, :], conv[:, c, :], ACT.Silu, bias=param("ln_conv_b", c),
                                     scale=param("ln_conv_g", c)).then_inc(conv_act, 1)
            act.wait_ge(emptied["w_out"], 4)
            norm("ffn")
            act.wait_ge(lmax_ready, 1)
            for t in range(TT):
                nc.scalar.activation(rt[:, t, 4:8], logit[:, t, 0:GROUPS], ACT.Exp, bias=rt[:, t, 0:1],
                                     accum_out=rt[:, t, 1:2]).then_inc(lexp_ready, 1)
            act.wait_ge(pair_ready, 1)
            nc.scalar.activation(rt[:, :, 21:22], rt[:, :, 20:21], ACT.Exp).then_inc(pexp_ready, 1)
            with act.Fori(0, TURNS) as e:
                for j in range(2):
                    for f in range(FC):
                        act.wait_ge(filled["gate_up"], e * 8 + (4 * j + f + 1))
                        nc.scalar.activation(silu[:, f], ps[f][:, 0:T], ACT.Silu).then_inc(silu_ready, 1)
            act.wait_ge(emptied["turn"], 4)
            norm("ple")
            act.wait_ge(filled["pT"], 1)
            nc.scalar.copy(pT[:].rearrange("p c n -> p (c n)"), bank("pT")[:]).then_inc(emptied["pT"], 1)
            for b in range(4):
                act.wait_ge(filled["ple_gate"], b + 1)
                nc.scalar.activation(gates_ab[:, 1, 2 * b:2 * b + 2, :].rearrange("p c n -> p (c n)"),
                                     bank("ple_gate", b)[:], ACT.Sigmoid).then_inc(emptied["ple_gate"], 1)

        @block.vector
        def _(dve):
            step = Chain(dve, dve_steps)
            vec = nc.vector

            def wide(x, n=2):
                return x.unsqueeze(1).broadcast_to([P, n, T])

            def normalise(name):
                dve.wait_ge(emptied["mean_" + name], 1)
                step(vec.reciprocal(rstd[:], stat[:]))
                step.settle()
                for c in range(DC):
                    vec.scalar_tensor_tensor(hT[:, c, :], xT[:, c, :], param("norm_" + name, c), rstd[:],
                                             ALU.mult, ALU.mult).then_inc(normed[name], 1)

            def chunks(b):
                return slice(2 * b, 2 * b + 2)

            def flat(x):
                return x.rearrange("p c n -> p (c n)")

            step(vec.memset(u[:, :, 0:TAPS - 1], 0.0))
            step(vec.memset(one_row[:], 1.0))
            dve.wait_ge(filled["params"], 1)
            vec.tensor_copy(par[:, 0:n_rows], bank("params")[:, 0:n_rows])
            vec.tensor_copy(par[:, TAP0:], bank("params")[:, TAP0:TAP0 + CC * TAPS]).then_inc(emptied["params"], 1)
            dve.wait_ge(emptied["params"], 1)
            step.settle()
            normalise("mix")
            for b in range(2):
                dve.wait_ge(emptied["cg"], b + 1)
                dve.wait_ge(filled["cu"], b + 1)
                vec.tensor_tensor(u[:, chunks(b), TAPS - 1:], bank("cu", b)[:].rearrange("p (c n) -> p c n", c=2),
                                  sig[:, b].rearrange("p (c n) -> p c n", c=2), ALU.mult).then_inc(emptied["cu"], 1)
            dve.wait_ge(emptied["cu"], 2)

            def taps(cs):
                for k in range(TAPS):
                    for c in cs:
                        x = u[:, c, k:k + T]
                        if k == 0:
                            step(vec.tensor_scalar(conv[:, c, :], x, tap(c, k), param("b_dw", c), ALU.mult, ALU.add))
                        elif k < TAPS - 1:
                            step(vec.scalar_tensor_tensor(conv[:, c, :], x, tap(c, k), conv[:, c, :], ALU.mult, ALU.add))
                        else:
                            vec.scalar_tensor_tensor(conv[:, c, :], x, tap(c, k), conv[:, c, :], ALU.mult, ALU.add).then_inc(conv_out, 1)
                    if k < TAPS - 1:
                        step.settle()

            def rope(n, stage):
                for b in range(2):
                    dve.wait_ge(rope_raw, 2 * n + b + 1)
                    three = "p (c n) -> p c n"
                    a, r = raw[:, b].rearrange(three, c=2), rot[:, b].rearrange(three, c=2)
                    step(vec.tensor_tensor(a, a, wide(const[:, C_COS:C_COS + T]), ALU.mult))
                    step(vec.tensor_tensor(r, r, wide(const[:, C_SIN:C_SIN + T]), ALU.mult))
                    step.settle()
                    vec.tensor_tensor(qk[:, n, chunks(b), :], a, r, ALU.add).then_inc(emptied[stage], 1)

            taps((0, 1))
            rope(0, "q")
            rope(1, "k")
            taps((2, 3))

            for h in range(HEADS + 1):
                if h < HEADS:
                    if h >= 2:
                        dve.wait_ge(exps_ready, 2 * (h - 1))
                    dve.wait_ge(filled["score"], h + 1)
                    s, m = S[:, h % 2], smax[:, h % 2]
                    vec.scalar_tensor_tensor(s, bank("score", h)[:, 0:3 * P], HD ** -0.5, const[:, C_MASK:C_MASK + 3 * P],
                                             ALU.mult, ALU.add).then_inc(emptied["score"], 1)
                    dve.wait_ge(emptied["score"], h + 1)
                    step(vec.tensor_reduce(m[:, 0:1], s[:, 0:P], AX_X, ALU.max))
                    step(vec.tensor_reduce(m[:, 1:2], s[:, P:], AX_X, ALU.max))
                    step.settle()
                    vec.tensor_scalar(m, m, -1.0, None, ALU.mult).then_inc(smax_ready, 1)
                if h >= 1:
                    g = (h - 1) % 2
                    dve.wait_ge(exps_ready, 2 * h)
                    step(vec.reciprocal(ssum[:, g], ssum[:, g]))
                    step.settle()
                    vec.tensor_scalar(E[:, g, 0:P], E[:, g, 0:P], ssum[:, g, 0:1], None, ALU.mult)
                    vec.tensor_scalar(E[:, g, P:], E[:, g, P:], ssum[:, g, 1:2], None, ALU.mult).then_inc(probs_ready, 1)

            dve.wait_ge(conv_out, CC)
            dve.wait_ge(filled["ln_mean"], 1)
            for c in range(CC):
                i = vec.tensor_tensor(conv[:, c, :], conv[:, c, :], bank("ln_mean")[:, 0:T], ALU.subtract)
                if c < CC - 1:
                    step(i)
            i.then_inc(emptied["ln_mean"], 1)
            dve.wait_ge(emptied["ln_mean"], 1)
            for c in range(CC):
                vec.tensor_tensor(sq[:, c, :], conv[:, c, :], conv[:, c, :], ALU.mult).then_inc(centred, 1)
            dve.wait_ge(emptied["ln_var"], 1)
            step(vec.reciprocal(rstd[:], stat[:]))
            step.settle()
            for c in range(CC):
                vec.tensor_tensor(conv[:, c, :], conv[:, c, :], rstd[:], ALU.mult).then_inc(ln_done, 1)
            dve.wait_ge(emptied["ga"], 4)
            dve.wait_ge(emptied["gb"], 4)
            for b in range(4):
                dve.wait_ge(filled["y_a"], b + 1)
                vec.tensor_tensor(flat(merged[:, chunks(b), :]), bank("y_a", b)[:], flat(gates_ab[:, 0, chunks(b), :]),
                                  ALU.mult).then_inc(emptied["y_a"], 1)
            dve.wait_ge(emptied["y_a"], 4)
            for b in range(4):
                dve.wait_ge(filled["y_b"], b + 1)
                for m in range(2):
                    c = 2 * b + m
                    step(vec.scalar_tensor_tensor(raw[:, b % 2, m * T:(m + 1) * T], bank("y_b", b)[:, m * T:(m + 1) * T],
                                                  param("b_conv_out", c), gates_ab[:, 1, c, :], ALU.add, ALU.mult))
                step.settle()
                vec.tensor_tensor(flat(merged[:, chunks(b), :]), flat(merged[:, chunks(b), :]), raw[:, b % 2],
                                  ALU.add).then_inc(emptied["y_b"], 1)

            def add_to_x(stage, b):
                dve.wait_ge(filled[stage], b + 1)
                x = flat(xT[:, chunks(b), :])
                vec.tensor_tensor(x, x, bank(stage, b)[:], ALU.add).then_inc(emptied[stage], 1)

            for b in range(4):
                add_to_x("w_out", b)
            dve.wait_ge(emptied["w_out"], 4)
            normalise("ffn")

            dve.wait_ge(filled["route"], 1)
            vec.tensor_copy(flat(logit[:]), bank("route")[:, 0:TT * ROUTES]).then_inc(emptied["route"], 1)
            step(vec.memset(rt[:, :, 8:16], -3.0e38))
            step.settle()
            dve.wait_ge(emptied["route"], 1)
            iota = const[:, C_IOTA:C_IOTA + 8]
            both = range(TT)

            def each(f):
                for t in both:
                    step(f(t))
                step.settle()

            step(vec.tensor_copy(rt[:, :, 8:8 + GROUPS], logit[:, :, 0:GROUPS]))
            step.settle()
            each(lambda t: vec.max(top[:, t, 0], rt[:, t, 8:16]))
            each(lambda t: vec.max_index(topi[:, t, 0], top[:, t, 0], rt[:, t, 8:16]))
            vec.tensor_scalar(rt[:, :, 0:1], top[:, :, 0, 0:1], -1.0, None, ALU.mult).then_inc(lmax_ready, 1)
            step(vec.tensor_copy(rt[:, :, 3:4], topi[:, :, 0, 0:1]))
            step.settle()
            each(lambda t: vec.tensor_scalar(rt[:, t, 24:24 + GROUPS], iota[:, 0:GROUPS], rt[:, t, 3:4], None, ALU.is_equal))
            for g in range(GROUPS):
                le = lambda t: logit[:, t, GROUPS + g * PER_GROUP:GROUPS + (g + 1) * PER_GROUP]
                if g == 0:
                    each(lambda t: vec.tensor_scalar(rt[:, t, 32:40], le(t), rt[:, t, 24:25], None, ALU.mult))
                else:
                    each(lambda t: vec.scalar_tensor_tensor(rt[:, t, 32:40], le(t), rt[:, t, 24 + g:25 + g], rt[:, t, 32:40],
                                                            ALU.mult, ALU.add))
            each(lambda t: vec.max(top[:, t, 1], rt[:, t, 32:40]))
            each(lambda t: vec.max_index(topi[:, t, 1], top[:, t, 1], rt[:, t, 32:40]))
            vec.tensor_tensor(rt[:, :, 20:21], top[:, :, 1, 1:2], top[:, :, 1, 0:1], ALU.subtract).then_inc(pair_ready, 1)
            step(vec.tensor_copy(rt[:, :, 28:30], topi[:, :, 1, 0:2]))
            dve.wait_ge(lexp_ready, TT)
            step(vec.reciprocal(rt[:, :, 2:3], rt[:, :, 1:2]))
            dve.wait_ge(pexp_ready, 1)
            step(vec.tensor_scalar(rt[:, :, 22:23], rt[:, :, 21:22], 1.0, None, ALU.add))
            step.settle()
            step(vec.reciprocal(rt[:, :, 23:24], rt[:, :, 22:23]))
            step.settle()
            step(vec.tensor_tensor(rt[:, :, 30:31], rt[:, :, 23:24], rt[:, :, 2:3], ALU.mult))
            step.settle()
            step(vec.tensor_tensor(rt[:, :, 31:32], rt[:, :, 30:31], rt[:, :, 21:22], ALU.mult))
            step.settle()
            each(lambda t: vec.tensor_scalar(rt[:, t, 40:48], iota, rt[:, t, 28:29], rt[:, t, 30:31], ALU.is_equal, ALU.mult))
            each(lambda t: vec.tensor_scalar(rt[:, t, 48:56], iota, rt[:, t, 29:30], rt[:, t, 31:32], ALU.is_equal, ALU.mult))
            step(vec.tensor_tensor(rt[:, :, 40:48], rt[:, :, 40:48], rt[:, :, 48:56], ALU.add))
            step.settle()
            for g in range(GROUPS):
                for t in both:
                    step(vec.tensor_scalar(gate[:, t, g * PER_GROUP:(g + 1) * PER_GROUP], rt[:, t, 40:48],
                                           rt[:, t, 24 + g:25 + g], None, ALU.mult))
            step(vec.memset(yacc, 0.0))
            step.settle()

            with dve.Fori(0, TURNS) as e:
                for j in range(2):
                    for f in range(FC):
                        dve.wait_ge(silu_ready, e * 8 + (4 * j + f + 1))
                        vec.tensor_tensor(hid[:, j, f, :], exp_bank(f)[:, T:2 * T], silu[:, f], ALU.mult).then_inc(emptied["gate_up"], 1)
                    dve.wait_ge(emptied["down"], e * 8 + (4 * j + 4))
                    for t in range(TT):
                        for half in range(2):
                            n = 2 * t + half
                            dve.wait_ge(filled["down"], e * 8 + (4 * j + n + 1))
                            y = yacc[:, t, half * BANK:(half + 1) * BANK]
                            vec.scalar_tensor_tensor(y, exp_bank(4 + n)[:], gate[:, t, bass.ds(e * 2 + j, 1)], y,
                                                     ALU.mult, ALU.add).then_inc(emptied["down"], 1)
            for b in range(4):
                add_to_x("turn", b)
            dve.wait_ge(emptied["turn"], 4)
            normalise("ple")
            for b in range(4):
                dve.wait_ge(emptied["ple_gate"], b + 1)
                dve.wait_ge(filled["ple"], b + 1)
                step(vec.tensor_tensor(raw[:, b % 2], bank("ple", b)[:], flat(gates_ab[:, 1, chunks(b), :]), ALU.mult))
                step.settle()
                x = flat(xT[:, chunks(b), :])
                vec.tensor_tensor(x, x, raw[:, b % 2], ALU.add).then_inc(emptied["ple"], 1)

    return sems


def second_block(nc, ctx, dram, const, keep, bias_rows, out):
    R = 3

    def sb(name, shape, dt=F32):
        return ctx.enter_context(nc.sbuf_tensor("b_" + name, shape, dt))

    sems = []

    def sem(name):
        sems.append(ctx.enter_context(nc.semaphore("b_" + name)))
        return sems[-1]

    xT, hT, sq, eps, ones, ps = (keep[k] for k in ("xT", "hT", "sq", "eps", "ones", "ps"))
    ident = const[:, C_ID:C_ID + P]
    ring = sb("ring", [P, R, 4096])
    rows = sb("rows", [64, P])
    rrows = sb("rrows", [8 * RC, RP])
    par = sb("par", [P, 64 + 8 * RC])
    w2k = sb("w2k", [P, 2, P])
    w2v = sb("w2v", [P, 2, HD])
    rel = sb("rel", [BUCKETS + 1, H2])
    sp_ = sb("softplus", [P, 8, RC])
    region_x = sb("region_x", [P, 3108])
    region_c = sb("region_c", [P, 3072])
    region_r = sb("region_r", [P, 6144])
    region_g = sb("region_g", [P, 3072])
    tmp = sb("tmp", [P, RB, T])
    gates_ab = sb("gates_ab", [P, 2, DC, T])
    qn = sb("qn", [P, DC, T])
    kn = sb("kn", [P, 2, KVG, T])
    vn = sb("vn", [P, 2, TT, KVW])
    gn = sb("gn", [P, TT, 3 * H2])
    stat = sb("stat", [P, 2, BANK])
    rstd = sb("rstd", [P, BANK])
    soft = sb("soft", [P, 3, 2, 3 * P])
    S, E, PT = soft[:, 0], soft[:, 1], soft[:, 2]
    ksq = soft[:].rearrange("p a b n -> p (a b n)")
    smax = sb("smax", [P, 2, 2])
    ssum = sb("ssum", [P, 2, 2])
    cbias = sb("cbias", [P, TT, H2, NCMP])
    sc = sb("sc", [P, TT, H2, NCMP])
    cm = sb("cm", [P, 2, TT, H2])
    hid_c = sb("hid_c", [P, 2, 2, KVG * NCMP])
    kcd = sb("kcd", [P, KVG * NCMP])
    merged = sq
    three = "p (c n) -> p c n"

    u_pad = region_x[0:RP, 0:RC * (T + RTAPS - 1)].rearrange(three, c=RC)
    tau = region_x[0:RP, 0:RC * T].rearrange(three, c=RC)
    xc = region_c[0:RP, 0:RC * T].rearrange(three, c=RC)
    ra = region_r[0:RP, 0:RC * T].rearrange(three, c=RC)
    ix = region_r[0:RP, RC * T:2 * RC * T].rearrange(three, c=RC)
    gel = region_g[0:RP, :].rearrange(three, c=RC)
    near = region_r[0:BUCKETS + 1, 0:TT * NCMP * P]
    far = region_r[0:BUCKETS + 1, 4096:4096 + 2 * T]
    er = region_r[0:H2, 5120:5120 + 2 * T]
    bias3 = region_r[:, 0:H2 * 3 * P].rearrange("p (h n) -> p h n", h=H2)
    Z = [region_x[:, 512 * n:512 * n + 512].rearrange("p (g n) -> p g n", g=KVG) for n in range(2)]
    NB = KVG * NCMP
    ZB = [region_x[:, 1024 + 960 * n:1024 + 960 * n + 16 * NB].rearrange("p (j g c) -> p j g c", j=16, g=KVG) for n in range(2)]
    pc = region_c[:, 0:1024].rearrange("p (t h c) -> p t h c", t=TT, h=H2)
    pcT = region_c[:, 1024:2048].rearrange("p (g n) -> p g n", g=KVG)
    vcz = region_c[:, 2048:3072].rearrange("p (g r n) -> p g r n", g=KVG, r=HPG)
    attn = region_g[:, 0:DC * T].rearrange(three, c=DC)

    def hidden(c, n=1):
        reg = (region_x, region_c, region_g)[c // 12]
        return reg[:, c % 12 * T:(c % 12 + n) * T]

    def head_squares(name, b):
        if name == "q":
            return sq[:, 2 * b:2 * b + 2, :].rearrange("p c n -> p (c n)")
        if name == "kc":
            return sc[:, 0].rearrange("p h c -> p (h c)")[:, 0:NB]
        n = ("ks", "kw").index(name)
        return ksq[:, (2 * n + b) * BANK:(2 * n + b + 1) * BANK]

    outtok = hT[:].rearrange("p (t c) n -> p t (c n)", t=TT)

    col, at = {}, 0
    for n, k in (("norm_final", DC), ("norm_mix_2", DC), ("norm_mlp_2", DC), ("phi_k_pe_2", 16), ("phi_v_pe_2", 16),
                 ("q_norm_2", 1), ("kc_norm_2", 1), ("ks_norm_2", 1), ("kw_norm_2", 1)):
        col[n] = at
        at += k
    n_rows = at
    rcol, at = {}, 0
    for n, k in (("conv_w_2", RTAPS * RC), ("conv_b_2", RC), ("gate_a_b_2", RC), ("gate_x_b_2", RC), ("lru_lambda_2", RC)):
        rcol[n] = at
        at += k
    assert n_rows <= 64 and at == 8 * RC

    def param(name, c=0):
        return par[:, col[name] + c:col[name] + c + 1]

    def rparam(name, c, n=1):
        return par[0:RP, 64 + rcol[name] + c:64 + rcol[name] + c + n]

    stages = dict(params=1, far=1, near=TT, mean_final=1, mean_mix=1, u_rnn=RC // 2, u_gate=RC // 2, lru_r=RC // 2,
                  lru_i=RC // 2, ga=4, gb=4, gn=1, q=4, ks=2, vs=1, mean_q=4, kw=2, vw=1, mean_ks=2, kc=1, vc=1,
                  mean_kw=2, y_a=4, hid_k=1, hid_v=1, kc2=1, vc2=1, mean_kc=1, scorec=2 * TT, pcT=2,
                  score=2 * H2, probT=2 * H2, o=H2 // 2, y_b=4, w_out=4, mean_mlp=1, mlp_in=16, mlp_out=4)
    banks, n = {}, 0
    for stage, count in stages.items():
        for i in range(count):
            if stage in ("score", "probT", "o"):
                banks[stage, i] = {"score": i % 3, "probT": 3 + i % 3, "o": 6 + i % 2}[stage]
            else:
                banks[stage, i] = n % BANKS
                n += 1

    def bank(stage, i=0):
        return ps[banks[stage, i]]

    filled = {s: sem("filled_" + s) for s in stages}
    emptied = {s: sem("emptied_" + s) for s in stages}
    landed = [sem(f"landed{i}") for i in range(R)]
    params_in, phi_in, er_out, bias_in, stored = (sem(n) for n in ("params_in", "phi_in", "er_out", "bias_in", "stored"))
    dve_steps, act_steps = sem("dve_steps"), sem("act_steps")
    squares = {n: sem("squares_" + n) for n in ("final", "mix", "mlp", "q", "ks", "kw", "kc")}
    normed = {n: sem("normed_" + n) for n in ("final", "mix", "mlp", "q", "ks", "kw", "kc")}
    (conv_ready, lam_exp, rates, taus, decays, ratios, mults, y_ready, zb_ready, cshift, root_read,
     cexp, pc_ready, smax_ready, exps_ready, probs_ready, squared) = (sem(n) for n in (
         "conv_ready", "lam_exp", "rates", "taus", "decays", "ratios", "mults", "y_ready", "zb_ready", "cshift", "root_read",
         "cexp", "pc_ready", "smax_ready", "exps_ready", "probs_ready", "squared"))

    def w_cols(name, c0, n=BANK, part=P):
        return dram[name][0, :, c0:c0 + n].rearrange("(c p) n -> p c n", p=part)

    stream = []
    for i in range(3):
        stream.append((w_cols("w_in_2", IN2["u_rnn"] + 4 * RP * i, 4 * RP), "u_rnn", 2 * i + 2))
    for i in range(3):
        stream.append((w_cols("w_in_2", IN2["u_gate"] + 4 * RP * i, 4 * RP), "u_gate", 2 * i + 2))
    for name, stage in (("gate_a_w_2", "lru_r"), ("gate_x_w_2", "lru_i")):
        stream.append((dram[name][0].rearrange("n (c p) m -> p (n c) m", p=RP), stage, RC // 2))
    for name in ("a", "b"):
        for i in range(2):
            stream.append((w_cols("w_in_2", IN2["g_" + name] + BANK * i), "g" + name, 2 * i + 2))
    stream.append((w_cols("w_in_2", IN2["g_nsa"], 3 * H2), "gn", 1))
    for i in range(2):
        stream.append((w_cols("w_in_2", IN2["q"] + BANK * i), "q", 2 * i + 2))
    for name in ("s", "w", "c"):
        stream.append((w_cols("w_in_2", IN2["k" + name]), "v" + name, 1))
    for i in range(4):
        stream.append((w_cols("proj_a_2", 2 * P * i, 2 * P, RP), "y_a", i + 1))
    for name, stage in (("phi_k_w1_2", "hid_k"), ("phi_v_w1_2", "hid_v")):
        stream.append((dram[name][0].rearrange("(c p) n -> p c n", p=P), stage, 1))
    for name, stage in (("proj_b_2", "y_b"), ("w_out_2", "w_out")):
        for i in range(2):
            stream.append((w_cols(name, BANK * i), stage, 2 * i + 2))
    for i in range(8):
        stream.append((w_cols("w_mlp_in_2", BANK * i), "mlp_in", 2 * i + 2))
    for i in range(8):
        stream.append((dram["w_mlp_out_2"][0, BANK * i:BANK * (i + 1)].rearrange("(c p) n -> p c n", p=P), "mlp_out", 4))
    S_OF, at = {}, 0
    for i, (_, stage, _) in enumerate(stream):
        S_OF.setdefault(stage, i)
    mlp_slots = sem("mlp_slots")

    def slot(i):
        p, c, n = stream[i][0].shape
        return ring[0:p, i % R, 0:c * n].rearrange(three, c=c)

    with nc.Block(no_gpsimd_drain=True) as block:

        @block.sync
        def _(sp):
            def small(dst, src):
                sp.dma_start(dst, src).then_inc(params_in, 16)

            small(rows[0:DC, :], dram["norm_final"].rearrange("(c p) -> c p", p=P))
            for n in ("norm_mix_2", "norm_mlp_2"):
                small(rows[col[n]:col[n] + DC, :], dram[n][0].rearrange("(c p) -> c p", p=P))
            for n in ("phi_k_pe_2", "phi_v_pe_2"):
                small(rows[col[n]:col[n] + 16, :], dram[n][0].rearrange("(j k) d -> j (k d)", k=2))
            for n in ("q_norm_2", "kc_norm_2", "ks_norm_2", "kw_norm_2"):
                for h in range(2):
                    small(rows[col[n]:col[n] + 1, HD * h:HD * h + HD], dram[n])
            small(rrows[0:RTAPS * RC, :], dram["conv_w_2"][0].rearrange("k (c p) -> (k c) p", p=RP))
            for n in ("conv_b_2", "lru_lambda_2"):
                small(rrows[rcol[n]:rcol[n] + RC, :], dram[n][0].rearrange("(c p) -> c p", p=RP))
            for n in ("gate_a_b_2", "gate_x_b_2"):
                small(rrows[rcol[n]:rcol[n] + RC, :], dram[n][0].rearrange("n (c p) -> (n c) p", p=RP))
            small(rel[0:BUCKETS, :], dram["rel_bias_2"])
            small(rel[BUCKETS:BUCKETS + 1, :], dram["off"])
            small(far, dram["far"])
            small(near, dram["near"])
            N_PARAMS = 3 + 2 + 8 + 1 + 2 + 2 + 4
            for h in range(2):
                sp.dma_start(w2k[:, :, HD * h:HD * h + HD], dram["phi_k_w2_2"][0].rearrange("(c p) n -> p c n", p=P)).then_inc(phi_in, 16)
            sp.dma_start(w2v[:], dram["phi_v_w2_2"][0].rearrange("(c p) n -> p c n", p=P)).then_inc(phi_in, 16)
            assert N_PARAMS == 22
            for i, (src, stage, n) in enumerate(stream):
                if i == R:
                    sp.wait_ge(emptied["far"], 1)
                    sp.dma_start(bias_rows[:, :, 0:2 * T], er.unsqueeze(1).broadcast_to([H2, P, 2 * T])).then_inc(er_out, 16)
                if i >= R:
                    _, before, m = stream[i - R]
                    if before == "mlp_out":
                        sp.wait_ge(mlp_slots, i - R - S_OF["mlp_out"] + 1)
                    else:
                        sp.wait_ge(filled[before], m)
                sp.dma_start(slot(i), src).then_inc(landed[i % R], 16)
                if i == S_OF["y_a"] + 2:
                    sp.wait_ge(er_out, 16)
                    sp.wait_ge(y_ready, RBLOCKS)
                    for c0, d0, k in ((0, 0, P), (P, P, 2 * P)):
                        src = bass.AP(bias_rows.tensor, T - 1 - d0, [[2 * T, P], [P * SKEW, H2], [1, k]])
                        sp.dma_start(bias3[:, :, c0:c0 + k], src).then_inc(bias_in, 16)
            for b in range(4):
                sp.wait_ge(emptied["mlp_out"], b + 1)
                t, half = b // 2, b % 2
                sp.dma_start(out[0, t * P:(t + 1) * P, half * BANK:(half + 1) * BANK],
                             outtok[:, t, half * BANK:(half + 1) * BANK]).then_inc(stored, 16)
            sp.wait_ge(stored, 64)

        @block.tensor
        def _(pe):
            last_in = {}

            def claim(stage, i):
                b = banks[stage, i]
                if b in last_in:
                    s, n = last_in[b]
                    pe.wait_ge(emptied[s], n + 1)
                last_in[b] = (stage, i)
                return ps[b]

            def weights(i):
                pe.wait_ge(landed[i % R], 16 * (i // R + 1))
                return slot(i)

            def mean(stage, ready):
                out = claim(stage, 0)
                for c in range(DC):
                    if c % 4 == 0:
                        pe.wait_ge(ready, c // 4 + 1)
                    mm = nc.tensor.matmul(out[:, 0:T], ones["D"][:], sq[:, c, :], start=(c == 0), stop=(c == DC - 1))
                mm.then_inc(filled[stage], 1)

            def head_means(name, b):
                out = claim("mean_" + name, b)
                pe.wait_ge(squares[name], b + 1)
                x = head_squares(name, b)
                nc.tensor.matmul(out[:, 0:x.shape[1]], const[:, C_HEAD:C_HEAD + P], x, start=True, stop=True).then_inc(filled["mean_" + name], 1)

            def project(i, stage, n0, src, cols=4, width=P):
                w = weights(i)
                kc = w.shape[1]
                for b in range(cols // 2):
                    out = claim(stage, n0 + b)
                    for m in range(2):
                        for k in range(kc):
                            c = 2 * b + m
                            mm = nc.tensor.matmul(out[0:width, m * T:(m + 1) * T], w[:, k, c * width:(c + 1) * width],
                                                  src(k), start=(k == 0), stop=(k == kc - 1))
                    mm.then_inc(filled[stage], 1)

            h = lambda k: hT[:, k, :]
            pe.wait_ge(params_in, 16 * 22)
            out = claim("params", 0)
            nc.tensor.transpose(out[:, 0:n_rows], rows[0:n_rows, :], ident[0:n_rows, 0:n_rows])
            nc.tensor.transpose(out[0:RP, 64:64 + 8 * RC], rrows[:], ident[0:8 * RC, 0:8 * RC]).then_inc(filled["params"], 1)
            nc.tensor.matmul(claim("far", 0)[0:H2, :], rel[:], far, start=True, stop=True).then_inc(filled["far"], 1)
            for t in range(TT):
                out = claim("near", t)
                for c in range(NCMP):
                    i = t * NCMP + c
                    mm = nc.tensor.matmul(out[:, c * H2:(c + 1) * H2], near[:, i * P:(i + 1) * P], rel[:], start=True, stop=True)
                mm.then_inc(filled["near"], 1)
            mean("mean_final", squares["final"])
            mean("mean_mix", squares["mix"])
            pe.wait_ge(normed["mix"], DC)
            for n, stage in enumerate(("u_rnn", "u_gate")):
                for i in range(3):
                    project(3 * n + i, stage, 2 * i, h, width=RP)
            pe.wait_ge(conv_ready, RC)
            for n, stage in enumerate(("lru_r", "lru_i")):
                w = weights(S_OF[stage])
                for b in range(RC // 2):
                    out = claim(stage, b)
                    for m in range(2):
                        c = 2 * b + m
                        for k in range(RB):
                            i = c // RB * RB + k
                            mm = nc.tensor.matmul(out[0:RP, m * T:(m + 1) * T], w[:, i, c % RB * RP:(c % RB + 1) * RP],
                                                  xc[:, i, :], start=(k == 0), stop=(k == RB - 1))
                    mm.then_inc(filled[stage], 1)
            for stage in ("ga", "gb"):
                for i in range(2):
                    project(S_OF[stage] + i, stage, 2 * i, h)
            w = weights(S_OF["gn"])
            out = claim("gn", 0)
            for t in range(TT):
                for k in range(DC):
                    mm = nc.tensor.matmul(out[:, t * 3 * H2:(t + 1) * 3 * H2], hT[:, k, t * P:(t + 1) * P], w[:, k, :],
                                          start=(k == 0), stop=(k == DC - 1))
            mm.then_inc(filled["gn"], 1)
            for i in range(2):
                project(S_OF["q"] + i, "q", 2 * i, h)

            def keys_values(name):
                w = weights(S_OF["v" + name])
                for b in range(2):
                    out = claim("k" + name, b)
                    for m in range(2):
                        g = 2 * b + m
                        for half in range(2):
                            for k in range(DC):
                                mm = nc.tensor.matmul(out[HD * half:HD * half + HD, m * T:(m + 1) * T], w[:, k, g * HD:(g + 1) * HD],
                                                      h(k), start=(k == 0), stop=(k == DC - 1))
                    mm.then_inc(filled["k" + name], 1)
                out = claim("v" + name, 0)
                for t in range(TT):
                    for k in range(DC):
                        mm = nc.tensor.matmul(out[:, t * KVW:(t + 1) * KVW], hT[:, k, t * P:(t + 1) * P], w[:, k, KVW:2 * KVW],
                                              start=(k == 0), stop=(k == DC - 1))
                mm.then_inc(filled["v" + name], 1)

            keys_values("s")
            for b in range(4):
                head_means("q", b)
            keys_values("w")
            for b in range(2):
                head_means("ks", b)
            w = weights(S_OF["vc"])
            for n, stage in enumerate(("kc", "vc")):
                out = claim(stage, 0)
                for m in range(2):
                    for k in range(DC):
                        c = 2 * n + m
                        mm = nc.tensor.matmul(out[:, m * T:(m + 1) * T], w[:, k, c * P:(c + 1) * P], h(k),
                                              start=(k == 0), stop=(k == DC - 1))
                mm.then_inc(filled[stage], 1)
            for b in range(2):
                head_means("kw", b)
            pe.wait_ge(y_ready, RBLOCKS)
            for i in range(4):
                project(S_OF["y_a"] + i, "y_a", i, lambda k: gel[:, k, :], cols=2)
            pe.wait_ge(phi_in, 48)
            for n, stage in enumerate(("hid_k", "hid_v")):
                w = weights(S_OF[stage])
                pe.wait_ge(zb_ready, KVG * (n + 1))
                out = claim(stage, 0)
                for f in range(2):
                    for j in range(16):
                        mm = nc.tensor.matmul(out[:, f * NB:(f + 1) * NB], w[:, j, f * P:(f + 1) * P],
                                              ZB[n][:, j].rearrange("p g c -> p (g c)"), start=(j == 0), stop=(j == 15))
                mm.then_inc(filled[stage], 1)
            pe.wait_ge(emptied["hid_k"], 1)
            out = claim("kc2", 0)
            for f in range(2):
                mm = nc.tensor.matmul(out[:, 0:NB], w2k[:, f, :], hid_c[:, 0, f, :], start=(f == 0), stop=(f == 1))
            mm.then_inc(filled["kc2"], 1)
            pe.wait_ge(emptied["hid_v"], 1)
            out = claim("vc2", 0)
            for r in range(HPG):
                for g in range(KVG):
                    for f in range(2):
                        mm = nc.tensor.matmul(out[32 * r:32 * r + NCMP, g * HD:(g + 1) * HD], hid_c[:, 1, f, g * NCMP:(g + 1) * NCMP],
                                              w2v[:, f, :], start=(f == 0), stop=(f == 1))
            mm.then_inc(filled["vc2"], 1)
            head_means("kc", 0)
            pe.wait_ge(normed["q"], 4)
            pe.wait_ge(normed["kc"], 1)
            for t in range(TT):
                for odd in range(2):
                    out = claim("scorec", 2 * t + odd)
                    r = slice(HD * odd, HD * odd + HD)
                    for n in range(H2 // 2):
                        g = 2 * n // HPG
                        mm = nc.tensor.matmul(out[:, n * NCMP:(n + 1) * NCMP], qn[r, n, t * P:(t + 1) * P],
                                              kcd[r, g * NCMP:(g + 1) * NCMP], start=True, stop=True)
                    mm.then_inc(filled["scorec"], 1)
            pe.wait_ge(pc_ready, TT)
            for b in range(2):
                out = claim("pcT", b)
                for m in range(2):
                    for t in range(TT):
                        g = 2 * b + m
                        mm = nc.tensor.transpose(out[:, m * T + t * P:m * T + (t + 1) * P],
                                                 pc[:, t, g * HPG:(g + 1) * HPG, :].rearrange("p h c -> p (h c)"), ident)
                mm.then_inc(filled["pcT"], 1)
            pe.wait_ge(normed["ks"], 2)
            pe.wait_ge(normed["kw"], 2)
            pe.wait_ge(emptied["vs"], 1)
            pe.wait_ge(emptied["vw"], 1)
            pe.wait_ge(emptied["pcT"], 2)
            pe.wait_ge(emptied["vc2"], 1)

            def score(i):
                hd, n = i // 2, i % 2
                out = claim("score", i)
                r = slice(HD * (hd % 2), HD * (hd % 2) + HD)
                q, k = qn[r, hd // 2, :], kn[r, n, hd // HPG, :]
                nc.tensor.matmul(out[:, 0:P], q[:, 0:P], k[:, 0:P], start=True, stop=True)
                nc.tensor.matmul(out[:, P:3 * P], q[:, P:T], k, start=True, stop=True).then_inc(filled["score"], 1)

            def prob_t(i):
                out = claim("probT", i)
                pe.wait_ge(probs_ready, i + 1)
                e = E[:, i % 2]
                nc.tensor.transpose(out[:, 0:P], e[:, 0:P], ident)
                nc.tensor.transpose(out[:, P:T], e[:, P:T], ident)
                nc.tensor.transpose(out[:, T:3 * P], e[:, T:3 * P], ident).then_inc(filled["probT"], 1)

            def values(i):
                hd, n = i // 2, i % 2
                g = hd // HPG
                if i % 4 == 0:
                    claim("o", i // 4)
                out = bank("o", hd // 2)[HD * (hd % 2):HD * (hd % 2) + HD, 0:T]
                if n == 0:
                    nc.tensor.matmul(out, vcz[:, g, hd % HPG, :], pcT[:, g, :], start=True, stop=False)
                pe.wait_ge(emptied["probT"], i + 1)
                pt = PT[:, i % 2]
                nc.tensor.matmul(out, vn[:, n, 0, g * HD:(g + 1) * HD], pt[:, 0:T], start=False, stop=False)
                nc.tensor.matmul(out[:, P:T], vn[:, n, 1, g * HD:(g + 1) * HD], pt[:, T:3 * P], start=False, stop=(n == 1))\
                    .then_inc(filled["o"], 1)

            N = 2 * H2
            for i in range(N + 3):
                if i < N:
                    score(i)
                if 2 <= i < N + 2:
                    prob_t(i - 2)
                if i >= 3:
                    values(i - 3)
            pe.wait_ge(emptied["o"], H2 // 2)
            for i in range(2):
                project(S_OF["y_b"] + i, "y_b", 2 * i, lambda k: attn[:, k, :])
            pe.wait_ge(emptied["y_b"], 4)
            for i in range(2):
                project(S_OF["w_out"] + i, "w_out", 2 * i, lambda k: merged[:, k, :])
            mean("mean_mlp", squares["mlp"])
            pe.wait_ge(normed["mlp"], DC)
            for i in range(8):
                project(S_OF["mlp_in"] + i, "mlp_in", 2 * i, h)
            outs = [claim("mlp_out", b) for b in range(4)]
            for s in range(8):
                w = weights(S_OF["mlp_out"] + s)
                pe.wait_ge(squared, 2 * s + 2)
                for k in range(4):
                    for b in range(4):
                        t, half = b // 2, b % 2
                        mm = nc.tensor.matmul(outs[b][:], hidden(4 * s + k)[:, t * P:(t + 1) * P], w[:, k, half * BANK:(half + 1) * BANK],
                                              start=(s == 0 and k == 0), stop=False)
                mm.then_inc(mlp_slots, 1)
            for b in range(4):
                t, half = b // 2, b % 2
                for c in range(4):
                    mm = nc.tensor.matmul(outs[b][:, c * P:(c + 1) * P], xT[:, 4 * half + c, t * P:(t + 1) * P], ident,
                                          start=False, stop=(c == 3))
                mm.then_inc(filled["mlp_out"], 1)

        @block.scalar
        def _(act):
            step = Chain(act, act_steps)
            sc_act = nc.scalar.activation

            def norm(name):
                for h in range(2):
                    sc_act(sq[:, 4 * h:4 * h + 4, :], xT[:, 4 * h:4 * h + 4, :], ACT.Square).then_inc(squares[name], 1)
                act.wait_ge(filled["mean_" + name], 1)
                sc_act(stat[:, 0, 0:T], bank("mean_" + name)[:, 0:T], ACT.Sqrt, bias=eps[:, 0:1]).then_inc(emptied["mean_" + name], 1)

            act.wait_ge(filled["far"], 1)
            nc.scalar.copy(er, bank("far")[0:H2, :]).then_inc(emptied["far"], 1)
            norm("final")
            act.wait_ge(normed["final"], DC)
            norm("mix")
            act.wait_ge(emptied["params"], 1)
            step(sc_act(sp_[0:RP, 0], rparam("lru_lambda_2", 0, RC), ACT.Abs))
            step.settle()
            sc_act(sp_[0:RP, 1], sp_[0:RP, 0], ACT.Exp, scale=-1.0).then_inc(lam_exp, 1)
            for b in range(RC // 2):
                act.wait_ge(filled["u_rnn"], b + 1)
                nc.scalar.copy(u_pad[:, 2 * b:2 * b + 2, RTAPS - 1:], bank("u_rnn", b)[0:RP].rearrange(three, c=2)).then_inc(emptied["u_rnn"], 1)
            for b in range(RC // 2):
                act.wait_ge(filled["u_gate"], b + 1)
                sc_act(gel[:, 2 * b:2 * b + 2, :].rearrange("p c n -> p (c n)"), bank("u_gate", b)[0:RP], ACT.Gelu_apprx_tanh).then_inc(emptied["u_gate"], 1)
            act.wait_ge(er_out, 16)
            for stage, dst, name in (("lru_r", ra, "gate_a_b_2"), ("lru_i", ix, "gate_x_b_2")):
                for b in range(RC // 2):
                    act.wait_ge(filled[stage], b + 1)
                    step(sc_act(dst[:, 2 * b, :], bank(stage, b)[0:RP, 0:T], ACT.Sigmoid, bias=rparam(name, 2 * b)))
                    sc_act(dst[:, 2 * b + 1, :], bank(stage, b)[0:RP, T:2 * T], ACT.Sigmoid, bias=rparam(name, 2 * b + 1)).then_inc(emptied[stage], 1)
            act.wait_ge(rates, 1)
            act.wait_ge(emptied["lru_r"], RC // 2)
            for c in range(RC):
                sc_act(tau[:, c, :], ra[:, c, :], ACT.Tanh, scale=sp_[0:RP, 6, c:c + 1]).then_inc(taus, 1)
            for c in range(RC):
                sc_act(ra[:, c, :], ra[:, c, :], ACT.Exp, scale=sp_[0:RP, 7, c:c + 1]).then_inc(decays, 1)
            for n, stage in enumerate(("ga", "gb")):
                for b in range(4):
                    act.wait_ge(filled[stage], b + 1)
                    sc_act(gates_ab[:, n, 2 * b:2 * b + 2, :].rearrange("p c n -> p (c n)"), bank(stage, b)[:], ACT.Sigmoid).then_inc(emptied[stage], 1)
            act.wait_ge(filled["gn"], 1)
            sc_act(gn[:].rearrange("p t n -> p (t n)"), bank("gn")[:, 0:TT * 3 * H2], ACT.Sigmoid).then_inc(emptied["gn"], 1)
            act.wait_ge(ratios, RBLOCKS)
            sc_act(tau.rearrange("p c n -> p (c n)"), tau.rearrange("p c n -> p (c n)"), ACT.Sqrt, scale=2.0).then_inc(mults, 1)

            flat = lambda x: x.rearrange("p c n -> p (c n)")
            n_roots = [0]

            def heads(name, dst, b):
                act.wait_ge(filled[name], b + 1)
                src = bank(name, b)[:, 0:dst.shape[1]]
                sc_act(head_squares(name[:2] if name != "kc2" else "kc", b), src, ACT.Square).then_inc(squares[name if name != "kc2" else "kc"], 1)
                nc.scalar.copy(dst, src).then_inc(emptied[name], 1)

            def roots(name, b, n=BANK):
                act.wait_ge(filled["mean_" + name], b + 1)
                i = n_roots[0]
                if i >= 2:
                    act.wait_ge(root_read, i - 1)
                n_roots[0] += 1
                sc_act(stat[:, i % 2, 0:n], bank("mean_" + name, b)[:, 0:n], ACT.Sqrt, bias=eps[:, 0:1]).then_inc(emptied["mean_" + name], 1)

            for b in range(4):
                heads("q", flat(qn[:, 2 * b:2 * b + 2, :]), b)
            for b in range(2):
                heads("ks", flat(kn[:, 0, 2 * b:2 * b + 2, :]), b)
            act.wait_ge(filled["vs"], 1)
            nc.scalar.copy(flat(vn[:, 0]), bank("vs")[:]).then_inc(emptied["vs"], 1)
            for b in range(4):
                roots("q", b)
            for b in range(2):
                heads("kw", flat(kn[:, 1, 2 * b:2 * b + 2, :]), b)
            act.wait_ge(filled["vw"], 1)
            nc.scalar.copy(flat(vn[:, 1]), bank("vw")[:]).then_inc(emptied["vw"], 1)
            for b in range(2):
                roots("ks", b)
            act.wait_ge(y_ready, RBLOCKS)
            for n, stage in enumerate(("kc", "vc")):
                act.wait_ge(filled[stage], 1)
                for jj in range(2):
                    for a in range(2):
                        src = bank(stage)[HD * a:HD * a + HD, :].rearrange("p (m t j) -> p m t j", m=2, j=2)[:, :, :, jj]
                        i = nc.scalar.copy(Z[n][HD * jj:HD * jj + HD, a::2, :], src)
                        if (jj, a) == (1, 1):
                            i.then_inc(emptied[stage], 1)
                        else:
                            step(i)
            for b in range(2):
                roots("kw", b)
            for n, stage in enumerate(("hid_k", "hid_v")):
                act.wait_ge(filled[stage], 1)
                sc_act(flat(hid_c[:, n]), bank(stage)[:, 0:2 * NB], ACT.Gelu_apprx_tanh).then_inc(emptied[stage], 1)
            heads("kc2", kcd[:], 0)
            roots("kc", 0, NB)
            act.wait_ge(cshift, TT)
            c_flat = sc[:].rearrange("p t h c -> p (t h c)")
            sc_act(c_flat, c_flat, ACT.Exp).then_inc(cexp, 1)
            for b in range(2):
                act.wait_ge(filled["pcT"], b + 1)
                nc.scalar.copy(flat(pcT[:, 2 * b:2 * b + 2, :]), bank("pcT", b)[:]).then_inc(emptied["pcT"], 1)
            N = 2 * H2
            for i in range(N + 1):
                if i < N:
                    act.wait_ge(smax_ready, i + 1)
                    if i >= 2:
                        act.wait_ge(filled["probT"], i - 1)
                    e, s = E[:, i % 2], S[:, i % 2]
                    sc_act(e[:, 0:P], s[:, 0:P], ACT.Exp, bias=smax[:, i % 2, 0:1], accum_out=ssum[:, i % 2, 0:1]).then_inc(exps_ready, 1)
                    sc_act(e[:, P:], s[:, P:], ACT.Exp, bias=smax[:, i % 2, 1:2], accum_out=ssum[:, i % 2, 1:2]).then_inc(exps_ready, 1)
                if i >= 1:
                    g = i - 1
                    act.wait_ge(filled["probT"], g + 1)
                    if g >= 2:
                        act.wait_ge(filled["o"], g - 1)
                    nc.scalar.copy(PT[:, g % 2], bank("probT", g)[:, 0:3 * P]).then_inc(emptied["probT"], 1)
                    if g % 4 == 1 and g >= 5:
                        c = g // 4 - 1
                        act.wait_ge(filled["o"], 4 * c + 4)
                        nc.scalar.copy(attn[:, c, :], bank("o", c)[:, 0:T]).then_inc(emptied["o"], 1)
            act.wait_ge(filled["o"], N)
            nc.scalar.copy(attn[:, DC - 1, :], bank("o", DC - 1)[:, 0:T]).then_inc(emptied["o"], 1)
            act.wait_ge(emptied["w_out"], 4)
            norm("mlp")
            for b in range(16):
                act.wait_ge(filled["mlp_in"], b + 1)
                if b >= 2:
                    act.wait_ge(squared, b - 1)
                sc_act(stat[:, b % 2], bank("mlp_in", b)[:], ACT.Relu).then_inc(emptied["mlp_in"], 1)
            for b in range(4):
                act.wait_ge(filled["mlp_out"], b + 1)
                nc.scalar.copy(outtok[:, b // 2, b % 2 * BANK:(b % 2 + 1) * BANK], bank("mlp_out", b)[:]).then_inc(emptied["mlp_out"], 1)

        @block.vector
        def _(dve):
            step = Chain(dve, dve_steps)
            vec = nc.vector
            flat = lambda x: x.rearrange("p c n -> p (c n)")

            def normalise(name, pname, dst):
                dve.wait_ge(emptied["mean_" + name], 1)
                step(vec.reciprocal(rstd[:, 0:T], stat[:, 0, 0:T]))
                step.settle()
                for c in range(DC):
                    vec.scalar_tensor_tensor(dst[:, c, :], xT[:, c, :], param(pname, c), rstd[:, 0:T],
                                             ALU.mult, ALU.mult).then_inc(normed[name], 1)

            step(vec.memset(u_pad[:, :, 0:RTAPS - 1], 0.0))
            dve.wait_ge(filled["params"], 1)
            vec.tensor_copy(par[:, 0:n_rows], bank("params")[:, 0:n_rows])
            vec.tensor_copy(par[0:RP, 64:], bank("params")[0:RP, 64:64 + 8 * RC]).then_inc(emptied["params"], 1)
            for t in range(TT):
                dve.wait_ge(filled["near"], t + 1)
                vec.tensor_copy(cbias[:, t], bank("near", t)[:, 0:NCMP * H2].rearrange("p (c h) -> p h c", c=NCMP)).then_inc(emptied["near"], 1)
            dve.wait_ge(emptied["params"], 1)
            normalise("final", "norm_final", xT)
            dve.wait_ge(normed["final"], DC)
            normalise("mix", "norm_mix_2", hT)

            t8 = [sp_[0:RP, i] for i in range(8)]

            def run(ins):
                step(ins)
                step.settle()

            dve.wait_ge(lam_exp, 1)
            run(vec.tensor_scalar(t8[2], t8[1], 2.0, None, ALU.add))
            run(vec.reciprocal(t8[2], t8[2]))
            run(vec.tensor_tensor(t8[2], t8[2], t8[1], ALU.mult))
            run(vec.tensor_tensor(t8[3], t8[2], t8[2], ALU.mult))
            run(vec.tensor_scalar(t8[4], t8[3], 1.0 / 19, None, ALU.mult))
            for k in range(17, 1, -2):
                run(vec.scalar_tensor_tensor(t8[4], t8[4], 1.0 / k, t8[3], ALU.add, ALU.mult))
            run(vec.scalar_tensor_tensor(t8[4], t8[4], 1.0, t8[2], ALU.add, ALU.mult))
            run(vec.tensor_scalar(t8[5], rparam("lru_lambda_2", 0, RC), -1.0, 0.0, ALU.mult, ALU.max))
            run(vec.scalar_tensor_tensor(t8[5], t8[4], 2.0, t8[5], ALU.mult, ALU.add))
            run(vec.tensor_scalar(t8[6], t8[5], 8.0, None, ALU.mult))
            vec.tensor_scalar(t8[7], t8[5], -8.0, None, ALU.mult).then_inc(rates, 1)

            for b in range(RC // 2):
                dve.wait_ge(emptied["u_rnn"], b + 1)
                for k in range(RTAPS):
                    for c in (2 * b, 2 * b + 1):
                        x, w = u_pad[:, c, k:k + T], rparam("conv_w_2", k * RC + c)
                        if k == 0:
                            i = vec.tensor_scalar(xc[:, c, :], x, w, rparam("conv_b_2", c), ALU.mult, ALU.add)
                        else:
                            i = vec.scalar_tensor_tensor(xc[:, c, :], x, w, xc[:, c, :], ALU.mult, ALU.add)
                        if k == RTAPS - 1:
                            i.then_inc(conv_ready, 1)
                        else:
                            step(i)
                    if k < RTAPS - 1:
                        step.settle()
            dve.wait_ge(conv_ready, RC)
            dve.wait_ge(emptied["lru_i"], RC // 2)
            step(vec.tensor_tensor(flat(ix), flat(ix), flat(xc), ALU.mult))
            for n in range(RBLOCKS):
                cs = slice(RB * n, RB * n + RB)
                dve.wait_ge(taus, RB * (n + 1))
                if n:
                    dve.wait_ge(ratios, n)
                run(vec.tensor_scalar(flat(tmp[0:RP]), flat(tau[:, cs, :]), 1.0, None, ALU.add))
                run(vec.reciprocal(flat(tmp[0:RP]), flat(tmp[0:RP])))
                vec.tensor_tensor(flat(tau[:, cs, :]), flat(tau[:, cs, :]), flat(tmp[0:RP]), ALU.mult).then_inc(ratios, 1)
            dve.wait_ge(mults, 1)
            run(vec.memset(tau[:, :, 0:1], 1.0))
            run(vec.tensor_tensor(flat(ix), flat(ix), flat(tau), ALU.mult))
            dve.wait_ge(decays, RC)
            dve.wait_ge(emptied["u_gate"], RC // 2)
            for c in range(RC):
                step(vec.tensor_tensor_scan(xc[:, c, :], ra[:, c, :], ix[:, c, :], 0.0, ALU.mult, ALU.add))
            step.settle()
            for n in range(RBLOCKS):
                cs = slice(RB * n, RB * n + RB)
                vec.tensor_tensor(flat(gel[:, cs, :]), flat(gel[:, cs, :]), flat(xc[:, cs, :]), ALU.mult).then_inc(y_ready, 1)

            n_roots = [0]

            def head_norm(name, b, dst):
                dve.wait_ge(emptied["mean_" + name], b + 1)
                i = n_roots[0]
                if i:
                    dve.wait_ge(last_norm[0], last_norm[1])
                n_roots[0] += 1
                k = dst.shape[1]
                vec.reciprocal(rstd[:, 0:k], stat[:, i % 2, 0:k]).then_inc(root_read, 1)
                dve.wait_ge(root_read, i + 1)
                vec.scalar_tensor_tensor(dst, dst, param(name.removesuffix("_") + "_norm_2"), rstd[:, 0:k],
                                         ALU.mult, ALU.mult).then_inc(normed[name], 1)
                last_norm[:] = [normed[name], b + 1]

            last_norm = [None, 0]
            for b in range(4):
                head_norm("q", b, flat(qn[:, 2 * b:2 * b + 2, :]))
            for b in range(2):
                head_norm("ks", b, flat(kn[:, 0, 2 * b:2 * b + 2, :]))
            for n, stage in enumerate(("kc", "vc")):
                dve.wait_ge(emptied[stage], 1)
                for g in range(KVG):
                    z = Z[n][:, g, :]
                    z = bass.AP(z.tensor, z.offset, [z.ap[0], [1, 16], [STRIDE // 2, NCMP]])
                    pe_ = par[:, col["phi_" + stage[0] + "_pe_2"]:][:, 0:16].unsqueeze(2).broadcast_to([P, 16, NCMP])
                    vec.tensor_tensor(ZB[n][:, :, g, :], z, pe_, ALU.add).then_inc(zb_ready, 1)
            for b in range(2):
                head_norm("kw", b, flat(kn[:, 1, 2 * b:2 * b + 2, :]))
            dve.wait_ge(emptied["ga"], 4)
            dve.wait_ge(emptied["gb"], 4)
            for b in range(4):
                dve.wait_ge(filled["y_a"], b + 1)
                vec.tensor_tensor(flat(merged[:, 2 * b:2 * b + 2, :]), bank("y_a", b)[:], flat(gates_ab[:, 0, 2 * b:2 * b + 2, :]),
                                  ALU.mult).then_inc(emptied["y_a"], 1)
            dve.wait_ge(y_ready, RBLOCKS)
            step(vec.memset(vcz, 0.0))
            step(vec.memset(pc, 0.0))
            step.settle()
            dve.wait_ge(filled["vc2"], 1)
            for r in range(HPG):
                q = slice(32 * r, 32 * r + NCMP)
                i = vec.tensor_copy(vcz[q, :, r, :], bank("vc2")[q, 0:KVG * HD].rearrange("p (g n) -> p g n", g=KVG))
                if r < HPG - 1:
                    step(i)
                else:
                    i.then_inc(emptied["vc2"], 1)
            dve.wait_ge(emptied["kc2"], 1)
            head_norm("kc", 0, kcd[:])

            over_c = lambda x: x.unsqueeze(2).broadcast_to([P, H2, NCMP])
            dve.wait_ge(emptied["near"], TT)
            dve.wait_ge(emptied["mean_kc"], 1)
            for t in range(TT):
                for odd in range(2):
                    dve.wait_ge(filled["scorec"], 2 * t + odd + 1)
                    vec.scalar_tensor_tensor(sc[:, t, odd::2, :], bank("scorec", 2 * t + odd)[:, 0:H2 // 2 * NCMP].rearrange("p (h c) -> p h c", c=NCMP),
                                             HD ** -0.5, cbias[:, t, odd::2, :], ALU.mult, ALU.add).then_inc(emptied["scorec"], 1)
                dve.wait_ge(emptied["scorec"], 2 * t + 2)
                run(vec.tensor_reduce(cm[:, 0, t], sc[:, t], AX_X, ALU.max))
                vec.tensor_tensor(sc[:, t], sc[:, t], over_c(cm[:, 0, t]), ALU.subtract).then_inc(cshift, 1)
            dve.wait_ge(cexp, 1)
            dve.wait_ge(emptied["gn"], 1)
            for t in range(TT):
                run(vec.tensor_reduce(cm[:, 0, t], sc[:, t], AX_X, ALU.add))
                run(vec.reciprocal(cm[:, 0, t], cm[:, 0, t]))
                run(vec.tensor_tensor(cm[:, 1, t], cm[:, 0, t], gn[:, t, 0:3 * H2:3], ALU.mult))
                seen = const[:, C_SEEN + t * NCMP:C_SEEN + (t + 1) * NCMP].unsqueeze(1).broadcast_to([P, H2, NCMP])
                run(vec.tensor_tensor(sc[:, t], sc[:, t], seen, ALU.mult))
                vec.tensor_tensor(pc[:, t, :, 0:NCMP], sc[:, t], over_c(cm[:, 1, t]), ALU.mult).then_inc(pc_ready, 1)

            dve.wait_ge(bias_in, 32)
            N = 2 * H2
            for i in range(N + 1):
                if i < N:
                    if i >= 2:
                        dve.wait_ge(exps_ready, 2 * (i - 1))
                    dve.wait_ge(filled["score"], i + 1)
                    s, m = S[:, i % 2], smax[:, i % 2]
                    vec.scalar_tensor_tensor(s, bank("score", i)[:, 0:3 * P], HD ** -0.5, bias3[:, i // 2, :],
                                             ALU.mult, ALU.add).then_inc(emptied["score"], 1)
                    dve.wait_ge(emptied["score"], i + 1)
                    step(vec.tensor_reduce(m[:, 0:1], s[:, 0:P], AX_X, ALU.max))
                    run(vec.tensor_reduce(m[:, 1:2], s[:, P:], AX_X, ALU.max))
                    vec.tensor_scalar(m, m, -1.0, None, ALU.mult).then_inc(smax_ready, 1)
                if i >= 1:
                    g = (i - 1) % 2
                    hd, n = (i - 1) // 2, (i - 1) % 2
                    dve.wait_ge(exps_ready, 2 * i)
                    run(vec.reciprocal(ssum[:, g], ssum[:, g]))
                    col_ = 3 * hd + 1 + n
                    run(vec.tensor_tensor(ssum[:, g], ssum[:, g], gn[:, :, col_], ALU.mult))
                    vec.tensor_scalar(E[:, g, 0:P], E[:, g, 0:P], ssum[:, g, 0:1], None, ALU.mult)
                    vec.tensor_scalar(E[:, g, P:], E[:, g, P:], ssum[:, g, 1:2], None, ALU.mult).then_inc(probs_ready, 1)
            for b in range(4):
                dve.wait_ge(filled["y_b"], b + 1)
                x = rstd[:]
                if b:
                    dve.wait_ge(emptied["y_b"], b)
                run(vec.tensor_tensor(x, bank("y_b", b)[:], flat(gates_ab[:, 1, 2 * b:2 * b + 2, :]), ALU.mult))
                y = flat(merged[:, 2 * b:2 * b + 2, :])
                vec.tensor_tensor(y, y, x, ALU.add).then_inc(emptied["y_b"], 1)
            for b in range(4):
                dve.wait_ge(filled["w_out"], b + 1)
                x = flat(xT[:, 2 * b:2 * b + 2, :])
                vec.tensor_tensor(x, x, bank("w_out", b)[:], ALU.add).then_inc(emptied["w_out"], 1)
            dve.wait_ge(emptied["w_out"], 4)
            normalise("mlp", "norm_mlp_2", hT)
            for b in range(16):
                dve.wait_ge(emptied["mlp_in"], b + 1)
                x = stat[:, b % 2]
                vec.tensor_tensor(hidden(2 * b, 2), x, x, ALU.mult).then_inc(squared, 1)

    return sems


_INS = ["x", "p", "norm_mix", "w_in", "w_dw", "b_dw", "ln_conv_g", "ln_conv_b", "w_attn_out", "w_conv_out", "b_conv_out",
        "w_out", "norm_ffn", "w_route_group", "b_route_group", "w_route_expert", "b_route_expert", "w_exp_gate",
        "w_exp_up", "w_exp_down", "norm_ple", "w_ple_proj", "w_ple_gate", "norm_final"]
_INS += [n + "_2" for n in (
    "norm_mix", "w_in", "conv_w", "conv_b", "gate_a_w", "gate_a_b", "gate_x_w", "gate_x_b", "lru_lambda", "phi_k_pe",
    "phi_k_w1", "phi_k_w2", "phi_v_pe", "phi_v_w1", "phi_v_w2", "q_norm", "kc_norm", "ks_norm", "kw_norm", "rel_bias",
    "proj_a", "proj_b", "w_out", "norm_mlp", "w_mlp_in", "w_mlp_out")]


def build(nc, dram, table, far, near, out):
    with ExitStack() as ctx:
        def sb(name, shape, dt=F32):
            return ctx.enter_context(nc.sbuf_tensor(name, shape, dt))

        keep = dict(xT=sb("xT", [P, DC, T]), hT=sb("hT", [P, DC, T]), sq=sb("sq", [P, DC, T]), eps=sb("eps", [P, 1]),
                    ones=dict(D=sb("ones_d", [P, P]), C=sb("ones_c", [P, P])))
        keep["ps"] = [ctx.enter_context(nc.psum_tensor(f"ps{i}", [P, BANK], F32)) for i in range(BANKS)]
        const = sb("const", [P, C_COLS])
        ps, xT = keep["ps"], keep["xT"]

        with ExitStack() as pro:
            xtok = pro.enter_context(nc.sbuf_tensor("xtok", [P, TT, D], F32))
            loaded, turned, copied = (pro.enter_context(nc.semaphore(n)) for n in ("loaded", "turned", "copied"))
            with nc.Block(no_gpsimd_drain=True) as block:
                @block.sync
                def _(sp):
                    sp.dma_start(xtok[:], dram["x"][0].rearrange("(t p) n -> p t n", p=P)).then_inc(loaded, 16)
                    sp.dma_start(const[:], table).then_inc(loaded, 16)

                @block.tensor
                def _(pe):
                    pe.wait_ge(loaded, 32)
                    for b in range(4):
                        for m in range(2):
                            for t in range(TT):
                                c = 2 * b + m
                                mm = nc.tensor.transpose(ps[b][:, m * T + t * P:m * T + (t + 1) * P], xtok[:, t, c * P:(c + 1) * P],
                                                         const[:, C_ID:C_ID + P])
                        mm.then_inc(turned, 1)

                @block.vector
                def _(dve):
                    nc.vector.memset(keep["eps"][:], EPS)
                    nc.vector.memset(keep["ones"]["D"][:], 1.0 / D)
                    nc.vector.memset(keep["ones"]["C"][:], 1.0 / CW)
                    for b in range(4):
                        dve.wait_ge(turned, b + 1)
                        nc.vector.tensor_copy(xT[:, 2 * b:2 * b + 2, :].rearrange("p c n -> p (c n)"), ps[b][:]).then_inc(copied, 1)

            clear(nc, (loaded, turned, copied))

        with ExitStack() as one:
            with nc.Fori(0, DEPTH) as layer:
                clear(nc, first_block_layer(nc, one, dram, const, keep, layer))
        with ExitStack() as two:
            second_block(nc, two, dram, const, keep, nc.dram_tensor("bias_rows", (H2, P, SKEW), F32).ap(), out)


def kernel(**inputs):
    import concourse.bacc as _bacc
    from concourse.bass_utils import run_bass_kernel_spmd as _run

    nc = _bacc.Bacc("TRN2", target_bir_lowering=False, num_devices=1)
    arrays, dram = {}, {}
    tables = dict(zip(("table", "far", "near"), constants()))
    tables["off"] = np.full((1, H2), NEG, np.float32)
    for name, a in [(n, inputs[n]) for n in _INS] + list(tables.items()):
        a = np.ascontiguousarray(a)
        arrays[f"in_{name}"] = a
        dram[name] = nc.dram_tensor(f"in_{name}", a.shape, mybir.dt.from_np(a.dtype), kind="ExternalInput").ap()
    out = nc.dram_tensor("out_0", (1, T, D), F32, kind="ExternalOutput").ap()
    build(nc, dram, dram["table"], dram["far"], dram["near"], out)
    r = _run(nc, [arrays], core_ids=[0])
    return r.results[0]["out_0"]
```

```python
from contextlib import ExitStack

import concourse.bass as bass
import numpy as np
from concourse import mybir

F32 = mybir.dt.float32
U32 = mybir.dt.uint32
ALU = mybir.AluOpType
ACT = mybir.ActivationFunctionType
AX_X = mybir.AxisListType.X

P = 128
T = 256
TT = T // P
D = 1024
DC = D // P
BANK = 512
BANKS = 8
EPS = 1e-6
NEG = -1e30

DEPTH = 2
HEADS, HD = 8, 64
AW = HEADS * HD
AC = AW // P
CW = 512
CC = CW // P
TAPS = 31
GROUPS, PER_GROUP, FF = 4, 8, 512
EXPERTS = GROUPS * PER_GROUP
FC = FF // P
SLOTS = 64
PLE = 256
ROUTES = GROUPS + EXPERTS
W_IN_COLS = 3 * AW + 2 * CW + 2 * D
DILATED = ((128, 1), (512, 4), (2048, 16))

RNN, RP = 1344, 112
RC = RNN // RP
RBLOCKS = 4
RB = RC // RBLOCKS
RTAPS = 4
H2, KVG = 16, 4
HPG = H2 // KVG
KVW = KVG * HD
CMP, STRIDE = 32, 16
NCMP = (T - CMP) // STRIDE + 1
PHI = 256
BUCKETS, MAX_DIST = 32, 128
SKEW = 2 * T + 1
DFF = 4 * D
IN2 = dict(u_rnn=0, u_gate=RNN, q=2 * RNN)
IN2["kc"] = IN2["q"] + H2 * HD
IN2["ks"] = IN2["kc"] + 2 * KVW
IN2["kw"] = IN2["ks"] + 2 * KVW
IN2["g_nsa"] = IN2["kw"] + 2 * KVW
IN2["g_a"] = IN2["g_nsa"] + 3 * H2
IN2["g_b"] = IN2["g_a"] + D
assert IN2["g_b"] + D == 7344

C_ID, C_MASK, C_COS, C_SIN, C_HEAD, C_IOTA, C_SEEN = 0, 128, 512, 768, 1024, 1152, 1160
C_SLOT = C_SEEN + TT * NCMP
C_UPTO = C_SLOT + SLOTS
C_ONE = C_UPTO + P
C_COLS = C_ONE + P


def constants():
    c = np.zeros((P, C_COLS), np.float32)
    c[:, C_ID:C_ID + P] = np.eye(P)
    for n, off in enumerate((0, P, 0)):
        d = off + np.arange(P)[:, None] - np.arange(P)[None, :]
        count = sum(((d >= 0) & (d % dil == 0) & (d <= win)).astype(np.float32) for win, dil in DILATED)
        c[:, C_MASK + n * P:C_MASK + (n + 1) * P] = np.where(count > 0, np.log(np.maximum(count, 1)), NEG)
    inv = np.power(np.float32(10000.0), -np.arange(0, HD, 2, dtype=np.float32) / np.float32(HD))
    ang = (np.arange(T, dtype=np.float32)[:, None] * inv[None, :]).T.astype(np.float32)
    for q in range(4):
        c[32 * q:32 * q + 32, C_COS:C_COS + T] = np.cos(ang)
        c[32 * q:32 * q + 32, C_SIN:C_SIN + T] = np.sin(ang) * (-1 if q % 2 == 0 else 1)
    for h in range(2):
        c[HD * h:HD * h + HD, C_HEAD + HD * h:C_HEAD + HD * h + HD] = 1.0 / HD
    c[:, C_IOTA:C_IOTA + 8] = np.arange(8)
    ends = np.arange(NCMP) * STRIDE + CMP - 1
    for t in range(TT):
        c[:, C_SEEN + t * NCMP:C_SEEN + (t + 1) * NCMP] = ends[None, :] <= (t * P + np.arange(P))[:, None]
    c[:, C_SLOT:C_SLOT + SLOTS] = 1 + np.arange(SLOTS)
    c[:, C_UPTO:C_UPTO + P] = np.arange(P)[:, None] <= np.arange(P)[None, :]
    c[:, C_ONE:C_ONE + P] = 1.0

    def one_hot(d):
        d = d.reshape(-1)
        near = BUCKETS // 2
        df = np.maximum(d, 1).astype(np.float32)
        large = near + (np.log(df / near) / np.float32(np.log(MAX_DIST / near)) * (BUCKETS - near)).astype(np.int32)
        b = np.where(d < near, d, np.minimum(large, BUCKETS - 1))
        b = np.where(d < 0, BUCKETS, b)
        return (np.arange(BUCKETS + 1)[:, None] == b[None, :]).astype(np.float32)

    far = one_hot(2 * T // 2 - 1 - np.arange(2 * T))
    cmp_d = np.arange(T).reshape(TT, 1, P) - ends.reshape(1, NCMP, 1)
    return c, far, one_hot(cmp_d)


class Chain:

    def __init__(self, eng, sem):
        self.eng, self.sem, self.n = eng, sem, 0

    def __call__(self, ins):
        ins.then_inc(self.sem, 1)
        self.n += 1

    def settle(self):
        self.eng.wait_ge(self.sem, self.n)


def clear(nc, sems):
    nums = sorted(s.num for s in sems)
    assert nums == list(range(nums[0], nums[0] + len(nums)))
    nc.sync.sem_clear(range(nums[0], nums[-1] + 1))
    nc.all_engine_barrier()


def first_block_layer(nc, ctx, dram, const, keep, layer):
    R = 6

    def sb(name, shape, dt=F32):
        return ctx.enter_context(nc.sbuf_tensor("l_" + name, shape, dt))

    sems = []

    def sem(name):
        sems.append(ctx.enter_context(nc.semaphore("l_" + name)))
        return sems[-1]

    xT, hT, sq, eps, ones = keep["xT"], keep["hT"], keep["sq"], keep["eps"], keep["ones"]
    ps = keep["ps"]
    ident = const[:, C_ID:C_ID + P]
    ring = sb("ring", [P, R, 4096])
    rows = sb("rows", [48, P])
    taprows = sb("taprows", [TAPS, CW])
    par = sb("par", [P, 48 + CC * TAPS])
    wroute = sb("wroute", [P, DC, ROUTES])
    broute = sb("broute", [1, ROUTES])
    one_row = sb("one_row", [1, P])
    ptok = sb("ptok", [P, TT, PLE])
    pT = sb("pT", [P, PLE // P, T])
    stat = sb("stat", [P, T])
    rstd = sb("rstd", [P, T])
    u = sb("u", [P, CC, TAPS - 1 + T])
    conv = sb("conv", [P, CC, T])
    sig = sb("sig", [P, 2, BANK])
    raw = sb("raw", [P, 2, BANK])
    rot = sb("rot", [P, 2, BANK])
    qk = sb("qk", [P, 2, AC, T])
    v = sb("v", [P, TT, AW])
    gates_ab = sb("gates_ab", [P, 2, DC, T])
    attn = sb("attn", [P, AC, T])
    merged = sq
    S = sb("S", [P, 2, 3 * P])
    E = sb("E", [P, 2, 3 * P])
    PT = sb("PT", [P, 2, 3 * P])
    smax = sb("smax", [P, 2, 2])
    ssum = sb("ssum", [P, 2, 2])
    logit = sb("logit", [P, TT, ROUTES])
    rt = sb("rt", [P, TT, 64])
    top = sb("top", [P, TT, 2, 8])
    topi = sb("topi", [P, TT, 2, 8], U32)
    gate = sb("gate", [P, TT, EXPERTS + 2])
    place = sb("place", [P, TT, EXPERTS + 2])
    gate_over = sb("gate_over", [P, TT, EXPERTS])
    most = sb("most", [1, 1], U32)
    silu = sb("silu", [P, FC, T])
    hid = qk[:, 0]
    htok = gates_ab[:, 0].rearrange("p (t c) n -> p t (c n)", t=TT)
    yacc = htok
    spare = gates_ab[:, 1].rearrange("p c n -> p (c n)")
    y_slots = spare[:, 0:D]
    x_slots = sq[:].rearrange("p c n -> p (c n)")[:, 0:DC * 2 * SLOTS].rearrange("p (c j s) -> p c j s", c=DC, j=2)
    pick = spare[:, 1536:1792].rearrange("p (t j s) -> p t j s", t=TT, j=2)
    pick_gate = spare[:, 1792:2048].rearrange("p (t j s) -> p t j s", t=TT, j=2)
    put = S[:, 0, 0:T]
    zrow = E[0:1].rearrange("p a n -> p (a n)")
    hid_slots = hid.rearrange("p c n -> p (c n)")[:, 0:FC * SLOTS]
    silu_slots = silu[:].rearrange("p c n -> p (c n)")[:, 0:FC * SLOTS]

    names = ("norm_mix", "b_dw", "ln_conv_g", "ln_conv_b", "b_conv_out", "norm_ffn", "norm_ple")
    col, at = {}, 0
    for n in names:
        col[n] = at
        at += dram[n].shape[-1] // P
    n_rows = at
    TAP0 = 48

    def param(name, c):
        return par[:, col[name] + c:col[name] + c + 1]

    def tap(c, k):
        return par[:, TAP0 + c * TAPS + k:TAP0 + c * TAPS + k + 1]

    stages = dict(params=1, mean_mix=1, cu=2, cg=2, q=2, k=2, v=2, ga=4, gb=4, score=HEADS, probT=HEADS,
                  o=AC, y_a=4, ln_mean=1, ln_var=1, y_b=4, w_out=4, mean_ffn=1, route=1,
                  htok=4, place=1, slots_x=2, slots_gate=2, slots_up=2, slots_down=2, slots_put=1,
                  gate_up=FC, down=4, turn=4, pT=1, ple=4, mean_ple=1, ple_gate=4)
    banks, n = {}, 0
    for stage, count in stages.items():
        if stage in ("gate_up", "down") or stage.startswith("slots"):
            n = 0
            continue
        for i in range(count):
            if stage in ("score", "probT", "o"):
                banks[stage, i] = {"score": i % 3, "probT": 3 + i % 3, "o": 6 + i % 2}[stage]
            else:
                banks[stage, i] = n % BANKS
                n += 1

    def bank(stage, i=0):
        return ps[banks[stage, i]]

    exp_bank = ps.__getitem__

    filled = {s: sem("filled_" + s) for s in stages}
    emptied = {s: sem("emptied_" + s) for s in stages}
    landed = [sem(f"landed{i}") for i in range(R)]
    params_in = sem("params_in")
    dve_steps, act_steps = sem("dve_steps"), sem("act_steps")
    squares = {n: sem("squares_" + n) for n in ("mix", "ffn", "ple")}
    normed = {n: sem("normed_" + n) for n in ("mix", "ffn", "ple")}
    centred, conv_act, rope_raw = sem("centred"), sem("conv_act"), sem("rope_raw")
    conv_out = sem("conv_out")
    ln_done = sem("ln_done")
    smax_ready, exps_ready, probs_ready = sem("smax_ready"), sem("exps_ready"), sem("probs_ready")
    silu_ready = sem("silu_ready")
    mask_ready, pick_ready, pick_gate_ready, combined = (sem(n) for n in ("mask_ready", "pick_ready", "pick_gate_ready", "combined"))
    place_steps, zeroed = sem("place_steps"), sem("zeroed")
    lmax_ready, lexp_ready, pair_ready, pexp_ready = sem("lmax"), sem("lexp"), sem("pair"), sem("pexp")

    lay = bass.ds(layer, 1)

    def w_cols(name, c0, n=BANK):
        return lambda: dram[name][lay, :, c0:c0 + n].rearrange("a (c p) n -> p (a c) n", p=P)

    def w_all(name):
        return lambda: dram[name][lay].rearrange("a (c p) n -> p (a c) n", p=P)

    cu0, cg0 = 3 * AW, 3 * AW + CW
    ga0, gb0 = cg0 + CW, cg0 + CW + D
    stream = [
        (w_cols("w_in", cu0), "cu", 2), (w_cols("w_in", cg0), "cg", 2),
        (w_cols("w_in", 0), "q", 2), (w_cols("w_in", AW), "k", 2), (w_cols("w_in", 2 * AW), "v", 2),
        (w_cols("w_in", ga0), "ga", 2), (w_cols("w_in", ga0 + BANK), "ga", 4),
        (w_cols("w_in", gb0), "gb", 2), (w_cols("w_in", gb0 + BANK), "gb", 4),
        (w_all("w_attn_out"), "y_a", 4), (w_all("w_conv_out"), "y_b", 4),
        (w_cols("w_out", 0), "w_out", 2), (w_cols("w_out", BANK), "w_out", 4),
    ]
    N0 = len(stream)
    TURNS = EXPERTS // 2
    PER_TURN = 6
    N1 = N0 + PER_TURN * TURNS
    over_slots = [N1 + 3 + j for j in range(3)]
    tail = [(w_cols("w_ple_gate", 0), "ple_gate", 2), (w_cols("w_ple_gate", BANK), "ple_gate", 4),
            (w_all("w_ple_proj"), "ple", 4)]

    def slot(i, rows_=DC, part=P):
        return ring[0:part, i % R].rearrange("p (c n) -> p c n", c=rows_)

    def expert_weights(e, j):
        name = ("w_exp_gate", "w_exp_up", "w_exp_down")[j % 3]
        w = dram[name][lay, bass.ds(e * 2 + j // 3, 1)].rearrange("a b (c p) n -> p (a b c) n", p=P)
        return w, (FC if j % 3 == 2 else DC)

    def wide(x, n=2):
        return x.unsqueeze(1).broadcast_to([P, n, T])

    def chunks(b):
        return slice(2 * b, 2 * b + 2)

    def flat(x):
        return x.rearrange("p c n -> p (c n)")

    def squares_and_root(act, name):
        for h in range(2):
            nc.scalar.activation(sq[:, 4 * h:4 * h + 4, :], xT[:, 4 * h:4 * h + 4, :], ACT.Square).then_inc(squares[name], 1)
        act.wait_ge(filled["mean_" + name], 1)
        nc.scalar.activation(stat[:], bank("mean_" + name)[:, 0:T], ACT.Sqrt, bias=eps[:, 0:1]).then_inc(emptied["mean_" + name], 1)

    def normalise(dve, step, name):
        dve.wait_ge(emptied["mean_" + name], 1)
        step(nc.vector.reciprocal(rstd[:], stat[:]))
        step.settle()
        for c in range(DC):
            nc.vector.scalar_tensor_tensor(hT[:, c, :], xT[:, c, :], param("norm_" + name, c), rstd[:],
                                           ALU.mult, ALU.mult).then_inc(normed[name], 1)

    def claimer(pe):
        last_in = {}

        def claim(stage, i):
            b = banks[stage, i]
            if b in last_in:
                s, n = last_in[b]
                pe.wait_ge(emptied[s], n + 1)
            last_in[b] = (stage, i)
            return ps[b]

        return claim, last_in

    def mean(pe, claim, name, src, chunks_, sem_ready, stage, step=4):
        out = claim(stage, 0)
        for c in range(chunks_):
            if c % step == 0:
                pe.wait_ge(sem_ready, c // step + 1)
            mm = nc.tensor.matmul(out[:, 0:T], ones[name][:], src[:, c, :], start=(c == 0), stop=(c == chunks_ - 1))
        mm.then_inc(filled[stage], 1)

    def project(claim, i, stage, n0, src, kc, cols=4):
        w = slot(i, kc)
        for b in range(cols // 2):
            out = claim(stage, n0 + b)
            for m in range(2):
                for k in range(kc):
                    mm = nc.tensor.matmul(out[:, m * T:(m + 1) * T], w[:, k, (2 * b + m) * P:(2 * b + m + 1) * P],
                                          src[:, k, :], start=(k == 0), stop=(k == kc - 1))
            mm.then_inc(filled[stage], 1)

    def over_block():
        with nc.Block(no_gpsimd_drain=True) as block:

            @block.sync
            def _(sp):
                def load(e, j):
                    w = dram[("w_exp_gate", "w_exp_up", "w_exp_down")[j]][lay, bass.ds(e, 1)]
                    sp.dma_start(slot(over_slots[j], FC if j == 2 else DC), w.rearrange("a b (c p) n -> p (a b c) n", p=P))\
                        .then_inc(landed[j], 16)

                for j in range(3):
                    load(0, j)
                with sp.Fori(1, EXPERTS) as e:
                    for j in range(3):
                        sp.wait_ge(filled["down" if j == 2 else "gate_up"], e * 4)
                        load(e, j)

            @block.tensor
            def _(pe):
                pe.sem_inc(emptied["gate_up"], 4)
                pe.sem_inc(emptied["down"], 4)
                with pe.Fori(0, EXPERTS) as e:
                    pe.wait_ge(landed[0], (e + 1) * 16)
                    pe.wait_ge(landed[1], (e + 1) * 16)
                    for f in range(FC):
                        pe.wait_ge(emptied["gate_up"], e * 4 + (f + 1))
                        for half in range(2):
                            for k in range(DC):
                                mm = nc.tensor.matmul(ps[f][:, half * T:(half + 1) * T], slot(over_slots[half])[:, k, f * P:(f + 1) * P],
                                                      hT[:, k, :], start=(k == 0), stop=(k == DC - 1))
                        mm.then_inc(filled["gate_up"], 1)
                    pe.wait_ge(landed[2], (e + 1) * 16)
                    pe.wait_ge(emptied["gate_up"], e * 4 + 8)
                    for t in range(TT):
                        for half in range(2):
                            n = 2 * t + half
                            pe.wait_ge(emptied["down"], e * 4 + (n + 1))
                            for k in range(FC):
                                mm = nc.tensor.matmul(ps[4 + n][:], hid[:, k, t * P:(t + 1) * P],
                                                      slot(over_slots[2], FC)[:, k, half * BANK:(half + 1) * BANK],
                                                      start=(k == 0), stop=(k == FC - 1))
                            mm.then_inc(filled["down"], 1)
                pe.wait_ge(emptied["down"], EXPERTS * 4 + 4)
                for b in range(4):
                    for m in range(2):
                        for t in range(TT):
                            c = 2 * b + m
                            mm = nc.tensor.transpose(bank("turn", b)[:, m * T + t * P:m * T + (t + 1) * P],
                                                     yacc[:, t, c * P:(c + 1) * P], ident)
                    mm.then_inc(filled["turn"], 1)

            @block.gpsimd
            def _(pool):
                nc.gpsimd.memset(yacc, 0.0).then_inc(zeroed, 1)

            @block.scalar
            def _(act):
                with act.Fori(0, EXPERTS) as e:
                    for f in range(FC):
                        act.wait_ge(filled["gate_up"], e * 4 + (f + 1))
                        nc.scalar.activation(silu[:, f], ps[f][:, 0:T], ACT.Silu).then_inc(silu_ready, 1)

            @block.vector
            def _(dve):
                vec = nc.vector
                dve.wait_ge(zeroed, 1)
                with dve.Fori(0, EXPERTS) as e:
                    for f in range(FC):
                        dve.wait_ge(silu_ready, e * 4 + (f + 1))
                        vec.tensor_tensor(hid[:, f, :], ps[f][:, T:2 * T], silu[:, f], ALU.mult).then_inc(emptied["gate_up"], 1)
                    dve.wait_ge(emptied["down"], e * 4 + 4)
                    for t in range(TT):
                        for half in range(2):
                            n = 2 * t + half
                            dve.wait_ge(filled["down"], e * 4 + (n + 1))
                            y = yacc[:, t, half * BANK:(half + 1) * BANK]
                            vec.scalar_tensor_tensor(y, ps[4 + n][:], gate_over[:, t, bass.ds(e, 1)], y,
                                                     ALU.mult, ALU.add).then_inc(emptied["down"], 1)
                for b in range(4):
                    dve.wait_ge(filled["turn"], b + 1)
                    x = flat(xT[:, chunks(b), :])
                    vec.tensor_tensor(x, x, bank("turn", b)[:], ALU.add)

    def ple_block():
        with nc.Block(no_gpsimd_drain=True) as block:

            @block.tensor
            def _(pe):
                claim, _ = claimer(pe)
                out = claim("pT", 0)
                for c in range(PLE // P):
                    for t in range(TT):
                        mm = nc.tensor.transpose(out[:, c * T + t * P:c * T + (t + 1) * P], ptok[:, t, c * P:(c + 1) * P], ident)
                mm.then_inc(filled["pT"], 1)
                pe.wait_ge(emptied["pT"], 1)
                for b in range(4):
                    out = claim("ple", b)
                    for m in range(2):
                        for k in range(PLE // P):
                            c = 2 * b + m
                            w = slot(N1 + 2, PLE // P)
                            mm = nc.tensor.matmul(out[:, m * T:(m + 1) * T], w[:, k, c * P:(c + 1) * P], pT[:, k, :],
                                                  start=(k == 0), stop=(k == PLE // P - 1))
                    mm.then_inc(filled["ple"], 1)
                mean(pe, claim, "D", sq, DC, squares["ple"], "mean_ple")
                pe.wait_ge(normed["ple"], DC)
                for i in range(2):
                    project(claim, N1 + i, "ple_gate", 2 * i, hT, DC)

            @block.scalar
            def _(act):
                for h in range(2):
                    nc.scalar.activation(sq[:, 4 * h:4 * h + 4, :], xT[:, 4 * h:4 * h + 4, :], ACT.Square).then_inc(squares["ple"], 1)
                act.wait_ge(filled["pT"], 1)
                nc.scalar.copy(pT[:].rearrange("p c n -> p (c n)"), bank("pT")[:]).then_inc(emptied["pT"], 1)
                act.wait_ge(filled["mean_ple"], 1)
                nc.scalar.activation(stat[:], bank("mean_ple")[:, 0:T], ACT.Sqrt, bias=eps[:, 0:1]).then_inc(emptied["mean_ple"], 1)
                for b in range(4):
                    act.wait_ge(filled["ple_gate"], b + 1)
                    nc.scalar.activation(flat(gates_ab[:, 1, chunks(b), :]), bank("ple_gate", b)[:], ACT.Sigmoid)\
                        .then_inc(emptied["ple_gate"], 1)

            @block.vector
            def _(dve):
                step = Chain(dve, dve_steps)
                vec = nc.vector
                for b in range(4):
                    dve.wait_ge(filled["ple"], b + 1)
                    vec.tensor_copy(flat(gates_ab[:, 0, chunks(b), :]), bank("ple", b)[:]).then_inc(emptied["ple"], 1)
                dve.wait_ge(emptied["ple"], 4)
                normalise(dve, step, "ple")
                for b in range(4):
                    dve.wait_ge(emptied["ple_gate"], b + 1)
                    y = flat(gates_ab[:, 0, chunks(b), :])
                    step(vec.tensor_tensor(y, y, flat(gates_ab[:, 1, chunks(b), :]), ALU.mult))
                    step.settle()
                    x = flat(xT[:, chunks(b), :])
                    vec.tensor_tensor(x, x, y, ALU.add)

    with nc.Block(no_gpsimd_drain=True) as block:

        @block.sync
        def _(sp):
            at = 0
            for n in names:
                k = dram[n].shape[-1] // P
                sp.dma_start(rows[at:at + k, :], dram[n][lay].rearrange("a (c p) -> (a c) p", p=P)).then_inc(params_in, 16)
                at += k
            sp.dma_start(taprows[:], dram["w_dw"][lay].rearrange("a k c -> (a k) c")).then_inc(params_in, 16)
            sp.dma_start(wroute[:, :, 0:GROUPS], dram["w_route_group"][lay].rearrange("a (c p) n -> p (a c) n", p=P)).then_inc(params_in, 16)
            sp.dma_start(wroute[:, :, GROUPS:], dram["w_route_expert"][lay].rearrange("a (c p) n -> p (a c) n", p=P)).then_inc(params_in, 16)
            sp.dma_start(broute[:, 0:GROUPS], dram["b_route_group"][lay]).then_inc(params_in, 16)
            sp.dma_start(broute[:, GROUPS:], dram["b_route_expert"][lay]).then_inc(params_in, 16)
            sp.dma_start(ptok[:], dram["p"][lay, 0].rearrange("a (t p) n -> p (a t) n", p=P)).then_inc(params_in, 16)
            for i, (src, _, _) in enumerate(stream):
                if i >= R:
                    _, stage, n = stream[i - R]
                    sp.wait_ge(filled[stage], n)
                s = src()
                sp.dma_start(slot(i, s.shape[1]), s).then_inc(landed[i % R], 16)
            for j in range(PER_TURN):
                _, stage, n = stream[N0 + j - R]
                sp.wait_ge(filled[stage], n)
                s, k = expert_weights(0, j)
                sp.dma_start(slot(N0 + j, k), s).then_inc(landed[(N0 + j) % R], 16)
            with sp.Fori(1, TURNS) as e:
                for j in range(PER_TURN):
                    sp.wait_ge(filled["slots_" + ("gate", "up", "down")[j % 3]], (e - 1) * 2 + (j // 3 + 1))
                    s, k = expert_weights(e, j)
                    sp.dma_start(slot(N0 + j, k), s).then_inc(landed[(N0 + j) % R], 16)
            for j, (src, _, _) in enumerate(tail):
                sp.wait_ge(filled["slots_" + ("gate", "up", "down")[j]], 2 * TURNS - 1)
                s = src()
                sp.dma_start(slot(N1 + j, s.shape[1])[:, :, 0:s.shape[2]], s).then_inc(landed[(N1 + j) % R], 16)
            for j in range(len(tail)):
                sp.wait_ge(landed[(N1 + j) % R], 16 * ((N1 + j) // R + 1))

        @block.tensor
        def _(pe):
            claim, last_in = claimer(pe)

            def weights(i):
                pe.wait_ge(landed[i % R], 16 * (i // R + 1))

            pe.wait_ge(params_in, 16 * (len(names) + 6))
            out = claim("params", 0)
            nc.tensor.transpose(out[:, 0:n_rows], rows[0:n_rows, :], ident[0:n_rows, 0:n_rows])
            for c in range(CC):
                mm = nc.tensor.transpose(out[:, TAP0 + c * TAPS:TAP0 + (c + 1) * TAPS],
                                         taprows[:, c * P:(c + 1) * P], ident[0:TAPS, 0:TAPS])
            mm.then_inc(filled["params"], 1)
            mean(pe, claim, "D", sq, DC, squares["mix"], "mean_mix")
            pe.wait_ge(normed["mix"], DC)
            for i, stage in enumerate(("cu", "cg", "q", "k")):
                weights(i)
                project(claim, i, stage, 0, hT, DC)
            weights(4)
            for t in range(TT):
                out = claim("v", t)
                for k in range(DC):
                    mm = nc.tensor.matmul(out[:], hT[:, k, t * P:(t + 1) * P], slot(4)[:, k, :], start=(k == 0), stop=(k == DC - 1))
                mm.then_inc(filled["v"], 1)
            for i, (stage, n0) in enumerate((("ga", 0), ("ga", 2), ("gb", 0), ("gb", 2))):
                weights(5 + i)
                project(claim, 5 + i, stage, n0, hT, DC)

            pe.wait_ge(emptied["q"], 2)
            pe.wait_ge(emptied["k"], 2)
            pe.wait_ge(emptied["v"], 2)

            def score(h):
                out = claim("score", h)
                r = slice(HD * (h % 2), HD * (h % 2) + HD)
                q, k = qk[r, 0, h // 2, :], qk[r, 1, h // 2, :]
                nc.tensor.matmul(out[:, 0:P], q[:, 0:P], k[:, 0:P], start=True, stop=True)
                nc.tensor.matmul(out[:, P:3 * P], q[:, P:T], k, start=True, stop=True).then_inc(filled["score"], 1)

            def prob_t(h):
                out = claim("probT", h)
                pe.wait_ge(probs_ready, h + 1)
                e = E[:, h % 2]
                nc.tensor.transpose(out[:, 0:P], e[:, 0:P], ident)
                nc.tensor.transpose(out[:, P:T], e[:, P:T], ident)
                nc.tensor.transpose(out[:, T:3 * P], e[:, T:3 * P], ident).then_inc(filled["probT"], 1)

            def values(h):
                if h % 2 == 0:
                    claim("o", h // 2)
                pe.wait_ge(emptied["probT"], h + 1)
                r = slice(HD * (h % 2), HD * (h % 2) + HD)
                out = ps[banks["o", h // 2]][r, 0:T]
                pt = PT[:, h % 2]
                nc.tensor.matmul(out, v[:, 0, h * HD:(h + 1) * HD], pt[:, 0:T], start=True, stop=False)
                mm = nc.tensor.matmul(out[:, P:T], v[:, 1, h * HD:(h + 1) * HD], pt[:, T:3 * P], start=False, stop=True)
                mm.then_inc(filled["o"], 1)

            for i in range(HEADS + 3):
                if i < HEADS:
                    score(i)
                if 2 <= i < HEADS + 2:
                    prob_t(i - 2)
                if i >= 3:
                    values(i - 3)

            mean(pe, claim, "C", conv, CC, conv_out, "ln_mean", 1)
            mean(pe, claim, "C", sq, CC, centred, "ln_var", 1)
            pe.wait_ge(emptied["o"], AC)
            weights(9)
            project(claim, 9, "y_a", 0, attn, AC, cols=8)
            pe.wait_ge(conv_act, CC)
            weights(10)
            project(claim, 10, "y_b", 0, conv, CC, cols=8)
            pe.wait_ge(emptied["y_b"], 4)
            weights(11)
            project(claim, 11, "w_out", 0, merged, DC)
            weights(12)
            project(claim, 12, "w_out", 2, merged, DC)
            mean(pe, claim, "D", sq, DC, squares["ffn"], "mean_ffn")
            pe.wait_ge(normed["ffn"], DC)
            out = claim("route", 0)
            for t in range(TT):
                o = out[:, t * ROUTES:(t + 1) * ROUTES]
                for k in range(DC):
                    nc.tensor.matmul(o, hT[:, k, t * P:(t + 1) * P], wroute[:, k, :], start=(k == 0), stop=False)
                mm = nc.tensor.matmul(o, one_row[:], broute[:], start=False, stop=True)
            mm.then_inc(filled["route"], 1)

            for b in range(4):
                out = claim("htok", b)
                t, half = b // 2, b % 2
                for c in range(4):
                    mm = nc.tensor.transpose(out[:, c * P:(c + 1) * P], hT[:, 4 * half + c, t * P:(t + 1) * P], ident)
                mm.then_inc(filled["htok"], 1)
            out = claim("place", 0)
            pe.wait_ge(mask_ready, 1)
            upto, one = const[:, C_UPTO:C_UPTO + P], const[:, C_ONE:C_ONE + P]
            nc.tensor.matmul(out[:, 0:EXPERTS], upto, gate_over[:, 0, :], start=True, stop=True)
            nc.tensor.matmul(out[:, EXPERTS:2 * EXPERTS], one, gate_over[:, 0, :], start=True, stop=False)
            nc.tensor.matmul(out[:, EXPERTS:2 * EXPERTS], upto, gate_over[:, 1, :], start=False, stop=True)
            nc.tensor.matmul(out[0:1, 2 * EXPERTS:3 * EXPERTS], one[:, 0:1], gate_over[:, 0, :], start=True, stop=False)
            nc.tensor.matmul(out[0:1, 2 * EXPERTS:3 * EXPERTS], one[:, 0:1], gate_over[:, 1, :], start=False, stop=True)\
                .then_inc(filled["place"], 1)

            for b in range(BANKS):
                st, n = last_in.pop(b)
                pe.wait_ge(emptied[st], n + 1)
            bank_x, bank_gu, banks_y, banks_out = ps[0], ps[1], ps[2:4], ps[4:8]

            def gather(half):
                for c in range(DC // 2):
                    for t in range(TT):
                        k = half * (DC // 2) + c
                        mm = nc.tensor.matmul(bank_x[:, c * 2 * SLOTS:(c + 1) * 2 * SLOTS], htok[:, t, k * P:(k + 1) * P],
                                              pick[:, t].rearrange("p j s -> p (j s)"), start=(t == 0), stop=(t == TT - 1))
                mm.then_inc(filled["slots_x"], 1)

            def gate_up(e, j):
                for n, stage in enumerate(("slots_gate", "slots_up")):
                    i = N0 + 3 * j + n
                    pe.wait_ge(landed[i % R], (e + (i // R + 1)) * 16)
                    for f in range(FC):
                        for k in range(DC):
                            mm = nc.tensor.matmul(bank_gu[:, (n * FC + f) * SLOTS:(n * FC + f + 1) * SLOTS], slot(i)[:, k, f * P:(f + 1) * P],
                                                  x_slots[:, k, j], start=(k == 0), stop=(k == DC - 1))
                    mm.then_inc(filled[stage], 1)

            def down(e, j):
                i = N0 + 3 * j + 2
                pe.wait_ge(landed[i % R], (e + (i // R + 1)) * 16)
                for half in range(2):
                    for f in range(FC):
                        mm = nc.tensor.matmul(banks_y[half][j * SLOTS:(j + 1) * SLOTS, :], hid_slots[:, f * SLOTS:(f + 1) * SLOTS],
                                              slot(i, FC)[:, f, half * BANK:(half + 1) * BANK], start=(f == 0), stop=(f == FC - 1))
                mm.then_inc(filled["slots_down"], 1)

            pe.wait_ge(zeroed, 1)
            for b in banks_out:
                nc.tensor.matmul(b[:], zrow[:, 0:P], zrow[:, P:P + BANK], start=True, stop=False)
            pe.wait_ge(emptied["htok"], 4)
            pe.wait_ge(pick_ready, 1)
            gather(0)
            pe.wait_ge(emptied["slots_x"], 1)
            gather(1)
            with pe.Fori(0, TURNS) as e:
                pe.wait_ge(emptied["slots_x"], e * 2 + 2)
                gate_up(e, 0)
                pe.wait_ge(pick_gate_ready, e + 1)
                for t in range(TT):
                    mm = nc.tensor.transpose(bank_x[:, t * P:(t + 1) * P], pick_gate[:, t].rearrange("p j s -> p (j s)"), ident)
                mm.then_inc(filled["slots_put"], 1)
                pe.wait_ge(emptied["slots_up"], e * 2 + 1)
                down(e, 0)
                gate_up(e, 1)
                pe.wait_ge(emptied["slots_put"], e + 1)
                pe.wait_ge(pick_ready, e + 2)
                gather(0)
                pe.wait_ge(emptied["slots_up"], e * 2 + 2)
                down(e, 1)
                pe.wait_ge(emptied["slots_x"], e * 2 + 3)
                gather(1)
                pe.wait_ge(emptied["slots_down"], e + 1)
                for c in range(DC):
                    nc.tensor.matmul(banks_out[c // 2][:, c % 2 * T:(c % 2 + 1) * T], y_slots[:, c * P:(c + 1) * P],
                                     put, start=False, stop=False)
            for b in banks_out:
                mm = nc.tensor.matmul(b[:], zrow[:, 0:P], zrow[:, P:P + BANK], start=False, stop=True)
            mm.then_inc(combined, 1)

        @block.scalar
        def _(act):
            step = Chain(act, act_steps)

            squares_and_root(act, "mix")
            for b in range(2):
                act.wait_ge(filled["cg"], b + 1)
                nc.scalar.activation(sig[:, b], bank("cg", b)[:], ACT.Sigmoid).then_inc(emptied["cg"], 1)
            for n, stage in enumerate(("q", "k")):
                for b in range(2):
                    act.wait_ge(filled[stage], b + 1)
                    if n == 1:
                        act.wait_ge(emptied["q"], b + 1)
                    src = bank(stage, b)
                    for g in range(4):
                        o = g ^ 1
                        step(nc.scalar.copy(rot[32 * g:32 * g + 32, b], src[32 * o:32 * o + 32, :]))
                    nc.scalar.copy(raw[:, b], src[:]).then_inc(rope_raw, 1)
            for t in range(TT):
                act.wait_ge(filled["v"], t + 1)
                nc.scalar.copy(v[:, t], bank("v", t)[:]).then_inc(emptied["v"], 1)
            for n, stage in enumerate(("ga", "gb")):
                for b in range(4):
                    act.wait_ge(filled[stage], b + 1)
                    nc.scalar.activation(gates_ab[:, n, 2 * b:2 * b + 2, :].rearrange("p c n -> p (c n)"),
                                         bank(stage, b)[:], ACT.Sigmoid).then_inc(emptied[stage], 1)
            for h in range(HEADS + 1):
                if h < HEADS:
                    act.wait_ge(smax_ready, h + 1)
                    if h >= 2:
                        act.wait_ge(filled["probT"], h - 1)
                    e, s = E[:, h % 2], S[:, h % 2]
                    nc.scalar.activation(e[:, 0:P], s[:, 0:P], ACT.Exp, bias=smax[:, h % 2, 0:1],
                                         accum_out=ssum[:, h % 2, 0:1]).then_inc(exps_ready, 1)
                    nc.scalar.activation(e[:, P:], s[:, P:], ACT.Exp, bias=smax[:, h % 2, 1:2],
                                         accum_out=ssum[:, h % 2, 1:2]).then_inc(exps_ready, 1)
                if h >= 1:
                    g = h - 1
                    act.wait_ge(filled["probT"], g + 1)
                    if g >= 2:
                        act.wait_ge(filled["o"], g - 1)
                    nc.scalar.copy(PT[:, g % 2], bank("probT", g)[:, 0:3 * P]).then_inc(emptied["probT"], 1)
                    if g % 2 and g >= 3:
                        c = g // 2 - 1
                        act.wait_ge(filled["o"], 2 * c + 2)
                        nc.scalar.copy(attn[:, c, :], bank("o", c)[:, 0:T]).then_inc(emptied["o"], 1)
            act.wait_ge(filled["o"], HEADS)
            nc.scalar.copy(attn[:, AC - 1, :], bank("o", AC - 1)[:, 0:T]).then_inc(emptied["o"], 1)
            act.wait_ge(filled["ln_var"], 1)
            nc.scalar.activation(stat[:], bank("ln_var")[:, 0:T], ACT.Sqrt, bias=eps[:, 0:1]).then_inc(emptied["ln_var"], 1)
            for c in range(CC):
                act.wait_ge(ln_done, c + 1)
                nc.scalar.activation(conv[:, c, :], conv[:, c, :], ACT.Silu, bias=param("ln_conv_b", c),
                                     scale=param("ln_conv_g", c)).then_inc(conv_act, 1)
            act.wait_ge(emptied["w_out"], 4)
            squares_and_root(act, "ffn")
            for b in range(4):
                act.wait_ge(filled["htok"], b + 1)
                nc.scalar.copy(htok[:, b // 2, b % 2 * BANK:(b % 2 + 1) * BANK], bank("htok", b)[:]).then_inc(emptied["htok"], 1)
            act.wait_ge(lmax_ready, 1)
            for t in range(TT):
                nc.scalar.activation(rt[:, t, 4:8], logit[:, t, 0:GROUPS], ACT.Exp, bias=rt[:, t, 0:1],
                                     accum_out=rt[:, t, 1:2]).then_inc(lexp_ready, 1)
            act.wait_ge(pair_ready, 1)
            nc.scalar.activation(rt[:, :, 21:22], rt[:, :, 20:21], ACT.Exp).then_inc(pexp_ready, 1)
            def slots_x(half):
                nc.scalar.copy(x_slots[:, half * 4:(half + 1) * 4].rearrange("p c j s -> p (c j s)"), ps[0][:])\
                    .then_inc(emptied["slots_x"], 1)

            def gate():
                nc.scalar.activation(silu_slots, ps[1][:, 0:FC * SLOTS], ACT.Silu).then_inc(silu_ready, 1)

            for half in range(2):
                act.wait_ge(filled["slots_x"], half + 1)
                slots_x(half)
            with act.Fori(0, TURNS) as e:
                act.wait_ge(filled["slots_up"], e * 2 + 1)
                gate()
                act.wait_ge(filled["slots_put"], e + 1)
                nc.scalar.copy(put, ps[0][:, 0:T]).then_inc(emptied["slots_put"], 1)
                act.wait_ge(filled["slots_up"], e * 2 + 2)
                gate()
                for half in range(2):
                    act.wait_ge(filled["slots_x"], e * 2 + (3 + half))
                    slots_x(half)

        @block.vector
        def _(dve):
            step = Chain(dve, dve_steps)
            vec = nc.vector

            step(vec.memset(u[:, :, 0:TAPS - 1], 0.0))
            step(vec.memset(one_row[:], 1.0))
            step(vec.memset(gate[:, :, EXPERTS:], 0.0))
            step(vec.memset(place[:, :, EXPERTS:], 0.0))
            dve.wait_ge(filled["params"], 1)
            vec.tensor_copy(par[:, 0:n_rows], bank("params")[:, 0:n_rows])
            vec.tensor_copy(par[:, TAP0:], bank("params")[:, TAP0:TAP0 + CC * TAPS]).then_inc(emptied["params"], 1)
            dve.wait_ge(emptied["params"], 1)
            step.settle()
            normalise(dve, step, "mix")
            for b in range(2):
                dve.wait_ge(emptied["cg"], b + 1)
                dve.wait_ge(filled["cu"], b + 1)
                vec.tensor_tensor(u[:, chunks(b), TAPS - 1:], bank("cu", b)[:].rearrange("p (c n) -> p c n", c=2),
                                  sig[:, b].rearrange("p (c n) -> p c n", c=2), ALU.mult).then_inc(emptied["cu"], 1)
            dve.wait_ge(emptied["cu"], 2)

            def taps(cs):
                for k in range(TAPS):
                    for c in cs:
                        x = u[:, c, k:k + T]
                        if k == 0:
                            step(vec.tensor_scalar(conv[:, c, :], x, tap(c, k), param("b_dw", c), ALU.mult, ALU.add))
                        elif k < TAPS - 1:
                            step(vec.scalar_tensor_tensor(conv[:, c, :], x, tap(c, k), conv[:, c, :], ALU.mult, ALU.add))
                        else:
                            vec.scalar_tensor_tensor(conv[:, c, :], x, tap(c, k), conv[:, c, :], ALU.mult, ALU.add).then_inc(conv_out, 1)
                    if k < TAPS - 1:
                        step.settle()

            def rope(n, stage):
                for b in range(2):
                    dve.wait_ge(rope_raw, 2 * n + b + 1)
                    three = "p (c n) -> p c n"
                    a, r = raw[:, b].rearrange(three, c=2), rot[:, b].rearrange(three, c=2)
                    step(vec.tensor_tensor(a, a, wide(const[:, C_COS:C_COS + T]), ALU.mult))
                    step(vec.tensor_tensor(r, r, wide(const[:, C_SIN:C_SIN + T]), ALU.mult))
                    step.settle()
                    vec.tensor_tensor(qk[:, n, chunks(b), :], a, r, ALU.add).then_inc(emptied[stage], 1)

            taps((0, 1))
            rope(0, "q")
            rope(1, "k")
            taps((2, 3))

            for h in range(HEADS + 1):
                if h < HEADS:
                    if h >= 2:
                        dve.wait_ge(exps_ready, 2 * (h - 1))
                    dve.wait_ge(filled["score"], h + 1)
                    s, m = S[:, h % 2], smax[:, h % 2]
                    vec.scalar_tensor_tensor(s, bank("score", h)[:, 0:3 * P], HD ** -0.5, const[:, C_MASK:C_MASK + 3 * P],
                                             ALU.mult, ALU.add).then_inc(emptied["score"], 1)
                    dve.wait_ge(emptied["score"], h + 1)
                    step(vec.tensor_reduce(m[:, 0:1], s[:, 0:P], AX_X, ALU.max))
                    step(vec.tensor_reduce(m[:, 1:2], s[:, P:], AX_X, ALU.max))
                    step.settle()
                    vec.tensor_scalar(m, m, -1.0, None, ALU.mult).then_inc(smax_ready, 1)
                if h >= 1:
                    g = (h - 1) % 2
                    dve.wait_ge(exps_ready, 2 * h)
                    step(vec.reciprocal(ssum[:, g], ssum[:, g]))
                    step.settle()
                    vec.tensor_scalar(E[:, g, 0:P], E[:, g, 0:P], ssum[:, g, 0:1], None, ALU.mult)
                    vec.tensor_scalar(E[:, g, P:], E[:, g, P:], ssum[:, g, 1:2], None, ALU.mult).then_inc(probs_ready, 1)

            dve.wait_ge(conv_out, CC)
            dve.wait_ge(filled["ln_mean"], 1)
            for c in range(CC):
                i = vec.tensor_tensor(conv[:, c, :], conv[:, c, :], bank("ln_mean")[:, 0:T], ALU.subtract)
                if c < CC - 1:
                    step(i)
            i.then_inc(emptied["ln_mean"], 1)
            dve.wait_ge(emptied["ln_mean"], 1)
            for c in range(CC):
                vec.tensor_tensor(sq[:, c, :], conv[:, c, :], conv[:, c, :], ALU.mult).then_inc(centred, 1)
            dve.wait_ge(emptied["ln_var"], 1)
            step(vec.reciprocal(rstd[:], stat[:]))
            step.settle()
            for c in range(CC):
                vec.tensor_tensor(conv[:, c, :], conv[:, c, :], rstd[:], ALU.mult).then_inc(ln_done, 1)
            dve.wait_ge(emptied["ga"], 4)
            dve.wait_ge(emptied["gb"], 4)
            for b in range(4):
                dve.wait_ge(filled["y_a"], b + 1)
                vec.tensor_tensor(flat(merged[:, chunks(b), :]), bank("y_a", b)[:], flat(gates_ab[:, 0, chunks(b), :]),
                                  ALU.mult).then_inc(emptied["y_a"], 1)
            dve.wait_ge(emptied["y_a"], 4)
            for b in range(4):
                dve.wait_ge(filled["y_b"], b + 1)
                for m in range(2):
                    c = 2 * b + m
                    step(vec.scalar_tensor_tensor(raw[:, b % 2, m * T:(m + 1) * T], bank("y_b", b)[:, m * T:(m + 1) * T],
                                                  param("b_conv_out", c), gates_ab[:, 1, c, :], ALU.add, ALU.mult))
                step.settle()
                vec.tensor_tensor(flat(merged[:, chunks(b), :]), flat(merged[:, chunks(b), :]), raw[:, b % 2],
                                  ALU.add).then_inc(emptied["y_b"], 1)

            def add_to_x(stage, b):
                dve.wait_ge(filled[stage], b + 1)
                x = flat(xT[:, chunks(b), :])
                vec.tensor_tensor(x, x, bank(stage, b)[:], ALU.add).then_inc(emptied[stage], 1)

            for b in range(4):
                add_to_x("w_out", b)
            dve.wait_ge(emptied["w_out"], 4)
            normalise(dve, step, "ffn")

            dve.wait_ge(filled["route"], 1)
            vec.tensor_copy(flat(logit[:]), bank("route")[:, 0:TT * ROUTES]).then_inc(emptied["route"], 1)
            step(vec.memset(rt[:, :, 8:16], -3.0e38))
            step.settle()
            dve.wait_ge(emptied["route"], 1)
            iota = const[:, C_IOTA:C_IOTA + 8]
            both = range(TT)

            def each(f):
                for t in both:
                    step(f(t))
                step.settle()

            step(vec.tensor_copy(rt[:, :, 8:8 + GROUPS], logit[:, :, 0:GROUPS]))
            step.settle()
            each(lambda t: vec.max(top[:, t, 0], rt[:, t, 8:16]))
            each(lambda t: vec.max_index(topi[:, t, 0], top[:, t, 0], rt[:, t, 8:16]))
            vec.tensor_scalar(rt[:, :, 0:1], top[:, :, 0, 0:1], -1.0, None, ALU.mult).then_inc(lmax_ready, 1)
            step(vec.tensor_copy(rt[:, :, 3:4], topi[:, :, 0, 0:1]))
            step.settle()
            each(lambda t: vec.tensor_scalar(rt[:, t, 24:24 + GROUPS], iota[:, 0:GROUPS], rt[:, t, 3:4], None, ALU.is_equal))
            for g in range(GROUPS):
                le = lambda t: logit[:, t, GROUPS + g * PER_GROUP:GROUPS + (g + 1) * PER_GROUP]
                if g == 0:
                    each(lambda t: vec.tensor_scalar(rt[:, t, 32:40], le(t), rt[:, t, 24:25], None, ALU.mult))
                else:
                    each(lambda t: vec.scalar_tensor_tensor(rt[:, t, 32:40], le(t), rt[:, t, 24 + g:25 + g], rt[:, t, 32:40],
                                                            ALU.mult, ALU.add))
            each(lambda t: vec.max(top[:, t, 1], rt[:, t, 32:40]))
            each(lambda t: vec.max_index(topi[:, t, 1], top[:, t, 1], rt[:, t, 32:40]))
            vec.tensor_tensor(rt[:, :, 20:21], top[:, :, 1, 1:2], top[:, :, 1, 0:1], ALU.subtract).then_inc(pair_ready, 1)
            step(vec.tensor_copy(rt[:, :, 28:30], topi[:, :, 1, 0:2]))
            dve.wait_ge(lexp_ready, TT)
            step(vec.reciprocal(rt[:, :, 2:3], rt[:, :, 1:2]))
            dve.wait_ge(pexp_ready, 1)
            step(vec.tensor_scalar(rt[:, :, 22:23], rt[:, :, 21:22], 1.0, None, ALU.add))
            step.settle()
            step(vec.reciprocal(rt[:, :, 23:24], rt[:, :, 22:23]))
            step.settle()
            step(vec.tensor_tensor(rt[:, :, 30:31], rt[:, :, 23:24], rt[:, :, 2:3], ALU.mult))
            step.settle()
            step(vec.tensor_tensor(rt[:, :, 31:32], rt[:, :, 30:31], rt[:, :, 21:22], ALU.mult))
            step.settle()
            each(lambda t: vec.tensor_scalar(rt[:, t, 40:48], iota, rt[:, t, 28:29], rt[:, t, 30:31], ALU.is_equal, ALU.mult))
            each(lambda t: vec.tensor_scalar(rt[:, t, 48:56], iota, rt[:, t, 29:30], rt[:, t, 31:32], ALU.is_equal, ALU.mult))
            step(vec.tensor_tensor(rt[:, :, 40:48], rt[:, :, 40:48], rt[:, :, 48:56], ALU.add))
            step.settle()
            for g in range(GROUPS):
                for t in both:
                    step(vec.tensor_scalar(gate[:, t, g * PER_GROUP:(g + 1) * PER_GROUP], rt[:, t, 40:48],
                                           rt[:, t, 24 + g:25 + g], None, ALU.mult))
            vec.memset(zrow, 0.0).then_inc(zeroed, 1)
            step.settle()
            own, placed = gate[:, :, 0:EXPERTS], place[:, :, 0:EXPERTS]
            vec.tensor_scalar(gate_over[:], own, 0.0, None, ALU.is_gt).then_inc(mask_ready, 1)
            dve.wait_ge(mask_ready, 1)
            dve.wait_ge(filled["place"], 1)
            upto = bank("place")[:, 0:TT * EXPERTS].rearrange("p (t e) -> p t e", t=TT)
            step(vec.tensor_tensor(placed, upto, gate_over[:], ALU.mult))
            step(vec.tensor_reduce(top[0:1, 0, 0, 0:1], bank("place")[0:1, 2 * EXPERTS:3 * EXPERTS], AX_X, ALU.max))
            step.settle()
            vec.tensor_copy(most[:], top[0:1, 0, 0, 0:1]).then_inc(emptied["place"], 1)
            step(vec.scalar_tensor_tensor(gate_over[:], placed, float(SLOTS), own, ALU.is_gt, ALU.mult))
            step.settle()

            ids = const[:, C_SLOT:C_SLOT + SLOTS].unsqueeze(1).unsqueeze(1).broadcast_to([P, TT, 2, SLOTS])

            def pair(x, at):
                return x[:, :, at].unsqueeze(3).broadcast_to([P, TT, 2, SLOTS])

            vec.tensor_tensor(pick, ids, pair(place, slice(0, 2)), ALU.is_equal).then_inc(pick_ready, 1)
            dve.wait_ge(pick_ready, 1)
            vec.tensor_tensor(pick_gate, pick, pair(gate, slice(0, 2)), ALU.mult).then_inc(pick_gate_ready, 1)

            def hidden():
                vec.tensor_tensor(hid_slots, ps[1][:, FC * SLOTS:2 * FC * SLOTS], silu_slots, ALU.mult).then_inc(emptied["slots_up"], 1)

            with dve.Fori(0, TURNS) as e:
                dve.wait_ge(silu_ready, e * 2 + 1)
                hidden()
                dve.wait_ge(filled["slots_x"], e * 2 + 2)
                dve.wait_ge(filled["slots_put"], e + 1)
                vec.tensor_tensor(pick, ids, pair(place, bass.ds(e * 2 + 2, 2)), ALU.is_equal).then_inc(pick_ready, 1)
                dve.wait_ge(pick_ready, e + 2)
                vec.tensor_tensor(pick_gate, pick, pair(gate, bass.ds(e * 2 + 2, 2)), ALU.mult).then_inc(pick_gate_ready, 1)
                dve.wait_ge(silu_ready, e * 2 + 2)
                hidden()
                dve.wait_ge(filled["slots_down"], e * 2 + 2)
                step(vec.tensor_copy(y_slots[:, 0:BANK], ps[2][:]))
                vec.tensor_copy(y_slots[:, BANK:], ps[3][:]).then_inc(emptied["slots_down"], 1)
            dve.wait_ge(combined, 1)
            for b in range(4):
                x = flat(xT[:, chunks(b), :])
                vec.tensor_tensor(x, x, ps[4 + b][:], ALU.add)

    clear(nc, sems)
    count = nc.values_load(most[0:1, 0:1], min_val=0, max_val=T)
    with nc.If(count > SLOTS):
        over_block()
    nc.end_ifs()
    clear(nc, sems)
    ple_block()
    return sems
    return sems


def second_block(nc, ctx, dram, const, keep, bias_rows, out):
    R = 3

    def sb(name, shape, dt=F32):
        return ctx.enter_context(nc.sbuf_tensor("b_" + name, shape, dt))

    sems = []

    def sem(name):
        sems.append(ctx.enter_context(nc.semaphore("b_" + name)))
        return sems[-1]

    xT, hT, sq, eps, ones, ps = (keep[k] for k in ("xT", "hT", "sq", "eps", "ones", "ps"))
    ident = const[:, C_ID:C_ID + P]
    ring = sb("ring", [P, R, 4096])
    rows = sb("rows", [64, P])
    rrows = sb("rrows", [8 * RC, RP])
    par = sb("par", [P, 64 + 8 * RC])
    w2k = sb("w2k", [P, 2, P])
    w2v = sb("w2v", [P, 2, HD])
    rel = sb("rel", [BUCKETS + 1, H2])
    sp_ = sb("softplus", [P, 8, RC])
    region_x = sb("region_x", [P, 3108])
    region_c = sb("region_c", [P, 3072])
    region_r = sb("region_r", [P, 6144])
    region_g = sb("region_g", [P, 3072])
    tmp = sb("tmp", [P, RB, T])
    gates_ab = sb("gates_ab", [P, 2, DC, T])
    qn = sb("qn", [P, DC, T])
    kn = sb("kn", [P, 2, KVG, T])
    vn = sb("vn", [P, 2, TT, KVW])
    gn = sb("gn", [P, TT, 3 * H2])
    stat = sb("stat", [P, 2, BANK])
    rstd = sb("rstd", [P, BANK])
    soft = sb("soft", [P, 3, 2, 3 * P])
    S, E, PT = soft[:, 0], soft[:, 1], soft[:, 2]
    ksq = soft[:].rearrange("p a b n -> p (a b n)")
    smax = sb("smax", [P, 2, 2])
    ssum = sb("ssum", [P, 2, 2])
    cbias = sb("cbias", [P, TT, H2, NCMP])
    sc = sb("sc", [P, TT, H2, NCMP])
    cm = sb("cm", [P, 2, TT, H2])
    hid_c = sb("hid_c", [P, 2, 2, KVG * NCMP])
    kcd = sb("kcd", [P, KVG * NCMP])
    merged = sq
    three = "p (c n) -> p c n"

    u_pad = region_x[0:RP, 0:RC * (T + RTAPS - 1)].rearrange(three, c=RC)
    tau = region_x[0:RP, 0:RC * T].rearrange(three, c=RC)
    xc = region_c[0:RP, 0:RC * T].rearrange(three, c=RC)
    ra = region_r[0:RP, 0:RC * T].rearrange(three, c=RC)
    ix = region_r[0:RP, RC * T:2 * RC * T].rearrange(three, c=RC)
    gel = region_g[0:RP, :].rearrange(three, c=RC)
    near = region_r[0:BUCKETS + 1, 0:TT * NCMP * P]
    far = region_r[0:BUCKETS + 1, 4096:4096 + 2 * T]
    er = region_r[0:H2, 5120:5120 + 2 * T]
    bias3 = region_r[:, 0:H2 * 3 * P].rearrange("p (h n) -> p h n", h=H2)
    Z = [region_x[:, 512 * n:512 * n + 512].rearrange("p (g n) -> p g n", g=KVG) for n in range(2)]
    NB = KVG * NCMP
    ZB = [region_x[:, 1024 + 960 * n:1024 + 960 * n + 16 * NB].rearrange("p (j g c) -> p j g c", j=16, g=KVG) for n in range(2)]
    pc = region_c[:, 0:1024].rearrange("p (t h c) -> p t h c", t=TT, h=H2)
    pcT = region_c[:, 1024:2048].rearrange("p (g n) -> p g n", g=KVG)
    vcz = region_c[:, 2048:3072].rearrange("p (g r n) -> p g r n", g=KVG, r=HPG)
    attn = region_g[:, 0:DC * T].rearrange(three, c=DC)

    def hidden(c, n=1):
        reg = (region_x, region_c, region_g)[c // 12]
        return reg[:, c % 12 * T:(c % 12 + n) * T]

    def head_squares(name, b):
        if name == "q":
            return sq[:, 2 * b:2 * b + 2, :].rearrange("p c n -> p (c n)")
        if name == "kc":
            return sc[:, 0].rearrange("p h c -> p (h c)")[:, 0:NB]
        n = ("ks", "kw").index(name)
        return ksq[:, (2 * n + b) * BANK:(2 * n + b + 1) * BANK]

    outtok = hT[:].rearrange("p (t c) n -> p t (c n)", t=TT)

    col, at = {}, 0
    for n, k in (("norm_final", DC), ("norm_mix_2", DC), ("norm_mlp_2", DC), ("phi_k_pe_2", 16), ("phi_v_pe_2", 16),
                 ("q_norm_2", 1), ("kc_norm_2", 1), ("ks_norm_2", 1), ("kw_norm_2", 1)):
        col[n] = at
        at += k
    n_rows = at
    rcol, at = {}, 0
    for n, k in (("conv_w_2", RTAPS * RC), ("conv_b_2", RC), ("gate_a_b_2", RC), ("gate_x_b_2", RC), ("lru_lambda_2", RC)):
        rcol[n] = at
        at += k
    assert n_rows <= 64 and at == 8 * RC

    def param(name, c=0):
        return par[:, col[name] + c:col[name] + c + 1]

    def rparam(name, c, n=1):
        return par[0:RP, 64 + rcol[name] + c:64 + rcol[name] + c + n]

    stages = dict(params=1, far=1, near=TT, mean_final=1, mean_mix=1, u_rnn=RC // 2, u_gate=RC // 2, lru_r=RC // 2,
                  lru_i=RC // 2, ga=4, gb=4, gn=1, q=4, ks=2, vs=1, mean_q=4, kw=2, vw=1, mean_ks=2, kc=1, vc=1,
                  mean_kw=2, y_a=4, hid_k=1, hid_v=1, kc2=1, vc2=1, mean_kc=1, scorec=2 * TT, pcT=2,
                  score=2 * H2, probT=2 * H2, o=H2 // 2, y_b=4, w_out=4, mean_mlp=1, mlp_in=16, mlp_out=4)
    banks, n = {}, 0
    for stage, count in stages.items():
        for i in range(count):
            if stage in ("score", "probT", "o"):
                banks[stage, i] = {"score": i % 3, "probT": 3 + i % 3, "o": 6 + i % 2}[stage]
            else:
                banks[stage, i] = n % BANKS
                n += 1

    def bank(stage, i=0):
        return ps[banks[stage, i]]

    filled = {s: sem("filled_" + s) for s in stages}
    emptied = {s: sem("emptied_" + s) for s in stages}
    landed = [sem(f"landed{i}") for i in range(R)]
    params_in, phi_in, er_out, bias_in, stored = (sem(n) for n in ("params_in", "phi_in", "er_out", "bias_in", "stored"))
    dve_steps, act_steps = sem("dve_steps"), sem("act_steps")
    squares = {n: sem("squares_" + n) for n in ("final", "mix", "mlp", "q", "ks", "kw", "kc")}
    normed = {n: sem("normed_" + n) for n in ("final", "mix", "mlp", "q", "ks", "kw", "kc")}
    (conv_ready, lam_exp, rates, taus, decays, ratios, mults, y_ready, zb_ready, cshift, root_read,
     cexp, pc_ready, smax_ready, exps_ready, probs_ready, squared) = (sem(n) for n in (
         "conv_ready", "lam_exp", "rates", "taus", "decays", "ratios", "mults", "y_ready", "zb_ready", "cshift", "root_read",
         "cexp", "pc_ready", "smax_ready", "exps_ready", "probs_ready", "squared"))

    def w_cols(name, c0, n=BANK, part=P):
        return dram[name][0, :, c0:c0 + n].rearrange("(c p) n -> p c n", p=part)

    stream = []
    for i in range(3):
        stream.append((w_cols("w_in_2", IN2["u_rnn"] + 4 * RP * i, 4 * RP), "u_rnn", 2 * i + 2))
    for i in range(3):
        stream.append((w_cols("w_in_2", IN2["u_gate"] + 4 * RP * i, 4 * RP), "u_gate", 2 * i + 2))
    for name, stage in (("gate_a_w_2", "lru_r"), ("gate_x_w_2", "lru_i")):
        stream.append((dram[name][0].rearrange("n (c p) m -> p (n c) m", p=RP), stage, RC // 2))
    for name in ("a", "b"):
        for i in range(2):
            stream.append((w_cols("w_in_2", IN2["g_" + name] + BANK * i), "g" + name, 2 * i + 2))
    stream.append((w_cols("w_in_2", IN2["g_nsa"], 3 * H2), "gn", 1))
    for i in range(2):
        stream.append((w_cols("w_in_2", IN2["q"] + BANK * i), "q", 2 * i + 2))
    for name in ("s", "w", "c"):
        stream.append((w_cols("w_in_2", IN2["k" + name]), "v" + name, 1))
    for i in range(4):
        stream.append((w_cols("proj_a_2", 2 * P * i, 2 * P, RP), "y_a", i + 1))
    for name, stage in (("phi_k_w1_2", "hid_k"), ("phi_v_w1_2", "hid_v")):
        stream.append((dram[name][0].rearrange("(c p) n -> p c n", p=P), stage, 1))
    for name, stage in (("proj_b_2", "y_b"), ("w_out_2", "w_out")):
        for i in range(2):
            stream.append((w_cols(name, BANK * i), stage, 2 * i + 2))
    for i in range(8):
        stream.append((w_cols("w_mlp_in_2", BANK * i), "mlp_in", 2 * i + 2))
    for i in range(8):
        stream.append((dram["w_mlp_out_2"][0, BANK * i:BANK * (i + 1)].rearrange("(c p) n -> p c n", p=P), "mlp_out", 4))
    S_OF, at = {}, 0
    for i, (_, stage, _) in enumerate(stream):
        S_OF.setdefault(stage, i)
    mlp_slots = sem("mlp_slots")

    def slot(i):
        p, c, n = stream[i][0].shape
        return ring[0:p, i % R, 0:c * n].rearrange(three, c=c)

    with nc.Block(no_gpsimd_drain=True) as block:

        @block.sync
        def _(sp):
            def small(dst, src):
                sp.dma_start(dst, src).then_inc(params_in, 16)

            small(rows[0:DC, :], dram["norm_final"].rearrange("(c p) -> c p", p=P))
            for n in ("norm_mix_2", "norm_mlp_2"):
                small(rows[col[n]:col[n] + DC, :], dram[n][0].rearrange("(c p) -> c p", p=P))
            for n in ("phi_k_pe_2", "phi_v_pe_2"):
                small(rows[col[n]:col[n] + 16, :], dram[n][0].rearrange("(j k) d -> j (k d)", k=2))
            for n in ("q_norm_2", "kc_norm_2", "ks_norm_2", "kw_norm_2"):
                for h in range(2):
                    small(rows[col[n]:col[n] + 1, HD * h:HD * h + HD], dram[n])
            small(rrows[0:RTAPS * RC, :], dram["conv_w_2"][0].rearrange("k (c p) -> (k c) p", p=RP))
            for n in ("conv_b_2", "lru_lambda_2"):
                small(rrows[rcol[n]:rcol[n] + RC, :], dram[n][0].rearrange("(c p) -> c p", p=RP))
            for n in ("gate_a_b_2", "gate_x_b_2"):
                small(rrows[rcol[n]:rcol[n] + RC, :], dram[n][0].rearrange("n (c p) -> (n c) p", p=RP))
            small(rel[0:BUCKETS, :], dram["rel_bias_2"])
            small(rel[BUCKETS:BUCKETS + 1, :], dram["off"])
            small(far, dram["far"])
            small(near, dram["near"])
            N_PARAMS = 3 + 2 + 8 + 1 + 2 + 2 + 4
            for h in range(2):
                sp.dma_start(w2k[:, :, HD * h:HD * h + HD], dram["phi_k_w2_2"][0].rearrange("(c p) n -> p c n", p=P)).then_inc(phi_in, 16)
            sp.dma_start(w2v[:], dram["phi_v_w2_2"][0].rearrange("(c p) n -> p c n", p=P)).then_inc(phi_in, 16)
            assert N_PARAMS == 22
            for i, (src, stage, n) in enumerate(stream):
                if i == R:
                    sp.wait_ge(emptied["far"], 1)
                    sp.dma_start(bias_rows[:, :, 0:2 * T], er.unsqueeze(1).broadcast_to([H2, P, 2 * T])).then_inc(er_out, 16)
                if i >= R:
                    _, before, m = stream[i - R]
                    if before == "mlp_out":
                        sp.wait_ge(mlp_slots, i - R - S_OF["mlp_out"] + 1)
                    else:
                        sp.wait_ge(filled[before], m)
                sp.dma_start(slot(i), src).then_inc(landed[i % R], 16)
                if i == S_OF["y_a"] + 2:
                    sp.wait_ge(er_out, 16)
                    sp.wait_ge(y_ready, RBLOCKS)
                    for c0, d0, k in ((0, 0, P), (P, P, 2 * P)):
                        src = bass.AP(bias_rows.tensor, T - 1 - d0, [[2 * T, P], [P * SKEW, H2], [1, k]])
                        sp.dma_start(bias3[:, :, c0:c0 + k], src).then_inc(bias_in, 16)
            for b in range(4):
                sp.wait_ge(emptied["mlp_out"], b + 1)
                t, half = b // 2, b % 2
                sp.dma_start(out[0, t * P:(t + 1) * P, half * BANK:(half + 1) * BANK],
                             outtok[:, t, half * BANK:(half + 1) * BANK]).then_inc(stored, 16)
            sp.wait_ge(stored, 64)

        @block.tensor
        def _(pe):
            last_in = {}

            def claim(stage, i):
                b = banks[stage, i]
                if b in last_in:
                    s, n = last_in[b]
                    pe.wait_ge(emptied[s], n + 1)
                last_in[b] = (stage, i)
                return ps[b]

            def weights(i):
                pe.wait_ge(landed[i % R], 16 * (i // R + 1))
                return slot(i)

            def mean(stage, ready):
                out = claim(stage, 0)
                for c in range(DC):
                    if c % 4 == 0:
                        pe.wait_ge(ready, c // 4 + 1)
                    mm = nc.tensor.matmul(out[:, 0:T], ones["D"][:], sq[:, c, :], start=(c == 0), stop=(c == DC - 1))
                mm.then_inc(filled[stage], 1)

            def head_means(name, b):
                out = claim("mean_" + name, b)
                pe.wait_ge(squares[name], b + 1)
                x = head_squares(name, b)
                nc.tensor.matmul(out[:, 0:x.shape[1]], const[:, C_HEAD:C_HEAD + P], x, start=True, stop=True).then_inc(filled["mean_" + name], 1)

            def project(i, stage, n0, src, cols=4, width=P):
                w = weights(i)
                kc = w.shape[1]
                for b in range(cols // 2):
                    out = claim(stage, n0 + b)
                    for m in range(2):
                        for k in range(kc):
                            c = 2 * b + m
                            mm = nc.tensor.matmul(out[0:width, m * T:(m + 1) * T], w[:, k, c * width:(c + 1) * width],
                                                  src(k), start=(k == 0), stop=(k == kc - 1))
                    mm.then_inc(filled[stage], 1)

            h = lambda k: hT[:, k, :]
            pe.wait_ge(params_in, 16 * 22)
            out = claim("params", 0)
            nc.tensor.transpose(out[:, 0:n_rows], rows[0:n_rows, :], ident[0:n_rows, 0:n_rows])
            nc.tensor.transpose(out[0:RP, 64:64 + 8 * RC], rrows[:], ident[0:8 * RC, 0:8 * RC]).then_inc(filled["params"], 1)
            nc.tensor.matmul(claim("far", 0)[0:H2, :], rel[:], far, start=True, stop=True).then_inc(filled["far"], 1)
            for t in range(TT):
                out = claim("near", t)
                for c in range(NCMP):
                    i = t * NCMP + c
                    mm = nc.tensor.matmul(out[:, c * H2:(c + 1) * H2], near[:, i * P:(i + 1) * P], rel[:], start=True, stop=True)
                mm.then_inc(filled["near"], 1)
            mean("mean_final", squares["final"])
            mean("mean_mix", squares["mix"])
            pe.wait_ge(normed["mix"], DC)
            for n, stage in enumerate(("u_rnn", "u_gate")):
                for i in range(3):
                    project(3 * n + i, stage, 2 * i, h, width=RP)
            pe.wait_ge(conv_ready, RC)
            for n, stage in enumerate(("lru_r", "lru_i")):
                w = weights(S_OF[stage])
                for b in range(RC // 2):
                    out = claim(stage, b)
                    for m in range(2):
                        c = 2 * b + m
                        for k in range(RB):
                            i = c // RB * RB + k
                            mm = nc.tensor.matmul(out[0:RP, m * T:(m + 1) * T], w[:, i, c % RB * RP:(c % RB + 1) * RP],
                                                  xc[:, i, :], start=(k == 0), stop=(k == RB - 1))
                    mm.then_inc(filled[stage], 1)
            for stage in ("ga", "gb"):
                for i in range(2):
                    project(S_OF[stage] + i, stage, 2 * i, h)
            w = weights(S_OF["gn"])
            out = claim("gn", 0)
            for t in range(TT):
                for k in range(DC):
                    mm = nc.tensor.matmul(out[:, t * 3 * H2:(t + 1) * 3 * H2], hT[:, k, t * P:(t + 1) * P], w[:, k, :],
                                          start=(k == 0), stop=(k == DC - 1))
            mm.then_inc(filled["gn"], 1)
            for i in range(2):
                project(S_OF["q"] + i, "q", 2 * i, h)

            def keys_values(name):
                w = weights(S_OF["v" + name])
                for b in range(2):
                    out = claim("k" + name, b)
                    for m in range(2):
                        g = 2 * b + m
                        for half in range(2):
                            for k in range(DC):
                                mm = nc.tensor.matmul(out[HD * half:HD * half + HD, m * T:(m + 1) * T], w[:, k, g * HD:(g + 1) * HD],
                                                      h(k), start=(k == 0), stop=(k == DC - 1))
                    mm.then_inc(filled["k" + name], 1)
                out = claim("v" + name, 0)
                for t in range(TT):
                    for k in range(DC):
                        mm = nc.tensor.matmul(out[:, t * KVW:(t + 1) * KVW], hT[:, k, t * P:(t + 1) * P], w[:, k, KVW:2 * KVW],
                                              start=(k == 0), stop=(k == DC - 1))
                mm.then_inc(filled["v" + name], 1)

            keys_values("s")
            for b in range(4):
                head_means("q", b)
            keys_values("w")
            for b in range(2):
                head_means("ks", b)
            w = weights(S_OF["vc"])
            for n, stage in enumerate(("kc", "vc")):
                out = claim(stage, 0)
                for m in range(2):
                    for k in range(DC):
                        c = 2 * n + m
                        mm = nc.tensor.matmul(out[:, m * T:(m + 1) * T], w[:, k, c * P:(c + 1) * P], h(k),
                                              start=(k == 0), stop=(k == DC - 1))
                mm.then_inc(filled[stage], 1)
            for b in range(2):
                head_means("kw", b)
            pe.wait_ge(y_ready, RBLOCKS)
            for i in range(4):
                project(S_OF["y_a"] + i, "y_a", i, lambda k: gel[:, k, :], cols=2)
            pe.wait_ge(phi_in, 48)
            for n, stage in enumerate(("hid_k", "hid_v")):
                w = weights(S_OF[stage])
                pe.wait_ge(zb_ready, KVG * (n + 1))
                out = claim(stage, 0)
                for f in range(2):
                    for j in range(16):
                        mm = nc.tensor.matmul(out[:, f * NB:(f + 1) * NB], w[:, j, f * P:(f + 1) * P],
                                              ZB[n][:, j].rearrange("p g c -> p (g c)"), start=(j == 0), stop=(j == 15))
                mm.then_inc(filled[stage], 1)
            pe.wait_ge(emptied["hid_k"], 1)
            out = claim("kc2", 0)
            for f in range(2):
                mm = nc.tensor.matmul(out[:, 0:NB], w2k[:, f, :], hid_c[:, 0, f, :], start=(f == 0), stop=(f == 1))
            mm.then_inc(filled["kc2"], 1)
            pe.wait_ge(emptied["hid_v"], 1)
            out = claim("vc2", 0)
            for r in range(HPG):
                for g in range(KVG):
                    for f in range(2):
                        mm = nc.tensor.matmul(out[32 * r:32 * r + NCMP, g * HD:(g + 1) * HD], hid_c[:, 1, f, g * NCMP:(g + 1) * NCMP],
                                              w2v[:, f, :], start=(f == 0), stop=(f == 1))
            mm.then_inc(filled["vc2"], 1)
            head_means("kc", 0)
            pe.wait_ge(normed["q"], 4)
            pe.wait_ge(normed["kc"], 1)
            for t in range(TT):
                for odd in range(2):
                    out = claim("scorec", 2 * t + odd)
                    r = slice(HD * odd, HD * odd + HD)
                    for n in range(H2 // 2):
                        g = 2 * n // HPG
                        mm = nc.tensor.matmul(out[:, n * NCMP:(n + 1) * NCMP], qn[r, n, t * P:(t + 1) * P],
                                              kcd[r, g * NCMP:(g + 1) * NCMP], start=True, stop=True)
                    mm.then_inc(filled["scorec"], 1)
            pe.wait_ge(pc_ready, TT)
            for b in range(2):
                out = claim("pcT", b)
                for m in range(2):
                    for t in range(TT):
                        g = 2 * b + m
                        mm = nc.tensor.transpose(out[:, m * T + t * P:m * T + (t + 1) * P],
                                                 pc[:, t, g * HPG:(g + 1) * HPG, :].rearrange("p h c -> p (h c)"), ident)
                mm.then_inc(filled["pcT"], 1)
            pe.wait_ge(normed["ks"], 2)
            pe.wait_ge(normed["kw"], 2)
            pe.wait_ge(emptied["vs"], 1)
            pe.wait_ge(emptied["vw"], 1)
            pe.wait_ge(emptied["pcT"], 2)
            pe.wait_ge(emptied["vc2"], 1)

            def score(i):
                hd, n = i // 2, i % 2
                out = claim("score", i)
                r = slice(HD * (hd % 2), HD * (hd % 2) + HD)
                q, k = qn[r, hd // 2, :], kn[r, n, hd // HPG, :]
                nc.tensor.matmul(out[:, 0:P], q[:, 0:P], k[:, 0:P], start=True, stop=True)
                nc.tensor.matmul(out[:, P:3 * P], q[:, P:T], k, start=True, stop=True).then_inc(filled["score"], 1)

            def prob_t(i):
                out = claim("probT", i)
                pe.wait_ge(probs_ready, i + 1)
                e = E[:, i % 2]
                nc.tensor.transpose(out[:, 0:P], e[:, 0:P], ident)
                nc.tensor.transpose(out[:, P:T], e[:, P:T], ident)
                nc.tensor.transpose(out[:, T:3 * P], e[:, T:3 * P], ident).then_inc(filled["probT"], 1)

            def values(i):
                hd, n = i // 2, i % 2
                g = hd // HPG
                if i % 4 == 0:
                    claim("o", i // 4)
                out = bank("o", hd // 2)[HD * (hd % 2):HD * (hd % 2) + HD, 0:T]
                if n == 0:
                    nc.tensor.matmul(out, vcz[:, g, hd % HPG, :], pcT[:, g, :], start=True, stop=False)
                pe.wait_ge(emptied["probT"], i + 1)
                pt = PT[:, i % 2]
                nc.tensor.matmul(out, vn[:, n, 0, g * HD:(g + 1) * HD], pt[:, 0:T], start=False, stop=False)
                nc.tensor.matmul(out[:, P:T], vn[:, n, 1, g * HD:(g + 1) * HD], pt[:, T:3 * P], start=False, stop=(n == 1))\
                    .then_inc(filled["o"], 1)

            N = 2 * H2
            for i in range(N + 3):
                if i < N:
                    score(i)
                if 2 <= i < N + 2:
                    prob_t(i - 2)
                if i >= 3:
                    values(i - 3)
            pe.wait_ge(emptied["o"], H2 // 2)
            for i in range(2):
                project(S_OF["y_b"] + i, "y_b", 2 * i, lambda k: attn[:, k, :])
            pe.wait_ge(emptied["y_b"], 4)
            for i in range(2):
                project(S_OF["w_out"] + i, "w_out", 2 * i, lambda k: merged[:, k, :])
            mean("mean_mlp", squares["mlp"])
            pe.wait_ge(normed["mlp"], DC)
            for i in range(8):
                project(S_OF["mlp_in"] + i, "mlp_in", 2 * i, h)
            outs = [claim("mlp_out", b) for b in range(4)]
            for s in range(8):
                w = weights(S_OF["mlp_out"] + s)
                pe.wait_ge(squared, 2 * s + 2)
                for k in range(4):
                    for b in range(4):
                        t, half = b // 2, b % 2
                        mm = nc.tensor.matmul(outs[b][:], hidden(4 * s + k)[:, t * P:(t + 1) * P], w[:, k, half * BANK:(half + 1) * BANK],
                                              start=(s == 0 and k == 0), stop=False)
                mm.then_inc(mlp_slots, 1)
            for b in range(4):
                t, half = b // 2, b % 2
                for c in range(4):
                    mm = nc.tensor.matmul(outs[b][:, c * P:(c + 1) * P], xT[:, 4 * half + c, t * P:(t + 1) * P], ident,
                                          start=False, stop=(c == 3))
                mm.then_inc(filled["mlp_out"], 1)

        @block.scalar
        def _(act):
            step = Chain(act, act_steps)
            sc_act = nc.scalar.activation

            def norm(name):
                for h in range(2):
                    sc_act(sq[:, 4 * h:4 * h + 4, :], xT[:, 4 * h:4 * h + 4, :], ACT.Square).then_inc(squares[name], 1)
                act.wait_ge(filled["mean_" + name], 1)
                sc_act(stat[:, 0, 0:T], bank("mean_" + name)[:, 0:T], ACT.Sqrt, bias=eps[:, 0:1]).then_inc(emptied["mean_" + name], 1)

            act.wait_ge(filled["far"], 1)
            nc.scalar.copy(er, bank("far")[0:H2, :]).then_inc(emptied["far"], 1)
            norm("final")
            act.wait_ge(normed["final"], DC)
            norm("mix")
            act.wait_ge(emptied["params"], 1)
            step(sc_act(sp_[0:RP, 0], rparam("lru_lambda_2", 0, RC), ACT.Abs))
            step.settle()
            sc_act(sp_[0:RP, 1], sp_[0:RP, 0], ACT.Exp, scale=-1.0).then_inc(lam_exp, 1)
            for b in range(RC // 2):
                act.wait_ge(filled["u_rnn"], b + 1)
                nc.scalar.copy(u_pad[:, 2 * b:2 * b + 2, RTAPS - 1:], bank("u_rnn", b)[0:RP].rearrange(three, c=2)).then_inc(emptied["u_rnn"], 1)
            for b in range(RC // 2):
                act.wait_ge(filled["u_gate"], b + 1)
                sc_act(gel[:, 2 * b:2 * b + 2, :].rearrange("p c n -> p (c n)"), bank("u_gate", b)[0:RP], ACT.Gelu_apprx_tanh).then_inc(emptied["u_gate"], 1)
            act.wait_ge(er_out, 16)
            for stage, dst, name in (("lru_r", ra, "gate_a_b_2"), ("lru_i", ix, "gate_x_b_2")):
                for b in range(RC // 2):
                    act.wait_ge(filled[stage], b + 1)
                    step(sc_act(dst[:, 2 * b, :], bank(stage, b)[0:RP, 0:T], ACT.Sigmoid, bias=rparam(name, 2 * b)))
                    sc_act(dst[:, 2 * b + 1, :], bank(stage, b)[0:RP, T:2 * T], ACT.Sigmoid, bias=rparam(name, 2 * b + 1)).then_inc(emptied[stage], 1)
            act.wait_ge(rates, 1)
            act.wait_ge(emptied["lru_r"], RC // 2)
            for c in range(RC):
                sc_act(tau[:, c, :], ra[:, c, :], ACT.Tanh, scale=sp_[0:RP, 6, c:c + 1]).then_inc(taus, 1)
            for c in range(RC):
                sc_act(ra[:, c, :], ra[:, c, :], ACT.Exp, scale=sp_[0:RP, 7, c:c + 1]).then_inc(decays, 1)
            for n, stage in enumerate(("ga", "gb")):
                for b in range(4):
                    act.wait_ge(filled[stage], b + 1)
                    sc_act(gates_ab[:, n, 2 * b:2 * b + 2, :].rearrange("p c n -> p (c n)"), bank(stage, b)[:], ACT.Sigmoid).then_inc(emptied[stage], 1)
            act.wait_ge(filled["gn"], 1)
            sc_act(gn[:].rearrange("p t n -> p (t n)"), bank("gn")[:, 0:TT * 3 * H2], ACT.Sigmoid).then_inc(emptied["gn"], 1)
            act.wait_ge(ratios, RBLOCKS)
            sc_act(tau.rearrange("p c n -> p (c n)"), tau.rearrange("p c n -> p (c n)"), ACT.Sqrt, scale=2.0).then_inc(mults, 1)

            flat = lambda x: x.rearrange("p c n -> p (c n)")
            n_roots = [0]

            def heads(name, dst, b):
                act.wait_ge(filled[name], b + 1)
                src = bank(name, b)[:, 0:dst.shape[1]]
                sc_act(head_squares(name[:2] if name != "kc2" else "kc", b), src, ACT.Square).then_inc(squares[name if name != "kc2" else "kc"], 1)
                nc.scalar.copy(dst, src).then_inc(emptied[name], 1)

            def roots(name, b, n=BANK):
                act.wait_ge(filled["mean_" + name], b + 1)
                i = n_roots[0]
                if i >= 2:
                    act.wait_ge(root_read, i - 1)
                n_roots[0] += 1
                sc_act(stat[:, i % 2, 0:n], bank("mean_" + name, b)[:, 0:n], ACT.Sqrt, bias=eps[:, 0:1]).then_inc(emptied["mean_" + name], 1)

            for b in range(4):
                heads("q", flat(qn[:, 2 * b:2 * b + 2, :]), b)
            for b in range(2):
                heads("ks", flat(kn[:, 0, 2 * b:2 * b + 2, :]), b)
            act.wait_ge(filled["vs"], 1)
            nc.scalar.copy(flat(vn[:, 0]), bank("vs")[:]).then_inc(emptied["vs"], 1)
            for b in range(4):
                roots("q", b)
            for b in range(2):
                heads("kw", flat(kn[:, 1, 2 * b:2 * b + 2, :]), b)
            act.wait_ge(filled["vw"], 1)
            nc.scalar.copy(flat(vn[:, 1]), bank("vw")[:]).then_inc(emptied["vw"], 1)
            for b in range(2):
                roots("ks", b)
            act.wait_ge(y_ready, RBLOCKS)
            for n, stage in enumerate(("kc", "vc")):
                act.wait_ge(filled[stage], 1)
                for jj in range(2):
                    for a in range(2):
                        src = bank(stage)[HD * a:HD * a + HD, :].rearrange("p (m t j) -> p m t j", m=2, j=2)[:, :, :, jj]
                        i = nc.scalar.copy(Z[n][HD * jj:HD * jj + HD, a::2, :], src)
                        if (jj, a) == (1, 1):
                            i.then_inc(emptied[stage], 1)
                        else:
                            step(i)
            for b in range(2):
                roots("kw", b)
            for n, stage in enumerate(("hid_k", "hid_v")):
                act.wait_ge(filled[stage], 1)
                sc_act(flat(hid_c[:, n]), bank(stage)[:, 0:2 * NB], ACT.Gelu_apprx_tanh).then_inc(emptied[stage], 1)
            heads("kc2", kcd[:], 0)
            roots("kc", 0, NB)
            act.wait_ge(cshift, TT)
            c_flat = sc[:].rearrange("p t h c -> p (t h c)")
            sc_act(c_flat, c_flat, ACT.Exp).then_inc(cexp, 1)
            for b in range(2):
                act.wait_ge(filled["pcT"], b + 1)
                nc.scalar.copy(flat(pcT[:, 2 * b:2 * b + 2, :]), bank("pcT", b)[:]).then_inc(emptied["pcT"], 1)
            N = 2 * H2
            for i in range(N + 1):
                if i < N:
                    act.wait_ge(smax_ready, i + 1)
                    if i >= 2:
                        act.wait_ge(filled["probT"], i - 1)
                    e, s = E[:, i % 2], S[:, i % 2]
                    sc_act(e[:, 0:P], s[:, 0:P], ACT.Exp, bias=smax[:, i % 2, 0:1], accum_out=ssum[:, i % 2, 0:1]).then_inc(exps_ready, 1)
                    sc_act(e[:, P:], s[:, P:], ACT.Exp, bias=smax[:, i % 2, 1:2], accum_out=ssum[:, i % 2, 1:2]).then_inc(exps_ready, 1)
                if i >= 1:
                    g = i - 1
                    act.wait_ge(filled["probT"], g + 1)
                    if g >= 2:
                        act.wait_ge(filled["o"], g - 1)
                    nc.scalar.copy(PT[:, g % 2], bank("probT", g)[:, 0:3 * P]).then_inc(emptied["probT"], 1)
                    if g % 4 == 1 and g >= 5:
                        c = g // 4 - 1
                        act.wait_ge(filled["o"], 4 * c + 4)
                        nc.scalar.copy(attn[:, c, :], bank("o", c)[:, 0:T]).then_inc(emptied["o"], 1)
            act.wait_ge(filled["o"], N)
            nc.scalar.copy(attn[:, DC - 1, :], bank("o", DC - 1)[:, 0:T]).then_inc(emptied["o"], 1)
            act.wait_ge(emptied["w_out"], 4)
            norm("mlp")
            for b in range(16):
                act.wait_ge(filled["mlp_in"], b + 1)
                if b >= 2:
                    act.wait_ge(squared, b - 1)
                sc_act(stat[:, b % 2], bank("mlp_in", b)[:], ACT.Relu).then_inc(emptied["mlp_in"], 1)
            for b in range(4):
                act.wait_ge(filled["mlp_out"], b + 1)
                nc.scalar.copy(outtok[:, b // 2, b % 2 * BANK:(b % 2 + 1) * BANK], bank("mlp_out", b)[:]).then_inc(emptied["mlp_out"], 1)

        @block.vector
        def _(dve):
            step = Chain(dve, dve_steps)
            vec = nc.vector
            flat = lambda x: x.rearrange("p c n -> p (c n)")

            def normalise(name, pname, dst):
                dve.wait_ge(emptied["mean_" + name], 1)
                step(vec.reciprocal(rstd[:, 0:T], stat[:, 0, 0:T]))
                step.settle()
                for c in range(DC):
                    vec.scalar_tensor_tensor(dst[:, c, :], xT[:, c, :], param(pname, c), rstd[:, 0:T],
                                             ALU.mult, ALU.mult).then_inc(normed[name], 1)

            step(vec.memset(u_pad[:, :, 0:RTAPS - 1], 0.0))
            dve.wait_ge(filled["params"], 1)
            vec.tensor_copy(par[:, 0:n_rows], bank("params")[:, 0:n_rows])
            vec.tensor_copy(par[0:RP, 64:], bank("params")[0:RP, 64:64 + 8 * RC]).then_inc(emptied["params"], 1)
            for t in range(TT):
                dve.wait_ge(filled["near"], t + 1)
                vec.tensor_copy(cbias[:, t], bank("near", t)[:, 0:NCMP * H2].rearrange("p (c h) -> p h c", c=NCMP)).then_inc(emptied["near"], 1)
            dve.wait_ge(emptied["params"], 1)
            normalise("final", "norm_final", xT)
            dve.wait_ge(normed["final"], DC)
            normalise("mix", "norm_mix_2", hT)

            t8 = [sp_[0:RP, i] for i in range(8)]

            def run(ins):
                step(ins)
                step.settle()

            dve.wait_ge(lam_exp, 1)
            run(vec.tensor_scalar(t8[2], t8[1], 2.0, None, ALU.add))
            run(vec.reciprocal(t8[2], t8[2]))
            run(vec.tensor_tensor(t8[2], t8[2], t8[1], ALU.mult))
            run(vec.tensor_tensor(t8[3], t8[2], t8[2], ALU.mult))
            run(vec.tensor_scalar(t8[4], t8[3], 1.0 / 19, None, ALU.mult))
            for k in range(17, 1, -2):
                run(vec.scalar_tensor_tensor(t8[4], t8[4], 1.0 / k, t8[3], ALU.add, ALU.mult))
            run(vec.scalar_tensor_tensor(t8[4], t8[4], 1.0, t8[2], ALU.add, ALU.mult))
            run(vec.tensor_scalar(t8[5], rparam("lru_lambda_2", 0, RC), -1.0, 0.0, ALU.mult, ALU.max))
            run(vec.scalar_tensor_tensor(t8[5], t8[4], 2.0, t8[5], ALU.mult, ALU.add))
            run(vec.tensor_scalar(t8[6], t8[5], 8.0, None, ALU.mult))
            vec.tensor_scalar(t8[7], t8[5], -8.0, None, ALU.mult).then_inc(rates, 1)

            for b in range(RC // 2):
                dve.wait_ge(emptied["u_rnn"], b + 1)
                for k in range(RTAPS):
                    for c in (2 * b, 2 * b + 1):
                        x, w = u_pad[:, c, k:k + T], rparam("conv_w_2", k * RC + c)
                        if k == 0:
                            i = vec.tensor_scalar(xc[:, c, :], x, w, rparam("conv_b_2", c), ALU.mult, ALU.add)
                        else:
                            i = vec.scalar_tensor_tensor(xc[:, c, :], x, w, xc[:, c, :], ALU.mult, ALU.add)
                        if k == RTAPS - 1:
                            i.then_inc(conv_ready, 1)
                        else:
                            step(i)
                    if k < RTAPS - 1:
                        step.settle()
            dve.wait_ge(conv_ready, RC)
            dve.wait_ge(emptied["lru_i"], RC // 2)
            step(vec.tensor_tensor(flat(ix), flat(ix), flat(xc), ALU.mult))
            for n in range(RBLOCKS):
                cs = slice(RB * n, RB * n + RB)
                dve.wait_ge(taus, RB * (n + 1))
                if n:
                    dve.wait_ge(ratios, n)
                run(vec.tensor_scalar(flat(tmp[0:RP]), flat(tau[:, cs, :]), 1.0, None, ALU.add))
                run(vec.reciprocal(flat(tmp[0:RP]), flat(tmp[0:RP])))
                vec.tensor_tensor(flat(tau[:, cs, :]), flat(tau[:, cs, :]), flat(tmp[0:RP]), ALU.mult).then_inc(ratios, 1)
            dve.wait_ge(mults, 1)
            run(vec.memset(tau[:, :, 0:1], 1.0))
            run(vec.tensor_tensor(flat(ix), flat(ix), flat(tau), ALU.mult))
            dve.wait_ge(decays, RC)
            dve.wait_ge(emptied["u_gate"], RC // 2)
            for c in range(RC):
                step(vec.tensor_tensor_scan(xc[:, c, :], ra[:, c, :], ix[:, c, :], 0.0, ALU.mult, ALU.add))
            step.settle()
            for n in range(RBLOCKS):
                cs = slice(RB * n, RB * n + RB)
                vec.tensor_tensor(flat(gel[:, cs, :]), flat(gel[:, cs, :]), flat(xc[:, cs, :]), ALU.mult).then_inc(y_ready, 1)

            n_roots = [0]

            def head_norm(name, b, dst):
                dve.wait_ge(emptied["mean_" + name], b + 1)
                i = n_roots[0]
                if i:
                    dve.wait_ge(last_norm[0], last_norm[1])
                n_roots[0] += 1
                k = dst.shape[1]
                vec.reciprocal(rstd[:, 0:k], stat[:, i % 2, 0:k]).then_inc(root_read, 1)
                dve.wait_ge(root_read, i + 1)
                vec.scalar_tensor_tensor(dst, dst, param(name.removesuffix("_") + "_norm_2"), rstd[:, 0:k],
                                         ALU.mult, ALU.mult).then_inc(normed[name], 1)
                last_norm[:] = [normed[name], b + 1]

            last_norm = [None, 0]
            for b in range(4):
                head_norm("q", b, flat(qn[:, 2 * b:2 * b + 2, :]))
            for b in range(2):
                head_norm("ks", b, flat(kn[:, 0, 2 * b:2 * b + 2, :]))
            for n, stage in enumerate(("kc", "vc")):
                dve.wait_ge(emptied[stage], 1)
                for g in range(KVG):
                    z = Z[n][:, g, :]
                    z = bass.AP(z.tensor, z.offset, [z.ap[0], [1, 16], [STRIDE // 2, NCMP]])
                    pe_ = par[:, col["phi_" + stage[0] + "_pe_2"]:][:, 0:16].unsqueeze(2).broadcast_to([P, 16, NCMP])
                    vec.tensor_tensor(ZB[n][:, :, g, :], z, pe_, ALU.add).then_inc(zb_ready, 1)
            for b in range(2):
                head_norm("kw", b, flat(kn[:, 1, 2 * b:2 * b + 2, :]))
            dve.wait_ge(emptied["ga"], 4)
            dve.wait_ge(emptied["gb"], 4)
            for b in range(4):
                dve.wait_ge(filled["y_a"], b + 1)
                vec.tensor_tensor(flat(merged[:, 2 * b:2 * b + 2, :]), bank("y_a", b)[:], flat(gates_ab[:, 0, 2 * b:2 * b + 2, :]),
                                  ALU.mult).then_inc(emptied["y_a"], 1)
            dve.wait_ge(y_ready, RBLOCKS)
            step(vec.memset(vcz, 0.0))
            step(vec.memset(pc, 0.0))
            step.settle()
            dve.wait_ge(filled["vc2"], 1)
            for r in range(HPG):
                q = slice(32 * r, 32 * r + NCMP)
                i = vec.tensor_copy(vcz[q, :, r, :], bank("vc2")[q, 0:KVG * HD].rearrange("p (g n) -> p g n", g=KVG))
                if r < HPG - 1:
                    step(i)
                else:
                    i.then_inc(emptied["vc2"], 1)
            dve.wait_ge(emptied["kc2"], 1)
            head_norm("kc", 0, kcd[:])

            over_c = lambda x: x.unsqueeze(2).broadcast_to([P, H2, NCMP])
            dve.wait_ge(emptied["near"], TT)
            dve.wait_ge(emptied["mean_kc"], 1)
            for t in range(TT):
                for odd in range(2):
                    dve.wait_ge(filled["scorec"], 2 * t + odd + 1)
                    vec.scalar_tensor_tensor(sc[:, t, odd::2, :], bank("scorec", 2 * t + odd)[:, 0:H2 // 2 * NCMP].rearrange("p (h c) -> p h c", c=NCMP),
                                             HD ** -0.5, cbias[:, t, odd::2, :], ALU.mult, ALU.add).then_inc(emptied["scorec"], 1)
                dve.wait_ge(emptied["scorec"], 2 * t + 2)
                run(vec.tensor_reduce(cm[:, 0, t], sc[:, t], AX_X, ALU.max))
                vec.tensor_tensor(sc[:, t], sc[:, t], over_c(cm[:, 0, t]), ALU.subtract).then_inc(cshift, 1)
            dve.wait_ge(cexp, 1)
            dve.wait_ge(emptied["gn"], 1)
            for t in range(TT):
                run(vec.tensor_reduce(cm[:, 0, t], sc[:, t], AX_X, ALU.add))
                run(vec.reciprocal(cm[:, 0, t], cm[:, 0, t]))
                run(vec.tensor_tensor(cm[:, 1, t], cm[:, 0, t], gn[:, t, 0:3 * H2:3], ALU.mult))
                seen = const[:, C_SEEN + t * NCMP:C_SEEN + (t + 1) * NCMP].unsqueeze(1).broadcast_to([P, H2, NCMP])
                run(vec.tensor_tensor(sc[:, t], sc[:, t], seen, ALU.mult))
                vec.tensor_tensor(pc[:, t, :, 0:NCMP], sc[:, t], over_c(cm[:, 1, t]), ALU.mult).then_inc(pc_ready, 1)

            dve.wait_ge(bias_in, 32)
            N = 2 * H2
            for i in range(N + 1):
                if i < N:
                    if i >= 2:
                        dve.wait_ge(exps_ready, 2 * (i - 1))
                    dve.wait_ge(filled["score"], i + 1)
                    s, m = S[:, i % 2], smax[:, i % 2]
                    vec.scalar_tensor_tensor(s, bank("score", i)[:, 0:3 * P], HD ** -0.5, bias3[:, i // 2, :],
                                             ALU.mult, ALU.add).then_inc(emptied["score"], 1)
                    dve.wait_ge(emptied["score"], i + 1)
                    step(vec.tensor_reduce(m[:, 0:1], s[:, 0:P], AX_X, ALU.max))
                    run(vec.tensor_reduce(m[:, 1:2], s[:, P:], AX_X, ALU.max))
                    vec.tensor_scalar(m, m, -1.0, None, ALU.mult).then_inc(smax_ready, 1)
                if i >= 1:
                    g = (i - 1) % 2
                    hd, n = (i - 1) // 2, (i - 1) % 2
                    dve.wait_ge(exps_ready, 2 * i)
                    run(vec.reciprocal(ssum[:, g], ssum[:, g]))
                    col_ = 3 * hd + 1 + n
                    run(vec.tensor_tensor(ssum[:, g], ssum[:, g], gn[:, :, col_], ALU.mult))
                    vec.tensor_scalar(E[:, g, 0:P], E[:, g, 0:P], ssum[:, g, 0:1], None, ALU.mult)
                    vec.tensor_scalar(E[:, g, P:], E[:, g, P:], ssum[:, g, 1:2], None, ALU.mult).then_inc(probs_ready, 1)
            for b in range(4):
                dve.wait_ge(filled["y_b"], b + 1)
                x = rstd[:]
                if b:
                    dve.wait_ge(emptied["y_b"], b)
                run(vec.tensor_tensor(x, bank("y_b", b)[:], flat(gates_ab[:, 1, 2 * b:2 * b + 2, :]), ALU.mult))
                y = flat(merged[:, 2 * b:2 * b + 2, :])
                vec.tensor_tensor(y, y, x, ALU.add).then_inc(emptied["y_b"], 1)
            for b in range(4):
                dve.wait_ge(filled["w_out"], b + 1)
                x = flat(xT[:, 2 * b:2 * b + 2, :])
                vec.tensor_tensor(x, x, bank("w_out", b)[:], ALU.add).then_inc(emptied["w_out"], 1)
            dve.wait_ge(emptied["w_out"], 4)
            normalise("mlp", "norm_mlp_2", hT)
            for b in range(16):
                dve.wait_ge(emptied["mlp_in"], b + 1)
                x = stat[:, b % 2]
                vec.tensor_tensor(hidden(2 * b, 2), x, x, ALU.mult).then_inc(squared, 1)

    return sems


_INS = ["x", "p", "norm_mix", "w_in", "w_dw", "b_dw", "ln_conv_g", "ln_conv_b", "w_attn_out", "w_conv_out", "b_conv_out",
        "w_out", "norm_ffn", "w_route_group", "b_route_group", "w_route_expert", "b_route_expert", "w_exp_gate",
        "w_exp_up", "w_exp_down", "norm_ple", "w_ple_proj", "w_ple_gate", "norm_final"]
_INS += [n + "_2" for n in (
    "norm_mix", "w_in", "conv_w", "conv_b", "gate_a_w", "gate_a_b", "gate_x_w", "gate_x_b", "lru_lambda", "phi_k_pe",
    "phi_k_w1", "phi_k_w2", "phi_v_pe", "phi_v_w1", "phi_v_w2", "q_norm", "kc_norm", "ks_norm", "kw_norm", "rel_bias",
    "proj_a", "proj_b", "w_out", "norm_mlp", "w_mlp_in", "w_mlp_out")]


def build(nc, dram, table, far, near, out):
    with ExitStack() as ctx:
        def sb(name, shape, dt=F32):
            return ctx.enter_context(nc.sbuf_tensor(name, shape, dt))

        keep = dict(xT=sb("xT", [P, DC, T]), hT=sb("hT", [P, DC, T]), sq=sb("sq", [P, DC, T]), eps=sb("eps", [P, 1]),
                    ones=dict(D=sb("ones_d", [P, P]), C=sb("ones_c", [P, P])))
        keep["ps"] = [ctx.enter_context(nc.psum_tensor(f"ps{i}", [P, BANK], F32)) for i in range(BANKS)]
        const = sb("const", [P, C_COLS])
        ps, xT = keep["ps"], keep["xT"]

        with ExitStack() as pro:
            xtok = pro.enter_context(nc.sbuf_tensor("xtok", [P, TT, D], F32))
            loaded, turned, copied = (pro.enter_context(nc.semaphore(n)) for n in ("loaded", "turned", "copied"))
            with nc.Block(no_gpsimd_drain=True) as block:
                @block.sync
                def _(sp):
                    sp.dma_start(xtok[:], dram["x"][0].rearrange("(t p) n -> p t n", p=P)).then_inc(loaded, 16)
                    sp.dma_start(const[:], table).then_inc(loaded, 16)

                @block.tensor
                def _(pe):
                    pe.wait_ge(loaded, 32)
                    for b in range(4):
                        for m in range(2):
                            for t in range(TT):
                                c = 2 * b + m
                                mm = nc.tensor.transpose(ps[b][:, m * T + t * P:m * T + (t + 1) * P], xtok[:, t, c * P:(c + 1) * P],
                                                         const[:, C_ID:C_ID + P])
                        mm.then_inc(turned, 1)

                @block.vector
                def _(dve):
                    nc.vector.memset(keep["eps"][:], EPS)
                    nc.vector.memset(keep["ones"]["D"][:], 1.0 / D)
                    nc.vector.memset(keep["ones"]["C"][:], 1.0 / CW)
                    for b in range(4):
                        dve.wait_ge(turned, b + 1)
                        nc.vector.tensor_copy(xT[:, 2 * b:2 * b + 2, :].rearrange("p c n -> p (c n)"), ps[b][:]).then_inc(copied, 1)

            clear(nc, (loaded, turned, copied))

        with ExitStack() as one:
            with nc.Fori(0, DEPTH) as layer:
                clear(nc, first_block_layer(nc, one, dram, const, keep, layer))
        with ExitStack() as two:
            second_block(nc, two, dram, const, keep, nc.dram_tensor("bias_rows", (H2, P, SKEW), F32).ap(), out)


def kernel(**inputs):
    import concourse.bacc as _bacc
    from concourse.bass_utils import run_bass_kernel_spmd as _run

    nc = _bacc.Bacc("TRN2", target_bir_lowering=False, num_devices=1)
    arrays, dram = {}, {}
    tables = dict(zip(("table", "far", "near"), constants()))
    tables["off"] = np.full((1, H2), NEG, np.float32)
    for name, a in [(n, inputs[n]) for n in _INS] + list(tables.items()):
        a = np.ascontiguousarray(a)
        arrays[f"in_{name}"] = a
        dram[name] = nc.dram_tensor(f"in_{name}", a.shape, mybir.dt.from_np(a.dtype), kind="ExternalInput").ap()
    out = nc.dram_tensor("out_0", (1, T, D), F32, kind="ExternalOutput").ap()
    build(nc, dram, dram["table"], dram["far"], dram["near"], out)
    r = _run(nc, [arrays], core_ids=[0])
    return r.results[0]["out_0"]
```
